# Optimizing a Trainium2 kernel written in Bass

```python
import math
import jax, jax.numpy as jnp
from jax import lax
import numpy as np

D_MODEL = 1024
BATCH = 1
SEQ = 256
DEPTH = 2

D_FF = 3 * D_MODEL
FFN_CONV = 3
N_BRANCH = 3
LRU_WIDTH = D_MODEL // 2
LRU_BLOCKS = 8
LRU_BLOCK_DIM = LRU_WIDTH // LRU_BLOCKS
LRU_CONV = 4
LRU_C = 8.0
DIFF_HEADS = 4
DIFF_HEAD_DIM = D_MODEL // 16
DIFF_WIDTH = DIFF_HEADS * 2 * DIFF_HEAD_DIM
ROT_DIM = DIFF_HEAD_DIM // 4
ROPE_THETA = 500000.0
Q_BLOCK = 128
RWKV_HEAD_DIM = 64
RWKV_WIDTH = D_MODEL // 2
RWKV_HEADS = RWKV_WIDTH // RWKV_HEAD_DIM
DECAY_LORA = 64
AAA_LORA = 64
GATE_LORA = 128
MV_LORA = 32
RWKV_COLS = 3 * RWKV_WIDTH + DECAY_LORA + AAA_LORA + GATE_LORA
NORM_EPS = 1e-6
SUBLN_EPS = 1e-5
GN_EPS = 64e-5
O_LX = N_BRANCH * D_MODEL
O_LY = O_LX + LRU_WIDTH
O_Q = O_LY + LRU_WIDTH
O_K = O_Q + DIFF_WIDTH
O_V = O_K + DIFF_WIDTH
O_RW = O_V + DIFF_WIDTH
IN_COLS = O_RW + RWKV_COLS

kernel_name = "hybrid_rglru_diffattn_rwkv7_adaln_block"

def rmsnorm(x, g, eps=NORM_EPS):
    x32 = x.astype(jnp.float32)
    y = x32 * lax.rsqrt(jnp.mean(x32 * x32, axis=-1, keepdims=True) + eps)
    return (y * g.astype(jnp.float32)).astype(x.dtype)

def causal_dwconv(x, w, b):
    K, C = w.shape
    y = lax.conv_general_dilated(x, w[:, None, :].astype(x.dtype), window_strides=(1,),
                                 padding=[(K - 1, 0)], dimension_numbers=("NWC", "WIO", "NWC"),
                                 feature_group_count=C)
    return y + b

def token_shift_mix(z, mu):
    prev = jnp.pad(z, ((0, 0), (1, 0), (0, 0)))[:, :-1]
    return z + (prev - z) * mu

def _linear_comb(e1, e2):
    a1, b1 = e1
    a2, b2 = e2
    return a1 * a2, a2 * b1 + b2

def rglru_branch(zx, zy, conv_w, conv_b, wa, ba, wx, bx, lam):
    xc = causal_dwconv(zx, conv_w, conv_b)
    B, S, W = xc.shape
    xb = xc.reshape(B, S, LRU_BLOCKS, LRU_BLOCK_DIM)
    r = jax.nn.sigmoid(jnp.einsum("bsnc,ncd->bsnd", xb, wa) + ba).reshape(B, S, W)
    i = jax.nn.sigmoid(jnp.einsum("bsnc,ncd->bsnd", xb, wx) + bx).reshape(B, S, W)
    log_a = -LRU_C * r.astype(jnp.float32) * jax.nn.softplus(-lam.astype(jnp.float32))
    a = jnp.exp(log_a)
    u = jnp.sqrt(-jnp.expm1(2.0 * log_a)) * (i * xc).astype(jnp.float32)
    _, h = lax.associative_scan(_linear_comb, (a, u), axis=1)
    return h.astype(zx.dtype) * jax.nn.gelu(zy, approximate=True)

def partial_rope(t, cos, sin):
    half = ROT_DIM // 2
    x1, x2, rest = t[..., :half], t[..., half:ROT_DIM], t[..., ROT_DIM:]
    return jnp.concatenate([x1 * cos - x2 * sin, x2 * cos + x1 * sin, rest], axis=-1)

def diff_attention(zq, zk, zv, positions, lq1, lk1, lq2, lk2, subln_g, lambda_init):
    B, S, _ = zq.shape
    H, d = DIFF_HEADS, DIFF_HEAD_DIM
    inv_freq = ROPE_THETA ** (-jnp.arange(0, ROT_DIM, 2, dtype=jnp.float32) / ROT_DIM)
    ang = positions.astype(jnp.float32)[..., None] * inv_freq
    cos = jnp.cos(ang)[:, :, None, None, :]
    sin = jnp.sin(ang)[:, :, None, None, :]
    q = partial_rope(zq.reshape(B, S, H, 2, d).astype(jnp.float32), cos, sin) * (d ** -0.5)
    k = partial_rope(zk.reshape(B, S, H, 2, d).astype(jnp.float32), cos, sin)
    v = zv.reshape(B, S, H, 2 * d)
    lam = (jnp.exp(jnp.sum(lq1.astype(jnp.float32) * lk1.astype(jnp.float32)))
           - jnp.exp(jnp.sum(lq2.astype(jnp.float32) * lk2.astype(jnp.float32))) + lambda_init)
    nblk = S // Q_BLOCK
    qb = q.reshape(B, nblk, Q_BLOCK, H, 2, d).transpose(1, 0, 2, 3, 4, 5)
    k_idx = jnp.arange(S)

    def block(args):
        q_blk, bi = args
        s = jnp.einsum("bqhcd,bkhcd->bhcqk", q_blk, k)
        q_idx = bi * Q_BLOCK + jnp.arange(Q_BLOCK)
        s = jnp.where(k_idx[None, :] <= q_idx[:, None], s, -1e30)
        p = jax.nn.softmax(s, axis=-1)
        p = p[:, :, 0] - lam * p[:, :, 1]
        return jnp.einsum("bhqk,bkhe->bqhe", p.astype(v.dtype), v)

    o = lax.map(block, (qb, jnp.arange(nblk)))
    o = o.transpose(1, 0, 2, 3, 4).reshape(B, S, H, 2 * d)
    o = rmsnorm(o, subln_g, SUBLN_EPS) * (1.0 - lambda_init)
    return o.reshape(B, S, DIFF_WIDTH)

def wkv7_scan(r, w, k, v, a, b):
    B, S, H, N = r.shape
    seq = tuple(jnp.swapaxes(t.astype(jnp.float32), 0, 1) for t in (r, w, k, v, a, b))

    def step(state, inp):
        r_t, w_t, k_t, v_t, a_t, b_t = inp
        sa = jnp.einsum("bhvk,bhk->bhv", state, a_t)
        state = (state * w_t[:, :, None, :] + sa[..., None] * b_t[:, :, None, :]
                 + v_t[..., None] * k_t[:, :, None, :])
        return state, jnp.einsum("bhvk,bhk->bhv", state, r_t)

    _, out = lax.scan(step, jnp.zeros((B, H, N, N), jnp.float32), seq)
    return jnp.swapaxes(out, 0, 1)

def rwkv7_mix(z, mu, w0, w2, a0, a2, g2, k_k, k_a, r_k, lnx_g, lnx_b, v_first,
              zvd=None, v_mu=None, v0=None, v2=None):
    B, S, _ = z.shape
    H, N, W = RWKV_HEADS, RWKV_HEAD_DIM, RWKV_WIDTH
    z = token_shift_mix(z, mu)
    r, k, v = z[..., :W], z[..., W:2 * W], z[..., 2 * W:3 * W]
    o = 3 * W
    wd = z[..., o:o + DECAY_LORA]
    o += DECAY_LORA
    ad = z[..., o:o + AAA_LORA]
    o += AAA_LORA
    gd = z[..., o:o + GATE_LORA]
    log_w = -jax.nn.softplus(-(w0 + jnp.tanh(wd) @ w2).astype(jnp.float32)) - 0.5
    decay = jnp.exp(-jnp.exp(log_w))
    a = jax.nn.sigmoid(a0 + ad @ a2)
    g = jax.nn.sigmoid(gd) @ g2
    if v_first is None:
        v_first = v
    else:
        v = v + (v_first - v) * jax.nn.sigmoid(v0 + token_shift_mix(zvd, v_mu) @ v2)
    kk = (k * k_k).astype(jnp.float32).reshape(B, S, H, N)
    kk = kk / jnp.maximum(jnp.sqrt(jnp.sum(kk * kk, axis=-1, keepdims=True)), 1e-12)
    k = k * (1 + (a - 1) * k_a)
    rh, kh, vh, ah = (t.reshape(B, S, H, N) for t in (r, k, v, a))
    out = wkv7_scan(rh, decay.reshape(B, S, H, N), kh, vh, -kk, kk * ah.astype(jnp.float32))
    mean = jnp.mean(out, axis=-1, keepdims=True)
    var = jnp.mean(jnp.square(out - mean), axis=-1, keepdims=True)
    out = ((out - mean) * lax.rsqrt(var + GN_EPS)).reshape(B, S, W)
    out = out * lnx_g.astype(jnp.float32) + lnx_b.astype(jnp.float32)
    bonus = jnp.sum((rh * kh * r_k).astype(jnp.float32), axis=-1, keepdims=True) * vh.astype(jnp.float32)
    y = (out + bonus.reshape(B, S, W)) * g.astype(jnp.float32)
    return y.astype(z.dtype), v_first

def conv_gated_mlp(h, w_up, conv_w, conv_b, w_down):
    u = causal_dwconv(h @ w_up, conv_w, conv_b)
    gate, val = u[..., :D_FF], u[..., D_FF:]
    return (jax.nn.gelu(gate, approximate=True) * val) @ w_down

def setup_inputs(seed: int = 0) -> dict:
    key = jax.random.key(seed)
    ks = iter(jax.random.split(key, 64))
    L, D = DEPTH, D_MODEL

    def nrm(shape, scale):
        return scale * jax.random.normal(next(ks), shape, jnp.float32)

    def uni(shape, lo, hi):
        return jax.random.uniform(next(ks), shape, jnp.float32, lo, hi)

    offsets = jax.random.randint(next(ks), (BATCH, 1), 0, 1024, dtype=jnp.int32)
    lru_u = uni((L, LRU_WIDTH), 0.9, 0.999)
    return {
        "x": nrm((BATCH, SEQ, D), 1.0),
        "c": nrm((BATCH, D), 1.0),
        "positions": offsets + jnp.arange(SEQ, dtype=jnp.int32)[None, :],
        "w_mod": nrm((L, D, 6 * D), 0.5 * D ** -0.5),
        "b_mod": nrm((L, 6 * D), 0.01),
        "norm1_g": 1.0 + nrm((L, D), 0.02),
        "norm2_g": 1.0 + nrm((L, D), 0.02),
        "final_g": 1.0 + nrm((D,), 0.02),
        "w_in": nrm((L, D, IN_COLS), D ** -0.5),
        "w_merge_a": nrm((L, LRU_WIDTH, D), LRU_WIDTH ** -0.5),
        "w_merge_b": nrm((L, DIFF_WIDTH, D), DIFF_WIDTH ** -0.5),
        "w_merge_c": nrm((L, RWKV_WIDTH, D), RWKV_WIDTH ** -0.5),
        "w_out": nrm((L, D, D), D ** -0.5),
        "lru_conv_w": nrm((L, LRU_CONV, LRU_WIDTH), 0.5),
        "lru_conv_b": nrm((L, LRU_WIDTH), 0.01),
        "lru_wa": nrm((L, LRU_BLOCKS, LRU_BLOCK_DIM, LRU_BLOCK_DIM), LRU_BLOCK_DIM ** -0.5),
        "lru_ba": nrm((L, LRU_BLOCKS, LRU_BLOCK_DIM), 0.01),
        "lru_wx": nrm((L, LRU_BLOCKS, LRU_BLOCK_DIM, LRU_BLOCK_DIM), LRU_BLOCK_DIM ** -0.5),
        "lru_bx": nrm((L, LRU_BLOCKS, LRU_BLOCK_DIM), 0.01),
        "lru_lambda": jnp.log(lru_u) - jnp.log1p(-lru_u),
        "diff_lq1": nrm((L, DIFF_HEAD_DIM), 0.1),
        "diff_lk1": nrm((L, DIFF_HEAD_DIM), 0.1),
        "diff_lq2": nrm((L, DIFF_HEAD_DIM), 0.1),
        "diff_lk2": nrm((L, DIFF_HEAD_DIM), 0.1),
        "diff_subln_g": 1.0 + nrm((L, 2 * DIFF_HEAD_DIM), 0.02),
        "rwkv_mu": uni((L, RWKV_COLS), 0.0, 1.0),
        "rwkv_w0": uni((L, RWKV_WIDTH), -6.5, -1.0),
        "rwkv_w2": nrm((L, DECAY_LORA, RWKV_WIDTH), 0.1),
        "rwkv_a0": nrm((L, RWKV_WIDTH), 0.01),
        "rwkv_a2": nrm((L, AAA_LORA, RWKV_WIDTH), 0.5 * AAA_LORA ** -0.5),
        "rwkv_g2": nrm((L, GATE_LORA, RWKV_WIDTH), GATE_LORA ** -0.5),
        "rwkv_kk": 0.85 + nrm((L, RWKV_WIDTH), 0.02),
        "rwkv_ka": 1.0 + nrm((L, RWKV_WIDTH), 0.02),
        "rwkv_rk": nrm((L, RWKV_HEADS, RWKV_HEAD_DIM), 0.1),
        "rwkv_lnx_g": 1.0 + nrm((L, RWKV_WIDTH), 0.02),
        "rwkv_lnx_b": nrm((L, RWKV_WIDTH), 0.01),
        "rwkv_v0": 1.0 + nrm((L - 1, RWKV_WIDTH), 0.02),
        "rwkv_v1": nrm((L - 1, D, MV_LORA), D ** -0.5),
        "rwkv_v2": nrm((L - 1, MV_LORA, RWKV_WIDTH), 0.5 * MV_LORA ** -0.5),
        "rwkv_vmu": uni((L - 1, MV_LORA), 0.0, 1.0),
        "ffn_up": nrm((L, D, 2 * D_FF), D ** -0.5),
        "ffn_conv_w": nrm((L, FFN_CONV, 2 * D_FF), 0.5),
        "ffn_conv_b": nrm((L, 2 * D_FF), 0.01),
        "ffn_down": nrm((L, D_FF, D), D_FF ** -0.5),
    }

def reference(x, c, positions, w_mod, b_mod, norm1_g, norm2_g, final_g, w_in,
              w_merge_a, w_merge_b, w_merge_c, w_out,
              lru_conv_w, lru_conv_b, lru_wa, lru_ba, lru_wx, lru_bx, lru_lambda,
              diff_lq1, diff_lk1, diff_lq2, diff_lk2, diff_subln_g,
              rwkv_mu, rwkv_w0, rwkv_w2, rwkv_a0, rwkv_a2, rwkv_g2, rwkv_kk, rwkv_ka,
              rwkv_rk, rwkv_lnx_g, rwkv_lnx_b, rwkv_v0, rwkv_v1, rwkv_v2, rwkv_vmu,
              ffn_up, ffn_conv_w, ffn_conv_b, ffn_down):
    D = D_MODEL
    c_act = jax.nn.silu(c)
    v_first = None
    for l in range(DEPTH):
        mod = (c_act @ w_mod[l] + b_mod[l])[:, None, :]
        sh1, sc1, gt1, sh2, sc2, gt2 = jnp.split(mod, 6, axis=-1)

        h = rmsnorm(x, norm1_g[l]) * (1 + sc1) + sh1
        w_cat = w_in[l] if l == 0 else jnp.concatenate([w_in[l], rwkv_v1[l - 1]], axis=1)
        z = h @ w_cat

        ya = rglru_branch(z[..., O_LX:O_LY], z[..., O_LY:O_Q], lru_conv_w[l], lru_conv_b[l],
                          lru_wa[l], lru_ba[l], lru_wx[l], lru_bx[l], lru_lambda[l])
        lambda_init = 0.8 - 0.6 * math.exp(-0.3 * l)
        yb = diff_attention(z[..., O_Q:O_K], z[..., O_K:O_V], z[..., O_V:O_RW], positions,
                            diff_lq1[l], diff_lk1[l], diff_lq2[l], diff_lk2[l],
                            diff_subln_g[l], lambda_init)
        if l == 0:
            yc, v_first = rwkv7_mix(z[..., O_RW:IN_COLS], rwkv_mu[l], rwkv_w0[l], rwkv_w2[l],
                                    rwkv_a0[l], rwkv_a2[l], rwkv_g2[l], rwkv_kk[l], rwkv_ka[l],
                                    rwkv_rk[l], rwkv_lnx_g[l], rwkv_lnx_b[l], None)
        else:
            yc, v_first = rwkv7_mix(z[..., O_RW:IN_COLS], rwkv_mu[l], rwkv_w0[l], rwkv_w2[l],
                                    rwkv_a0[l], rwkv_a2[l], rwkv_g2[l], rwkv_kk[l], rwkv_ka[l],
                                    rwkv_rk[l], rwkv_lnx_g[l], rwkv_lnx_b[l], v_first,
                                    zvd=z[..., IN_COLS:], v_mu=rwkv_vmu[l - 1],
                                    v0=rwkv_v0[l - 1], v2=rwkv_v2[l - 1])

        merged = (jax.nn.sigmoid(z[..., 0:D]) * (ya @ w_merge_a[l])
                  + jax.nn.sigmoid(z[..., D:2 * D]) * (yb @ w_merge_b[l])
                  + jax.nn.sigmoid(z[..., 2 * D:3 * D]) * (yc @ w_merge_c[l]))
        x = x + gt1 * (merged @ w_out[l])

        h2 = rmsnorm(x, norm2_g[l]) * (1 + sc2) + sh2
        x = x + gt2 * conv_gated_mlp(h2, ffn_up[l], ffn_conv_w[l], ffn_conv_b[l], ffn_down[l])
    return rmsnorm(x, final_g)


_drawn_inputs = setup_inputs


def setup_inputs(seed=0):
    import zlib

    import numpy as np

    out = dict(_drawn_inputs(seed))
    spreads = {}
    factors = {'b_mod': 4.004,
     'norm1_g': 7.739,
     'norm2_g': 29.607,
     'final_g': 28.709,
     'lru_conv_b': 60.875,
     'lru_ba': 173.354,
     'lru_bx': 64.0,
     'diff_lq1': 64.0,
     'diff_lk1': 3.034,
     'diff_lq2': 6.382,
     'diff_lk2': 7.719,
     'diff_subln_g': 200.0,
     'rwkv_w2': 29.025,
     'rwkv_a0': 8.0,
     'rwkv_kk': 200.0,
     'rwkv_ka': 8.0,
     'rwkv_lnx_g': 200.0,
     'rwkv_lnx_b': 200.0,
     'rwkv_v0': 200.0,
     'rwkv_v1': 4.048,
     'rwkv_v2': 3.926,
     'rwkv_vmu': 8.0,
     'ffn_conv_b': 51.899,
     'rwkv_w0': 4.39}
    for name, (base, spread) in spreads.items():
        noise = np.random.default_rng([zlib.crc32(name.encode()), seed]).standard_normal(out[name].shape)
        drawn = base * np.exp(spread * noise) if base else spread * noise
        out[name] = __import__('jax').numpy.asarray(drawn.astype(out[name].dtype))
    for name, factor in factors.items():
        out[name] = (out[name] * factor).astype(out[name].dtype)
    return out
```

```python
import math
from contextlib import ExitStack

import numpy as np

import concourse.bass as bass
from concourse import mybir

ALU = mybir.AluOpType
ACT = mybir.ActivationFunctionType
F32 = mybir.dt.float32
I32 = mybir.dt.int32
AX_X = mybir.AxisListType.X

P = 128
D = 1024
S = 256
L = 2
KT = D // P
W = 512
WT = W // P
FT = 3 * D // P
CH = 64
NCH = S // CH

RW, LR, AT, GA, MG, OU, UP, DN, PAIRS = 0, 7, 11, 17, 29, 35, 39, 63, 75
SLOTS = 4
PAIR = 2048

_NAMES = [("n1g", 8), ("n2g", 8), ("bmod", 48), ("mu", 14), ("w0", 4), ("a0", 4), ("v0", 4), ("ba", 4), ("bx", 4),
          ("kk", 4), ("ka", 4), ("rk", 4), ("lng", 4), ("lnb", 4), ("vmu", 1), ("sub", 1), ("cw", 16), ("cb", 4),
          ("lam", 4), ("fw", 144), ("fb", 48), ("fg", 8), ("cc", 8)]
COL, NP = {}, 0
for _n, _w in _NAMES:
    COL[_n] = NP
    NP += _w

(IDENT, BLOCKS, M_LOW, M_UP, M_UPI, M_L1, M_U1, M_U2, M_U4, M_U8, M_U16, M_U32, ROT) = range(13)
NMAT = 13
NEG0 = NMAT * P
RESET = NEG0 + 256
FREQ = RESET + 256
NC_ = FREQ + 1

WL, WG, WA, WX = 0, 512, 1024, 1536

SQ2PI = 2.0 * math.pi
MAGIC = 1.5 * 2.0 ** 23
C1 = 6.28125
C2 = float(np.float32(SQ2PI - C1))
C3 = SQ2PI - C1 - C2
PI_IN = 3.1415925
EM05 = math.exp(-0.5)


def lambda_init(l):
    return 0.8 - 0.6 * math.exp(-0.3 * l)


def banks_of(g):
    l, k = divmod(g, PAIRS)
    if MG <= k < OU:
        return [(2 * (k - MG)) % 4, (2 * (k - MG) + 1) % 4]
    return [g % 4]


def _emptied():
    count, out = [0] * 4, []
    for g in range(L * PAIRS):
        out.append(list(count))
        if not DN <= g % PAIRS < PAIRS - 4:
            for b in banks_of(g):
                count[b] += 1
    return out


EMPTIED = _emptied()

FILL = [16] * 4 + [8] * 14
FILLED = np.cumsum(FILL) // 16

SCORES = [(0, 0, 0, 4), (0, 1, 0, 4), (1, 0, 0, 2), (1, 1, 0, 2), (1, 0, 2, 2), (1, 1, 2, 2)]
SCORE_BANK = [6, 7, 4, 5, 6, 7]
LEVELS = [M_U2, M_U4, M_U8, M_U16, M_U32]


def solve_steps():
    steps = [("ak", 0, 0, 4), ("ak", 1, 0, 5), ("n", 0, 0, 6), ("n", 1, 0, 7), ("nt", 0, 0, 4), ("nt", 1, 0, 5)]
    other = 6
    for v in range(len(LEVELS)):
        for kind in ("m", "x", "xt"):
            if kind == "xt" and v == len(LEVELS) - 1:
                continue
            for par in (0, 1):
                steps.append((kind, par, v, other + par))
            other = 10 - other
    return steps


STEPS = solve_steps()
NSTEP = len(STEPS)


def step_no(kind, par, v):
    return next(i for i, s in enumerate(STEPS) if s[:3] == (kind, par, v))


def trunk_kernel(nc, wmain, wmod, small, v1v2, params, consts, lqk, x_t, positions, y_t):
    ctx = ExitStack()
    with ctx:
        def sb(name, shape, dt=F32):
            return ctx.enter_context(nc.sbuf_tensor(name, shape, dt))

        def sem(name):
            return ctx.enter_context(nc.semaphore(name))

        X = sb("X", [P, KT, S])
        H = sb("H", [P, KT, S])
        ring = sb("ring", [P, SLOTS, PAIR])
        mring = sb("mring", [P, 2, D])
        macc = sb("macc", [P, D])
        C = sb("C", [P, NC_])
        PR = sb("PR", [P, L, NP])
        PH = sb("PH", [P, L, 20])
        SW = sb("SW", [P, 2048])
        COS = sb("COS", [P, S])
        SIN = sb("SIN", [P, S])
        G = sb("G", [P, FT, S])
        ZS = sb("ZS", [P, 12, S])
        AB = sb("AB", [P, WT, S])
        KK = sb("KK", [P, WT, S])
        GG = sb("GG", [P, WT, S])
        BON = sb("BON", [P, WT, S])
        E = sb("E", [P, WT, S])
        WY = sb("WY", [P, 2, W])
        TK = sb("TK", [P, 16, S])
        R = sb("R", [P, 24, S])
        YA = sb("YA", [P, WT, S])
        YB = sb("YB", [P, WT, S])
        RT = sb("RT", [P, S])
        mod = sb("mod", [P, 12, KT])
        Acol = sb("Acol", [P, KT])
        ones = sb("ones", [P, P])
        sm = sb("sm", [P, 80])
        CSIL, NLAM, N8, SUBG, ONE1 = 0, 8, 10, 18, 20
        EPS6, EPS5, EPSG = 21, 22, 23
        MIDS, GF, MX, LSUM = 24, 40, 52, 60
        FH = 68

        ps = ctx.enter_context(nc.psum_tensor("ps", [P, 8, 512], F32))

        K_, R_, V_ = ZS[:, 0:4, :], ZS[:, 4:8, :], ZS[:, 8:12, :]
        LD, CUM = G[:, 14:18, :], G[:, 18:22, :]
        V1 = G[:, 22, :].rearrange("p (k m) -> p k m", k=KT)
        V2 = YB[:, 0:2, :].rearrange("p a b -> p (a b)")
        ZX, XC, LRA, LRI = TK[:, 0:4, :], TK[:, 4:8, :], TK[:, 8:12, :], TK[:, 12:16, :]
        QK, VR = R[:, 0:8, :], R[:, 8:12, :]
        VF = R[:, 0:4, :]
        AVT = R[:, 12:16, :].rearrange("p a b -> p (a b)").rearrange("p (t w) -> p t w", t=2)
        S0 = R[:, 16:20, :].rearrange("p a b -> p (a b)").rearrange("p (c h k) -> p c h k", c=2, h=4)
        S1 = TK[:, 8:16, :].rearrange("p (c h) k -> p c h k", c=2)
        PT = R[:, 0:8, :].rearrange("p (t h) q -> p t h q", t=2)

        def tok(i):
            return TK[:, 4 * i:4 * i + 4, :].rearrange("p a b -> p (a b)").rearrange("p (t w) -> p t w", t=2)

        AT_, BT_, KT_, VT_ = tok(0), tok(1), tok(2), tok(3)

        def mats(a, b):
            return R[:, a:b, :].rearrange("p a b -> p (a b)").rearrange("p (g j s) -> p g j s", j=4, s=P)

        TTm, Nm, Tm, Mm = mats(0, 8), mats(8, 12), mats(12, 16), mats(16, 20)
        RBm, RKm = mats(8, 16), mats(16, 24)
        ge = E[:, :, :].rearrange("p a b -> p (a b)").rearrange("p (c j s) -> p c j s", c=2, j=4)
        ga = TK[:, 0:4, :].rearrange("p a b -> p (a b)").rearrange("p (c j s) -> p c j s", c=2, j=4)
        GM = [ge[:, 0], ge[:, 1], ga[:, 0]]
        ST = ga[:, 1]
        UB = TK[:, 0:4, :].rearrange("p (u t) s -> p u t s", u=2)

        def mat(i):
            return C[:, i * P:(i + 1) * P]

        def col(l, name, i=0, n=1):
            return PR[:, l, COL[name] + i:COL[name] + i + n]

        def flat(ap):
            return ap.rearrange("p a b -> p (a b)")

        def over(ap, n):
            return ap.unsqueeze(1).broadcast_to([ap.shape[0], n, ap.shape[1]])

        def along(ap, n):
            return ap.unsqueeze(2).broadcast_to([ap.shape[0], ap.shape[1], n])

        def quad(b):
            return ps[:, b, :].rearrange("p (j s) -> p j s", j=4)

        def duo(b):
            return ps[:, b, :].rearrange("p (t s) -> p t s", t=2)

        s_w = [sem(f"pair_landed{i}") for i in range(SLOTS)]
        s_m = [sem(f"mod_block_landed{i}") for i in range(2)]
        s_par, s_sw, s_v12 = sem("params_landed"), sem("small_weights_landed"), sem("value_lora_landed")
        s_out = sem("output_written")
        pair_done = sem("pair_done")
        bank_free = [sem(f"bank_free{i}") for i in range(4)]
        pre_act, pre_dve = sem("preamble_act"), sem("preamble_dve")
        bd_zero = sem("block_diagonals_zeroed")
        mod_used, mod_mm, mod_ready = sem("mod_block_used"), sem("mod_summed"), sem("mod_ready")
        x_sq, x_ss, x_rt = sem("x_squared"), sem("x_summed"), sem("x_rooted")
        h_pre, h_ready = sem("h_scaled"), sem("h_ready")
        step = sem("dve_step")
        astep = sem("act_step")
        zr_up = sem("rwkv_raw_ready")
        lora_z, lora_t, lora_mm, lora_act = sem("lora_shifted"), sem("lora_activated"), sem("lora_products"), sem("lora_read")
        zv_up, zv_ready, vf_moved, v_ready = sem("value_lora_up"), sem("value_lora_shifted"), sem("v_first_moved"), sem("v_ready")
        kk_raw, kk_sq, kk_mm, kk_rt = sem("kk_raw"), sem("kk_squared"), sem("kk_summed"), sem("kk_rooted")
        kk_used = sem("kk_root_used")
        rk_ready, bon_mm, bon_ready = sem("bonus_terms"), sem("bonus_summed"), sem("bonus_ready")
        cc_ready, cm_ready, exps = sem("log_decay_ready"), sem("log_decay_before_ready"), sem("decay_exps")
        feat = sem("rwkv_operands_ready")
        lr_up, xc_ready, lr_mm, lr_act = sem("lru_inputs_ready"), sem("lru_conv_ready"), sem("lru_gates_summed"), sem("lru_gates_ready")
        la_ready, la_act, lq_ready, lq_rt = sem("lru_log_a"), sem("lru_exps"), sem("lru_var"), sem("lru_root")
        ya_ready = sem("ya_ready")
        at_up, rot_mm, rope_mul, qk_ready = sem("qkv_ready"), sem("rotated"), sem("rotated_read"), sem("qk_ready")
        avt_mm, avt_ev = sem("v_turned"), sem("v_by_position")
        sc_mm, sc_read, mx_ready, p_exp, p_ready = (sem("scores_summed"), sem("scores_read"), sem("maxima_ready"),
                                                    sem("weights_exp"), sem("weights_ready"))
        pt_mm, pt_ev, ao_mm, ao_sq, as_mm, as_rt, yb_ready = (
            sem("weights_turned"), sem("weights_turned_read"), sem("heads_summed"), sem("heads_squared"),
            sem("head_squares_summed"), sem("head_roots"), sem("yb_ready"))
        tk_mm, tk_ev = sem("operands_turned"), sem("operands_by_position")
        t_mm, t_ev, t_init, w1_mm, w1_ev = (sem("solve_products"), sem("solve_read"), sem("solve_begun"),
                                            sem("akv_summed"), sem("akv_ready"))
        zy_mm, zy_ev, rb_mm, rb_ev = sem("zy_summed"), sem("zy_ready"), sem("read_products"), sem("read_ready")
        gm_ready = sem("state_factors_ready")
        u_mm, u_ready, s_mm, st_ready, o_mm, o_ev = (sem("u_summed"), sem("u_ready"), sem("state_summed"),
                                                     sem("state_ready"), sem("out_summed"), sem("out_ready"))
        gn_mm, gn_c, gn_sq, gn_rt, yc_ready = (sem("norm_summed"), sem("centred"), sem("centred_squared"),
                                               sem("norm_rooted"), sem("yc_ready"))
        ga_up = sem("gates_ready")
        mg_ready = sem("merged_ready")
        cv_step = sem("first_taps_done")
        u_begun, cv_done, gl_done, g_ready = sem("conv_begun"), sem("conv_done"), sem("gelu_done"), sem("hidden_ready")

        n_step, n_astep = [0], [0]

        def tick(n):
            n[0] += 1
            return 1

        block = ctx.enter_context(nc.Block())

        @block.sync
        def _(sp):
            sp.dma_start(C[:, :], consts).then_inc(s_par, 16)
            sp.dma_start(PR[:, :, :], params).then_inc(s_par, 16)
            sp.dma_start(E[:, 0:2, :].rearrange("p a b -> p (a b)"), lqk.partition_broadcast(P)).then_inc(s_par, 16)
            sp.dma_start(YA[:, 0, :].bitcast(I32), positions.partition_broadcast(P)).then_inc(s_par, 16)
            sp.dma_start(X[:, :, :], x_t).then_inc(s_par, 16)

            def pair(g, ahead=True):
                if g >= SLOTS:
                    sp.wait_ge(pair_done, g - SLOTS + 1)
                sp.dma_start(ring[:, g % SLOTS, :], wmain[g]).then_inc(s_w[g % SLOTS], 16)

            for l in range(L):
                for g in range(PAIRS * l, PAIRS * l + 4):
                    pair(g)
                if l:
                    sp.wait_ge(lr_mm, 4 * l)
                else:
                    sp.wait_ge(bd_zero, 1)
                sp.dma_start(SW[:, WL:WL + 1024], small[l, :, 0:1024]).then_inc(s_sw, 16)
                for i in range(2):
                    for par in range(2):
                        at = WA + W * i
                        sp.dma_start(SW[64 * par:64 * par + 64, at:at + W].rearrange("p (j m) -> p j m", j=4)
                                     [:, :, 64 * par:64 * par + 64],
                                     small[l, 64 * par:64 * par + 64, 1024 + 256 * i:1280 + 256 * i]
                                     .rearrange("p (j m) -> p j m", j=4)).then_inc(s_sw, 16)
                if l:
                    sp.wait_ge(pair_done, PAIRS * l)
                    sp.dma_start(V1, v1v2[:, 0:256].rearrange("p (k m) -> p k m", k=KT)).then_inc(s_v12, 16)
                    sp.dma_start(V2[0:32, :], v1v2[0:32, 256:768]).then_inc(s_v12, 16)
                for k in range(4, UP):
                    pair(PAIRS * l + k)
                with sp.Fori(0, (PAIRS - UP) // 4) as i:
                    for q in range(4):
                        g0 = PAIRS * l + UP + q
                        sp.wait_ge(pair_done, i * 4 + (g0 - SLOTS + 1))
                        sp.dma_start(ring[:, g0 % SLOTS, :], wmain[i * 4 + g0]).then_inc(s_w[g0 % SLOTS], 16)
            sp.wait_ge(h_pre, 8 * 5)
            sp.dma_start(y_t, H[:, :, :]).then_inc(s_out, 16)
            sp.wait_ge(s_out, 16)

        @block.gpsimd
        def _(pool):
            pool.memset(SW[:, WA:WA + 2 * W], 0.0).then_inc(bd_zero, 1)
            pool.memset(sm[:, ONE1:ONE1 + 1], 1.0).then_inc(bd_zero, 1)
            pool.memset(sm[:, EPS6:EPS6 + 1], 1e-6).then_inc(bd_zero, 1)
            pool.memset(sm[:, EPS5:EPS5 + 1], 1e-5).then_inc(bd_zero, 1)
            pool.memset(sm[:, EPSG:EPSG + 1], 64e-5).then_inc(bd_zero, 1)
            pool.memset(ones[:, :], 1.0).then_inc(bd_zero, 1)

            def mod_blocks(a, b):
                for n in range(a, b):
                    if n >= 2:
                        pool.wait_ge(mod_used, n - 1)
                    pool.dma_start(mring[:, n % 2, :], wmod[n]).then_inc(s_m[n % 2], 16)

            mod_blocks(0, 16)
            for l in range(L):
                if l == 0:
                    mod_blocks(16, 26)
                for tt in range(2):
                    base = NSTEP * (2 * l + tt)
                    for par in range(2):
                        pool.wait_ge(t_ev, base + step_no("n", par, 0) + 1)
                        if tt:
                            pool.wait_ge(t_mm, base + step_no("n", par, 0) + 1)
                        pool.tensor_tensor(Tm[:, par], Nm[:, par], over(mat(M_L1), 4), ALU.mult).then_inc(t_init, 1)
                        pool.wait_ge(t_init, 6 * (2 * l + tt) + 3 * par + 1)
                        pool.tensor_tensor(Tm[:, par], Tm[:, par], over(mat(IDENT), 4), ALU.add).then_inc(t_init, 1)
                        pool.wait_ge(t_ev, base + step_no("nt", par, 0) + 1)
                        pool.tensor_tensor(TTm[:, 2 * tt + par], TTm[:, 2 * tt + par], over(mat(IDENT), 4),
                                           ALU.add).then_inc(t_init, 1)
                pool.wait_ge(zy_ev, 4 * (l + 1))
                pool.wait_ge(yb_ready, 2 * (l + 1))
                for c in range(3):
                    gf = sm[:, GF:GF + 12].rearrange("p (j c) -> p j c", c=3)[:, :, c]
                    pool.tensor_tensor(GM[c], along(gf, P), over(mat(BLOCKS), 4), ALU.mult).then_inc(gm_ready, 1)
                if l == 0:
                    mod_blocks(26, 32)
                for n in range(8):
                    m = 2 * (n % 4)
                    br = 1 + n // 4
                    if l == 0 and n == 4:
                        mod_blocks(32, 42)
                    g = PAIRS * l + MG + 2 + n // 2
                    b = banks_of(g)[n % 2]
                    pool.wait_ge(bank_free[b], EMPTIED[g][b] + 1)
                    if n >= 4:
                        pool.wait_ge(mg_ready, 8 * l + n - 3)
                    pool.tensor_tensor(H[:, m:m + 2, :], H[:, m:m + 2, :], G[:, 8 * br + m:8 * br + m + 2, :],
                                       ALU.add).then_inc(mg_ready, 1)
                if l == 0:
                    mod_blocks(42, 96)

        @block.scalar
        def _(act):
            A = nc.scalar.activation
            act.wait_ge(s_par, 80)
            act.wait_ge(bd_zero, 6)
            A(sm[:, CSIL:CSIL + 8], PR[:, 0, COL["cc"]:COL["cc"] + 8], ACT.Tanh, scale=0.5).then_inc(pre_act, 1)
            act.wait_ge(pre_dve, 3)
            A(sm[:, 24:28], sm[:, 24:28], ACT.Exp).then_inc(pre_act, 1)
            A(sm[:, 40:48], sm[:, 40:48], ACT.Exp, scale=-1.0).then_inc(pre_act, 1)
            act.wait_ge(pre_act, 3)
            A(sm[:, 48:56], sm[:, 40:48], ACT.Ln, bias=sm[:, ONE1:ONE1 + 1]).then_inc(pre_act, 1)
            act.wait_ge(pre_dve, 5)
            A(SIN[:, :], RT[:, :], ACT.Sin).then_inc(pre_act, 1)
            A(COS[:, :], YA[:, 1, :], ACT.Sin).then_inc(pre_act, 1)

            def squares(n):
                for m in range(KT):
                    if n:
                        g = PAIRS * ((n - 1) // 2) + (OU if n % 2 else PAIRS - 4) + m // 2
                        act.wait_ge(bank_free[g % 4], EMPTIED[g][g % 4] + 1)
                    if m == 0 and n:
                        act.wait_ge(pair_done, PAIRS * ((n - 1) // 2) + (OU + 4 if n % 2 else PAIRS))
                    A(H[:, m, :], X[:, m, :], ACT.Square).then_inc(x_sq, 1)
                act.wait_ge(x_ss, n + 1)
                A(RT[:, :], ps[:, 4, 0:S], ACT.Sqrt, bias=sm[:, EPS6:EPS6 + 1], scale=1.0 / D).then_inc(x_rt, 1)

            def shifts(n, u):
                for m in range(KT):
                    act.wait_ge(h_pre, 8 * n + m + 1)
                    if m == 0:
                        act.wait_ge(mod_ready, u + 1)
                    A(H[:, m, :], H[:, m, :], ACT.Identity, bias=mod[:, u, m:m + 1]).then_inc(h_ready, 1)

            def evac(l, k, out, func=ACT.Identity, scale=1.0):
                g = PAIRS * l + k
                act.wait_ge(pair_done, g + 1)
                return A(out, duo(g % 4), func, scale=scale).then_inc(bank_free[g % 4], 1)

            for l in range(L):
                squares(2 * l)
                shifts(2 * l, 1 if l == 0 else 7)
                for k in range(0, 3):
                    evac(l, k, G[:, 2 * k:2 * k + 2, :])
                act.wait_ge(lora_z, 2 * l + 2)
                A(YA[0:64, 0, :], YA[0:64, 0, :], ACT.Tanh).then_inc(lora_t, 1)
                A(YA[:, 1, :], YA[:, 1, :], ACT.Tanh, scale=0.5).then_inc(lora_t, 1)
                act.wait_ge(lora_t, 3 * l + 2)
                A(YA[:, 1, :], YA[:, 1, :], ACT.Copy, scale=0.5, bias=0.5).then_inc(lora_t, 1)
                evac(l, 3, G[:, 6:8, :])
                base = 10 * l
                for i, (dst, h) in enumerate(((LD, 0), (AB, 4))):
                    act.wait_ge(lora_mm, 3 * l + i + 1)
                    for j in range(4):
                        A(dst[:, j, :], duo(4 + 2 * i + j // 2)[:, j % 2, :], ACT.Tanh, scale=0.5,
                          bias=PH[:, l, h + j:h + j + 1]).then_inc(lora_act, 1)
                evac(l, 4, G[:, 8:10, :])
                evac(l, 5, G[:, 10:12, :])
                act.wait_ge(lora_mm, 3 * l + 3)
                for b in range(2):
                    A(GG[:, 2 * b:2 * b + 2, :], duo(4 + b), ACT.Copy).then_inc(lora_act, 1)
                evac(l, 6, G[:, 12:14, :])
                if l:
                    act.wait_ge(zv_up, 1)
                    A(RT[0:32, :], ps[0:32, 6, 0:S], ACT.Copy).then_inc(zv_up, 1)
                    act.wait_ge(zv_up, 3)
                    for j in range(4):
                        A(E[:, j, :], duo(6 + j // 2)[:, j % 2, :], ACT.Tanh, scale=0.5,
                          bias=PH[:, l, 8 + j:9 + j]).then_inc(zv_up, 1)
                for k in (LR, LR + 1):
                    evac(l, k, ZX[:, 2 * (k - LR):2 * (k - LR) + 2, :])
                act.wait_ge(kk_raw, 4 * l + 4)
                if l:
                    act.wait_ge(v_ready, 2)
                A(E[:, :, :], KK[:, :, :], ACT.Square).then_inc(kk_sq, 1)
                act.wait_ge(kk_mm, l + 1)
                for b in range(2):
                    A(E[:, 2 * b:2 * b + 2, :], duo(4 + b), ACT.Sqrt).then_inc(kk_rt, 1)
                for k in (LR + 2, LR + 3):
                    if k == LR + 2:
                        act.wait_ge(lora_mm, 3 * l + 3)
                    evac(l, k, YA[:, 2 * (k - LR) - 4:2 * (k - LR) - 2, :], ACT.Gelu_apprx_tanh)
                act.wait_ge(cc_ready, l + 1)
                act.wait_ge(kk_used, l + 1)
                A(sm[:, GF:GF + 12], sm[:, GF:GF + 12], ACT.Exp).then_inc(exps, 1)
                A(E[:, :, :], CUM, ACT.Exp).then_inc(exps, 1)
                A(LRI, CUM, ACT.Exp, scale=-1.0).then_inc(exps, 1)
                act.wait_ge(cm_ready, l + 1)
                A(LRA, LRA, ACT.Exp).then_inc(exps, 1)
                for k in range(AT, AT + 6):
                    if l and k == AT:
                        act.wait_ge(v_ready, 2)
                    g = PAIRS * l + k
                    act.wait_ge(pair_done, g + 1)
                    A(R[:, 2 * (k - AT):2 * (k - AT) + 2, :], duo(g % 4), ACT.Identity).then_inc(bank_free[g % 4], 1)
                for t in range(2):
                    act.wait_ge(avt_mm, 2 * l + t + 1)
                    A(AVT[:, t, :], ps[:, 4 + t, :], ACT.Copy).then_inc(avt_ev, 1)
                act.wait_ge(feat, 4 * (l + 1))
                for i in range(2):
                    for j in range(4):
                        act.wait_ge(lr_mm, 4 * l + 2 * i + j // 2 + 1)
                        A((LRA if i == 0 else LRI)[:, j, :], duo((4 if i == 0 else 6) + j // 2)[:, j % 2, :], ACT.Tanh, scale=0.5,
                          bias=PH[:, l, 12 + 4 * i + j:13 + 4 * i + j]).then_inc(lr_act, 1)
                gates_out = [0]

                def gates(point):
                    done = int(FILLED[point]) if point < len(FILL) else 12
                    while gates_out[0] < done:
                        k = GA + gates_out[0]
                        g = PAIRS * l + k
                        act.wait_ge(pair_done, g + 1)
                        if k == GA:
                            act.wait_ge(feat, 4 * (l + 1))
                        A(G[:, 2 * (k - GA):2 * (k - GA) + 2, :], duo(g % 4), ACT.Tanh, scale=0.5).then_inc(bank_free[g % 4], 1)
                        gates_out[0] += 1

                gates(0)
                act.wait_ge(la_ready, 4 * (l + 1))
                A(E[:, :, :], LRA, ACT.Exp).then_inc(la_act, 1)
                A(ZX, LRA, ACT.Tanh).then_inc(la_act, 1)
                gates(1)
                act.wait_ge(lq_ready, l + 1)
                A(LRA, LRA, ACT.Sqrt).then_inc(lq_rt, 1)
                for tt in range(2):
                    gates(2 + tt)
                    act.wait_ge(mx_ready, 2 * l + tt + 1)
                    sc = S0 if tt == 0 else S1
                    for c in range(2):
                        for h in range(4):
                            A(sc[:, c, h, :], sc[:, c, h, :], ACT.Exp, scale=0.125, bias=sm[:, MX + 4 * c + h:MX + 4 * c + h + 1],
                              accum_out=sm[:, LSUM + 4 * c + h:LSUM + 4 * c + h + 1]).then_inc(p_exp, 1)
                gates(4)
                for n, (kt, qt) in enumerate(((0, 0), (0, 1), (1, 1))):
                    act.wait_ge(pt_mm, 3 * l + n + 1)
                    A(PT[:, kt, :, qt * P:(qt + 1) * P], quad(4 + n), ACT.Copy).then_inc(pt_ev, 1)
                gates(5)
                for n, b in enumerate((7, 4)):
                    act.wait_ge(ao_mm, 2 * l + n + 1)
                    A(E[:, 2 * n:2 * n + 2, :], duo(b), ACT.Square).then_inc(ao_sq, 1)
                for n in range(2):
                    act.wait_ge(as_mm, 2 * l + n + 1)
                    A(E[:, 2 * n:2 * n + 2, :], duo(5 + n), ACT.Sqrt, scale=1.0 / P, bias=sm[:, EPS5:EPS5 + 1]).then_inc(as_rt, 1)
                gates(6)
                for n in range(8):
                    act.wait_ge(tk_mm, 8 * l + n + 1)
                    if n == 0:
                        act.wait_ge(ya_ready, 4 * (l + 1))
                        act.wait_ge(pt_mm, 3 * (l + 1))
                    A(tok(n // 2)[:, n % 2, :], ps[:, 4 + n % 4, :], ACT.Copy).then_inc(tk_ev, 1)
                gates(7)
                for tt in range(2):
                    act.wait_ge(w1_mm, 2 * l + tt + 1)
                    A(WY[:, tt, :], ps[:, 6, :], ACT.Copy).then_inc(w1_ev, 1)
                    for v in range(5):
                        gates(8 + 5 * tt + v)
                for n in range(4):
                    act.wait_ge(zy_mm, 4 * l + n + 1)
                    if n < 2:
                        A(KK[:, :, n * P:(n + 1) * P], quad(4 + n), ACT.Copy).then_inc(zy_ev, 1)
                    else:
                        A(WY[:, n - 2, :], ps[:, 4 + n, :], ACT.Copy).then_inc(zy_ev, 1)
                gates(99)
                for tt in range(2):
                    act.wait_ge(o_mm, 2 * l + tt + 1)
                    A(AB[:, :, tt * P:(tt + 1) * P], quad(6 + tt), ACT.Copy).then_inc(o_ev, 1)
                act.wait_ge(gn_c, 2 * l + 2)
                A(E[:, :, :], AB[:, :, :], ACT.Square).then_inc(gn_sq, 1)
                for b in range(2):
                    act.wait_ge(gn_mm, 4 * l + 3 + b)
                    A(E[:, 2 * b:2 * b + 2, :], duo(6 + b), ACT.Sqrt, scale=1.0 / 64, bias=sm[:, EPSG:EPSG + 1]).then_inc(gn_rt, 1)
                squares(2 * l + 1)
                shifts(2 * l + 1, 3 if l == 0 else 9)
                g0 = PAIRS * l + UP

                def begin(i, q, first=False):
                    b = (g0 + q) % 4
                    act.wait_ge(pair_done, i * 4 + (g0 + q + 1))
                    if not (first and q < 2):
                        act.wait_ge(g_ready, i * 4 + (FT * l + q - 1))
                    for t in range(2):
                        j = i * 4 + (q + FT * t)
                        A(UB[:, q % 2, t, :], duo(b)[:, t, :], ACT.Identity, scale=PR[:, l, bass.ds(j + (COL["fw"] + 96), 1)],
                          bias=PR[:, l, bass.ds(j + COL["fb"], 1)]).then_inc(u_begun, 1)

                def gelu(i, q):
                    act.wait_ge(cv_done, i * 4 + (FT * l + q + 1))
                    A(UB[:, q % 2, 0, :], UB[:, q % 2, 0, :], ACT.Gelu_apprx_tanh).then_inc(gl_done, 1)

                for q in range(4):
                    begin(0, q, True)
                    if q:
                        gelu(0, q - 1)
                with act.Fori(1, FT // 4) as i:
                    for q in range(4):
                        begin(i, q)
                        gelu(i, q - 1)
                gelu(0, FT - 1)
            squares(4)

        @block.vector
        def _(dve):
            V = nc.vector

            def after():
                dve.wait_ge(step, n_step[0])

            dve.wait_ge(s_par, 80)
            dve.wait_ge(bd_zero, 6)
            for l in range(L):
                V.tensor_scalar(PH[:, l, :], PR[:, l, COL["w0"]:COL["w0"] + 20], 0.5, None, ALU.mult).then_inc(step, tick(n_step))
            lq = E[:, 0:2, :].rearrange("p a b -> p (a b)").rearrange("p (n two d) -> p n two d", n=4, two=2)
            V.tensor_tensor(E[:, 2, :].rearrange("p (n d) -> p n d", n=4), lq[:, :, 0, :], lq[:, :, 1, :], ALU.mult).then_inc(step, tick(n_step))
            after()
            V.reduce_sum(sm[:, 24:28], E[:, 2, :].rearrange("p (n d) -> p n d", n=4), AX_X).then_inc(pre_dve, 1)
            for l in range(L):
                lam = col(l, "lam", 0, 4)
                V.scalar_tensor_tensor(sm[:, 40 + 4 * l:44 + 4 * l], lam, -1.0, lam, ALU.mult, ALU.max).then_inc(pre_dve, 1)
            ang, k1, red = YA[:, 2, :], YA[:, 3, :], RT[:, :]
            V.tensor_copy(YA[:, 1, :], YA[:, 0, :].bitcast(I32)).then_inc(step, tick(n_step))
            after()
            V.tensor_scalar(ang, YA[:, 1, :], C[:, FREQ:FREQ + 1], None, ALU.mult).then_inc(step, tick(n_step))
            for n, out in enumerate((red, YA[:, 1, :])):
                after()
                V.tensor_scalar(k1, ang, 1.0 / SQ2PI, 0.25 * n, ALU.mult, ALU.add).then_inc(step, tick(n_step))
                after()
                V.tensor_scalar(k1, k1, MAGIC, None, ALU.add).then_inc(step, tick(n_step))
                after()
                V.tensor_scalar(k1, k1, -MAGIC, None, ALU.add).then_inc(step, tick(n_step))
                after()
                V.scalar_tensor_tensor(out, k1, -C1, ang, ALU.mult, ALU.add).then_inc(step, tick(n_step))
                after()
                V.scalar_tensor_tensor(out, k1, -C2, out, ALU.mult, ALU.add).then_inc(step, tick(n_step))
                after()
                V.scalar_tensor_tensor(out, k1, -C3, out, ALU.mult, ALU.add).then_inc(step, tick(n_step))
                after()
                V.tensor_scalar(out, out, 0.5 * math.pi * n, PI_IN, ALU.add, ALU.min).then_inc(step, tick(n_step))
                after()
                V.tensor_scalar(out, out, -PI_IN, None, ALU.max).then_inc(pre_dve, 1)
            dve.wait_ge(pre_act, 1)
            V.scalar_tensor_tensor(sm[:, CSIL:CSIL + 8], sm[:, CSIL:CSIL + 8], 1.0, PR[:, 0, COL["cc"]:COL["cc"] + 8],
                                   ALU.add, ALU.mult).then_inc(step, tick(n_step))
            after()
            V.tensor_scalar(sm[:, CSIL:CSIL + 8], sm[:, CSIL:CSIL + 8], 0.5, None, ALU.mult).then_inc(step, tick(n_step))
            dve.wait_ge(pre_act, 4)
            for l in range(L):
                lam = col(l, "lam", 0, 4)
                V.tensor_tensor(sm[:, NLAM + l:NLAM + l + 1], sm[:, 25 + 2 * l:26 + 2 * l], sm[:, 24 + 2 * l:25 + 2 * l],
                                ALU.subtract).then_inc(step, tick(n_step))
                after()
                V.tensor_scalar(sm[:, NLAM + l:NLAM + l + 1], sm[:, NLAM + l:NLAM + l + 1], -lambda_init(l), None,
                                ALU.add).then_inc(step, tick(n_step))
                V.tensor_scalar(sm[:, SUBG + l:SUBG + l + 1], col(l, "sub"), 1.0 - lambda_init(l), None, ALU.mult).then_inc(step, tick(n_step))
                V.tensor_scalar(sm[:, N8 + 4 * l:N8 + 4 * l + 4], lam, -1.0, 0.0, ALU.mult, ALU.max).then_inc(step, tick(n_step))
                after()
                V.tensor_tensor(sm[:, N8 + 4 * l:N8 + 4 * l + 4], sm[:, N8 + 4 * l:N8 + 4 * l + 4], sm[:, 48 + 4 * l:52 + 4 * l],
                                ALU.add).then_inc(step, tick(n_step))
                after()
                V.tensor_scalar(sm[:, N8 + 4 * l:N8 + 4 * l + 4], sm[:, N8 + 4 * l:N8 + 4 * l + 4], -4.0, None,
                                ALU.mult).then_inc(step, tick(n_step))
            after()
            dve.wait_ge(pre_act, 6)

            def mod_loop_block(i, kt):
                dve.wait_ge(s_m[kt % 2], i * 64 + (16 * (20 + kt // 2) + 16))
                if kt == 0:
                    dve.wait_ge(mod_mm, i + 5)
                    V.tensor_scalar(macc[:, :], mring[:, 0, :], sm[:, CSIL:CSIL + 1], None, ALU.mult).then_inc(mod_used, 1)
                else:
                    dve.wait_ge(mod_used, i * 8 + (40 + kt))
                    V.scalar_tensor_tensor(macc[:, :], mring[:, kt % 2, :], sm[:, CSIL + kt:CSIL + kt + 1], macc[:, :],
                                           ALU.mult, ALU.add).then_inc(mod_used, 1)

            def mod_block(n):
                u, kt = divmod(n, 8)
                dve.wait_ge(s_m[n % 2], 16 * (n // 2 + 1))
                if kt == 0:
                    if u:
                        dve.wait_ge(mod_mm, u)
                    V.tensor_scalar(macc[:, :], mring[:, n % 2, :], sm[:, CSIL:CSIL + 1], None, ALU.mult).then_inc(mod_used, 1)
                else:
                    dve.wait_ge(mod_used, n)
                    V.scalar_tensor_tensor(macc[:, :], mring[:, n % 2, :], sm[:, CSIL + kt:CSIL + kt + 1], macc[:, :],
                                           ALU.mult, ALU.add).then_inc(mod_used, 1)

            def mod_vector(u):
                dve.wait_ge(mod_mm, u + 1)
                lay = 0 if u < 6 else 1
                V.tensor_tensor(mod[:, u, :], ps[:, 7, 0:8], col(lay, "bmod", 8 * (u % 6), 8), ALU.add).then_inc(mod_ready, 1)

            def mod_unit(u):
                for kt in range(8):
                    mod_block(8 * u + kt)
                mod_vector(u)

            mod_unit(0)
            mod_unit(1)

            def norm(n, gain, u):
                if u is None:
                    A_ = gain
                else:
                    dve.wait_ge(mod_ready, u + 1)
                    V.scalar_tensor_tensor(Acol[:, :], mod[:, u, :], 1.0, gain, ALU.add, ALU.mult).then_inc(step, tick(n_step))
                    A_ = Acol
                dve.wait_ge(x_rt, n + 1)
                V.reciprocal(RT[:, :], RT[:, :]).then_inc(step, tick(n_step))
                after()
                for m in range(KT):
                    V.scalar_tensor_tensor(H[:, m, :], X[:, m, :], A_[:, m:m + 1], RT[:, :], ALU.mult, ALU.mult).then_inc(h_pre, 1)

            def shift(src, dst, n, l, mu, out=None):
                V.tensor_tensor(dst[:, :, 1:S], src[:, :, 0:S - 1], src[:, :, 1:S], ALU.subtract).then_inc(step, tick(n_step))
                V.tensor_scalar(dst[:, :, 0:1], src[:, :, 0:1], -1.0, None, ALU.mult).then_inc(step, tick(n_step))
                after()
                for j in range(n):
                    i = V.scalar_tensor_tensor(dst[:, j, :], dst[:, j, :], col(l, "mu", mu + j), src[:, j, :], ALU.mult, ALU.add)
                    if out is None:
                        i.then_inc(step, tick(n_step))
                    else:
                        i.then_inc(out, 1)

            for l in range(L):
                norm(2 * l, col(l, "n1g", 0, 8), 0 if l == 0 else 6)
                mod_unit(2 if l == 0 else 11)
                dve.wait_ge(bank_free[(PAIRS * l) % 4], EMPTIED[PAIRS * l][(PAIRS * l) % 4] + 1)
                shift(G[:, 0:2, :], YA[:, 0:2, :], 2, l, 0, lora_z)
                for k in (1, 2):
                    g = PAIRS * l + k
                    dve.wait_ge(bank_free[g % 4], EMPTIED[g][g % 4] + 1)
                shift(G[:, 2:6, :], K_, 4, l, 2)
                after()
                for j in range(4):
                    V.tensor_scalar(KK[:, j, :], K_[:, j, :], col(l, "kk", j), None, ALU.mult).then_inc(kk_raw, 1)
                if l:
                    V.tensor_copy(VF, V_).then_inc(vf_moved, 1)
                dve.wait_ge(lora_act, 10 * l + 8)
                V.tensor_scalar(AB[:, :, :], AB[:, :, :], 0.5, 0.5, ALU.mult, ALU.add).then_inc(step, tick(n_step))
                V.tensor_scalar(LD, LD, -0.5 * EM05, -0.5 * EM05, ALU.mult, ALU.add).then_inc(step, tick(n_step))
                after()
                for j in range(4):
                    V.tensor_tensor_scan(CUM[:, j, :], C[:, RESET:RESET + S], LD[:, j, :], 0.0, ALU.mult, ALU.add).then_inc(step, tick(n_step))
                for k in (3, 4):
                    g = PAIRS * l + k
                    dve.wait_ge(bank_free[g % 4], EMPTIED[g][g % 4] + 1)
                shift(G[:, 6:10, :], R_, 4, l, 6)
                after()
                cum4 = CUM.rearrange("p j (c t) -> p (j c) t", t=CH)
                mids = sm[:, MIDS:MIDS + 16]
                V.tensor_copy(mids, cum4[:, :, CH // 2 - 1]).then_inc(step, tick(n_step))
                after()
                V.tensor_tensor(cum4, cum4, along(mids, CH), ALU.subtract).then_inc(step, tick(n_step))
                after()
                V.tensor_tensor(sm[:, GF:GF + 12].rearrange("p (j c) -> p j c", c=3),
                                cum4.rearrange("p (j c) t -> p j c t", c=NCH)[:, :, 0:3, CH - 1],
                                mids.rearrange("p (j c) -> p j c", c=NCH)[:, :, 1:4], ALU.add).then_inc(cc_ready, 1)
                for j in range(4):
                    V.tensor_scalar(BON[:, j, :], AB[:, j, :], -1.0, col(l, "ka", j), ALU.add, ALU.mult).then_inc(step, tick(n_step))
                after()
                V.scalar_tensor_tensor(K_, BON[:, :, :], 1.0, K_, ALU.add, ALU.mult).then_inc(step, tick(n_step))
                after()
                for k in (5, 6):
                    g = PAIRS * l + k
                    dve.wait_ge(bank_free[g % 4], EMPTIED[g][g % 4] + 1)
                if l:
                    dve.wait_ge(vf_moved, 1)
                shift(G[:, 10:14, :], V_, 4, l, 10)
                after()
                for j in range(4):
                    V.scalar_tensor_tensor(BON[:, j, :], R_[:, j, :], col(l, "rk", j), K_[:, j, :], ALU.mult, ALU.mult).then_inc(rk_ready, 1)
                if l:
                    dve.wait_ge(zv_up, 2)
                    zv, zd = RT[0:32, :], Acol
                    V.tensor_tensor(YB[0:32, 2, 1:S], zv[:, 0:S - 1], zv[:, 1:S], ALU.subtract).then_inc(step, tick(n_step))
                    V.tensor_scalar(YB[0:32, 2, 0:1], zv[:, 0:1], -1.0, None, ALU.mult).then_inc(step, tick(n_step))
                    after()
                    V.scalar_tensor_tensor(YB[0:32, 2, :], YB[0:32, 2, :], PR[0:32, l, COL["vmu"]:COL["vmu"] + 1], zv,
                                           ALU.mult, ALU.add).then_inc(zv_ready, 1)
                    V.tensor_tensor(VF, VF, V_, ALU.subtract).then_inc(step, tick(n_step))
                    dve.wait_ge(zv_up, 7)
                    V.tensor_scalar(E[:, :, :], E[:, :, :], 0.5, 0.5, ALU.mult, ALU.add).then_inc(step, tick(n_step))
                    after()
                    V.tensor_tensor(E[:, :, :], E[:, :, :], VF, ALU.mult).then_inc(v_ready, 1)
                    dve.wait_ge(v_ready, 1)
                    V.tensor_tensor(V_, V_, E[:, :, :], ALU.add).then_inc(v_ready, 1)
                dve.wait_ge(kk_rt, 2 * (l + 1))
                V.tensor_scalar(E[:, :, :], E[:, :, :], 1e-12, None, ALU.max).then_inc(step, tick(n_step))
                after()
                V.reciprocal(E[:, :, :], E[:, :, :]).then_inc(step, tick(n_step))
                after()
                V.tensor_tensor(KK[:, :, :], KK[:, :, :], E[:, :, :], ALU.mult).then_inc(kk_used, 1)
                V.tensor_tensor(LRA, CUM, LD, ALU.subtract).then_inc(cm_ready, 1)
                dve.wait_ge(kk_used, l + 1)
                V.tensor_tensor(AB[:, :, :], AB[:, :, :], KK[:, :, :], ALU.mult).then_inc(step, tick(n_step))
                if l:
                    dve.wait_ge(v_ready, 2)
                dve.wait_ge(bon_mm, l + 1)
                for b in range(2):
                    V.tensor_tensor(BON[:, 2 * b:2 * b + 2, :], duo(6 + b), V_[:, 2 * b:2 * b + 2, :], ALU.mult).then_inc(bon_ready, 1)
                dve.wait_ge(exps, 4 * l + 2)
                V.tensor_tensor(R_, R_, E[:, :, :], ALU.mult).then_inc(feat, 1)
                dve.wait_ge(exps, 4 * l + 3)
                V.tensor_tensor(K_, K_, LRI, ALU.mult).then_inc(feat, 1)
                after()
                V.tensor_tensor(AB[:, :, :], AB[:, :, :], LRI, ALU.mult).then_inc(feat, 1)
                dve.wait_ge(exps, 4 * l + 4)
                V.scalar_tensor_tensor(KK[:, :, :], KK[:, :, :], -1.0, LRA, ALU.mult, ALU.mult).then_inc(feat, 1)
                for b in range(4):
                    g = PAIRS * l + AT + b
                    dve.wait_ge(bank_free[g % 4], EMPTIED[g][g % 4] + 1)
                    dve.wait_ge(rot_mm, 4 * l + b + 1)
                    tmp = R[:, 16 + 2 * b:18 + 2 * b, :]
                    qk = QK[:, 2 * b:2 * b + 2, :]
                    V.tensor_tensor(tmp, duo(4 + b), over(SIN[:, :], 2), ALU.mult).then_inc(rope_mul, 1)
                    V.tensor_tensor(qk, qk, over(COS[:, :], 2), ALU.mult).then_inc(step, tick(n_step))
                    after()
                    dve.wait_ge(rope_mul, 4 * l + b + 1)
                    V.tensor_tensor(qk, qk, tmp, ALU.add).then_inc(qk_ready, 1)
                for k in (LR, LR + 1):
                    g = PAIRS * l + k
                    dve.wait_ge(bank_free[g % 4], EMPTIED[g][g % 4] + 1)
                for j in range(4):
                    V.tensor_scalar(XC[:, j, :], ZX[:, j, :], col(l, "cw", 12 + j), col(l, "cb", j), ALU.mult, ALU.add).then_inc(step, tick(n_step))
                for d in (1, 2, 3):
                    after()
                    for j in range(4):
                        i = V.scalar_tensor_tensor(XC[:, j, d:S], ZX[:, j, 0:S - d], col(l, "cw", 4 * (3 - d) + j), XC[:, j, d:S],
                                                   ALU.mult, ALU.add)
                        if d == 3:
                            i.then_inc(xc_ready, 1)
                        else:
                            i.then_inc(step, tick(n_step))

                def read_scores(tt):
                    sc = S0 if tt == 0 else S1
                    for n, (t, c, h0, nh) in enumerate(SCORES):
                        if t != tt:
                            continue
                        dve.wait_ge(sc_mm, 6 * l + n + 1)
                        b = SCORE_BANK[n]
                        if tt == 0:
                            V.tensor_tensor(sc[:, c], quad(b), over(C[:, NEG0 + P:NEG0 + 2 * P], 4), ALU.add).then_inc(sc_read, 1)
                        else:
                            V.tensor_tensor(sc[:, c, h0:h0 + 2, :], duo(b), over(C[:, NEG0:NEG0 + 2 * P], 2), ALU.add).then_inc(sc_read, 1)
                    dve.wait_ge(sc_read, 6 * l + (2 if tt == 0 else 6))
                    if tt:
                        dve.wait_ge(p_exp, 16 * l + 8)
                    V.reduce_max(sm[:, MX:MX + 8].rearrange("p (c h) -> p c h", c=2), sc, AX_X).then_inc(step, tick(n_step))
                    after()
                    V.tensor_scalar(sm[:, MX:MX + 8], sm[:, MX:MX + 8], -0.125, None, ALU.mult).then_inc(mx_ready, 1)

                def weights(tt):
                    sc = S0 if tt == 0 else S1
                    dve.wait_ge(p_exp, 16 * l + 8 * (tt + 1))
                    V.reciprocal(sm[:, LSUM:LSUM + 8], sm[:, LSUM:LSUM + 8]).then_inc(step, tick(n_step))
                    after()
                    V.tensor_scalar(sm[:, LSUM + 4:LSUM + 8], sm[:, LSUM + 4:LSUM + 8], sm[:, NLAM + l:NLAM + l + 1], None,
                                    ALU.mult).then_inc(step, tick(n_step))
                    for h in range(4):
                        V.tensor_scalar(sc[:, 0, h, :], sc[:, 0, h, :], sm[:, LSUM + h:LSUM + h + 1], None, ALU.mult).then_inc(step, tick(n_step))
                    after()
                    for h in range(4):
                        V.scalar_tensor_tensor(sc[:, 0, h, :], sc[:, 1, h, :], sm[:, LSUM + 4 + h:LSUM + 5 + h], sc[:, 0, h, :],
                                               ALU.mult, ALU.add).then_inc(p_ready, 1)

                read_scores(0)
                for j in range(4):
                    dve.wait_ge(lr_act, 8 * l + j + 1)
                    V.tensor_scalar(LRA[:, j, :], LRA[:, j, :], 1.0, sm[:, N8 + 4 * l + j:N8 + 4 * l + j + 1], ALU.add, ALU.mult).then_inc(la_ready, 1)
                dve.wait_ge(lr_act, 8 * (l + 1))
                dve.wait_ge(xc_ready, 4 * (l + 1))
                V.scalar_tensor_tensor(XC, LRI, 1.0, XC, ALU.add, ALU.mult).then_inc(step, tick(n_step))
                dve.wait_ge(la_act, 2 * (l + 1))
                V.tensor_scalar(LRA, ZX, -1.0, 1.0, ALU.mult, ALU.add).then_inc(step, tick(n_step))
                after()
                V.reciprocal(LRA, LRA).then_inc(step, tick(n_step))
                after()
                V.scalar_tensor_tensor(LRA, ZX, -2.0, LRA, ALU.mult, ALU.mult).then_inc(lq_ready, 1)
                weights(0)
                dve.wait_ge(lq_rt, l + 1)
                V.scalar_tensor_tensor(LRI, LRA, 0.5, XC, ALU.mult, ALU.mult).then_inc(step, tick(n_step))
                after()
                for j in range(4):
                    V.tensor_tensor_scan(ZX[:, j, :], E[:, j, :], LRI[:, j, :], 0.0, ALU.mult, ALU.add).then_inc(step, tick(n_step))
                after()
                for k in (LR + 2, LR + 3):
                    g = PAIRS * l + k
                    dve.wait_ge(bank_free[g % 4], EMPTIED[g][g % 4] + 1)
                for j in range(4):
                    V.tensor_tensor(YA[:, j, :], YA[:, j, :], ZX[:, j, :], ALU.mult).then_inc(ya_ready, 1)
                read_scores(1)
                weights(1)
                for n, b in enumerate((7, 4)):
                    dve.wait_ge(as_rt, 2 * l + n + 1)
                    e = E[:, 2 * n:2 * n + 2, :]
                    V.reciprocal(e, e).then_inc(step, tick(n_step))
                    after()
                    V.scalar_tensor_tensor(YB[:, 2 * n:2 * n + 2, :], duo(b), sm[:, SUBG + l:SUBG + l + 1], e,
                                           ALU.mult, ALU.mult).then_inc(yb_ready, 1)
                for tt in range(2):
                    base = NSTEP * (2 * l + tt)
                    for n, (kind, par, v, b) in enumerate(STEPS):
                        dve.wait_ge(t_mm, base + n + 1)
                        if kind == "ak":
                            V.tensor_tensor(Mm[:, par], quad(b), over(mat(M_UP), 4), ALU.mult).then_inc(t_ev, 1)
                        elif kind == "n":
                            V.tensor_tensor(Nm[:, par], quad(b), over(mat(M_LOW), 4), ALU.mult).then_inc(t_ev, 1)
                        elif kind == "nt":
                            V.tensor_tensor(TTm[:, 2 * tt + par], quad(b), over(mat(M_U1), 4), ALU.mult).then_inc(t_ev, 1)
                        elif kind == "m":
                            V.tensor_tensor(Mm[:, par], quad(b), over(mat(LEVELS[v]), 4), ALU.mult).then_inc(t_ev, 1)
                        elif kind == "x":
                            T_ = TTm[:, 2 * tt + par]
                            V.tensor_tensor(T_, T_, quad(b), ALU.add).then_inc(t_ev, 1)
                        else:
                            T_ = Tm[:, par]
                            V.tensor_tensor(T_, T_, quad(b), ALU.add).then_inc(t_ev, 1)
                for n in range(8):
                    dst = (RKm if n % 2 == 0 else RBm)[:, n // 2]
                    dve.wait_ge(rb_mm, 8 * l + n + 1)
                    V.tensor_tensor(dst, quad(4 + n % 4), over(mat(M_UPI), 4), ALU.mult).then_inc(rb_ev, 1)
                for c in range(NCH):
                    tt, rows = c // 2, slice(64 * (c % 2), 64 * (c % 2) + 64)
                    if c:
                        dve.wait_ge(u_mm, 3 * l + c)
                        V.tensor_tensor(WY[rows, tt, :], ps[rows, 4, :], WY[rows, tt, :], ALU.add).then_inc(u_ready, 1)
                    if c < NCH - 1:
                        dve.wait_ge(s_mm, 3 * l + c + 1)
                        dve.wait_ge(gm_ready, 3 * l + c + 1)
                        if c == 0:
                            V.tensor_tensor(ST, quad(5), GM[c], ALU.mult).then_inc(st_ready, 1)
                        else:
                            dve.wait_ge(st_ready, 3 * l + c)
                            V.tensor_tensor(ST, ST, quad(5), ALU.add).then_inc(step, tick(n_step))
                            after()
                            V.tensor_tensor(ST, ST, GM[c], ALU.mult).then_inc(st_ready, 1)

                def gated(p):
                    br, half = p // 2, p % 2
                    g = PAIRS * l + MG + p
                    dve.wait_ge(pair_done, g + 1)
                    for i, b in enumerate(banks_of(g)):
                        m = 4 * half + 2 * i
                        gate = G[:, 8 * br + m:8 * br + m + 2, :]
                        dst = H[:, m:m + 2, :] if br == 0 else gate
                        V.scalar_tensor_tensor(dst, gate, 1.0, duo(b), ALU.add, ALU.mult).then_inc(bank_free[b], 1)

                gk = PAIRS * l + GA
                for k in range(8, 12):
                    dve.wait_ge(bank_free[(gk + k) % 4], EMPTIED[gk + k][(gk + k) % 4] + 1)
                for p in range(4):
                    gated(p)
                for b in range(2):
                    dve.wait_ge(gn_mm, 4 * l + 1 + b)
                    o = AB[:, 2 * b:2 * b + 2, :]
                    V.scalar_tensor_tensor(o, duo(4 + b), -1.0 / 64, o, ALU.mult, ALU.add).then_inc(gn_c, 1)
                dve.wait_ge(gn_rt, 2 * (l + 1))
                V.reciprocal(E[:, :, :], E[:, :, :]).then_inc(step, tick(n_step))
                after()
                V.tensor_tensor(AB[:, :, :], AB[:, :, :], E[:, :, :], ALU.mult).then_inc(step, tick(n_step))
                after()
                for j in range(4):
                    V.tensor_scalar(AB[:, j, :], AB[:, j, :], col(l, "lng", j), col(l, "lnb", j), ALU.mult, ALU.add).then_inc(step, tick(n_step))
                after()
                V.tensor_tensor(AB[:, :, :], AB[:, :, :], BON[:, :, :], ALU.add).then_inc(step, tick(n_step))
                after()
                V.tensor_tensor(AB[:, :, :], AB[:, :, :], GG[:, :, :], ALU.mult).then_inc(yc_ready, 1)
                if l == 0:
                    mod_unit(3)
                for p in (4, 5):
                    gated(p)
                if l == 0:
                    mod_unit(4)
                u = 2 if l == 0 else 8
                dve.wait_ge(mod_ready, u + 1)
                V.tensor_scalar(sm[:, FH:FH + 8], mod[:, u, :], 0.5, None, ALU.mult).then_inc(step, tick(n_step))
                after()

                def residuals(g0, scale):
                    for g in range(g0, g0 + 4):
                        dve.wait_ge(pair_done, g + 1)
                        for i in range(2):
                            m = 2 * (g - g0) + i
                            ins = V.scalar_tensor_tensor(X[:, m, :], duo(g % 4)[:, i, :], scale[:, m:m + 1], X[:, m, :],
                                                         ALU.mult, ALU.add)
                        ins.then_inc(bank_free[g % 4], 1)

                residuals(PAIRS * l + OU, sm[:, FH:FH + 8])
                norm(2 * l + 1, col(l, "n2g", 0, 8), 4 if l == 0 else 10)
                g0 = PAIRS * l + UP

                def conv_read(i, q):
                    if q < 0:
                        return i + EMPTIED[g0 + q + 4][(g0 + q) % 4]
                    return i + (EMPTIED[g0 + q][(g0 + q) % 4] + 1)

                def taps(i, q):
                    b = (g0 + q) % 4
                    for d in (1, 2):
                        for t in range(2):
                            j = i * 4 + (q + FT * t)
                            dve.wait_ge(u_begun if d == 1 else cv_step, i * 8 + (2 * (FT * l + q) + (2 if d == 1 else 1 + t)))
                            ins = V.scalar_tensor_tensor(UB[:, q % 2, t, d:S], duo(b)[:, t, 0:S - d],
                                                         PR[:, l, bass.ds(j + (COL["fw"] + 48 * (2 - d)), 1)], UB[:, q % 2, t, d:S],
                                                         ALU.mult, ALU.add)
                            ins.then_inc(cv_step if d == 1 else (cv_done, bank_free[b])[t], 1)

                def product(i, q):
                    dve.wait_ge(gl_done, i * 4 + (FT * l + q + 1))
                    dve.wait_ge(bank_free[(g0 + q) % 4], conv_read(i, q))
                    V.tensor_tensor(G[:, bass.ds(i * 4 + q, 1), :], UB[:, q % 2, 0:1, :], UB[:, q % 2, 1:2, :], ALU.mult).then_inc(g_ready, 1)

                def up_tile(i, q, first=False):
                    taps(i, q)
                    if not (first and q == 0):
                        product(i, q - 1)

                if l == 0:
                    for q in range(8):
                        up_tile(0, q, True)
                        if q < 4:
                            mod_block(40 + 2 * q)
                            mod_block(41 + 2 * q)
                    mod_vector(5)
                    with dve.Fori(1, 3) as i:
                        for q in range(8):
                            up_tile(i * 2, q)
                            if q < 4:
                                mod_loop_block(i, 2 * q)
                                mod_loop_block(i, 2 * q + 1)
                        dve.wait_ge(mod_mm, i + 6)
                        V.tensor_tensor(mod[:, bass.ds(i + 5, 1), :], ps[:, 7, 0:8].unsqueeze(1),
                                        PR[:, 1, bass.ds(i * 8 + (COL["bmod"] - 8), 8)].unsqueeze(1), ALU.add).then_inc(mod_ready, 1)
                    product(0, FT - 1)
                    for u in range(8, 11):
                        mod_unit(u)
                else:
                    for q in range(4):
                        up_tile(0, q, True)
                    with dve.Fori(1, FT // 4) as i:
                        for q in range(4):
                            up_tile(i, q)
                    product(0, FT - 1)
                u = 5 if l == 0 else 11
                dve.wait_ge(mod_ready, u + 1)
                g1 = PAIRS * l + PAIRS - 4
                residuals(g1, mod[:, u, :])
            norm(4, col(0, "fg", 0, 8), None)

        @block.tensor
        def _(pe):
            MM = nc.tensor.matmul

            def mod_sum(u):
                pe.wait_ge(mod_used, 8 * (u + 1))
                if u:
                    pe.wait_ge(mod_ready, u)
                for j in range(KT):
                    i = MM(ps[:, 7, j:j + 1], macc[:, j * P:(j + 1) * P], sm[:, ONE1:ONE1 + 1], start=True, stop=True)
                i.then_inc(mod_mm, 1)

            def ones_sum(n):
                for m in range(KT):
                    pe.wait_ge(x_sq, 8 * n + m + 1)
                    i = MM(ps[:, 4, 0:S], ones[:, :], H[:, m, :], start=(m == 0), stop=(m == KT - 1))
                i.then_inc(x_ss, 1)

            def landed(g):
                pe.wait_ge(s_w[g % 4], 16 * (g // 4 + 1))

            def emptied(g, b):
                if EMPTIED[g][b]:
                    pe.wait_ge(bank_free[b], EMPTIED[g][b])

            def w_of(g, m, k, n=KT):
                return ring[:, g % 4, (m * n + k) * P:(m * n + k + 1) * P]

            def product(l, k, rhs, wait_h=None):
                g = PAIRS * l + k
                landed(g)
                emptied(g, g % 4)
                for m in range(2):
                    for i in range(KT):
                        if wait_h is not None and m == 0:
                            pe.wait_ge(h_ready, wait_h + i + 1)
                        last = MM(ps[:, g % 4, m * S:(m + 1) * S], w_of(g, m, i), rhs[:, i, :], start=(i == 0), stop=(i == KT - 1))
                last.then_inc(pair_done, 1)

            pe.wait_ge(s_par, 80)
            pe.wait_ge(bd_zero, 6)
            mod_sum(0)
            mod_sum(1)
            for l in range(L):
                ones_sum(2 * l)
                product(l, 0, H, wait_h=16 * l)
                mod_sum(2 if l == 0 else 11)
                for k in range(1, 4):
                    product(l, k, H)
                pe.wait_ge(s_sw, 80 * (l + 1))
                pe.wait_ge(lora_t, 3 * l + 3)
                pe.wait_ge(x_rt, 2 * l + 1)
                pe.wait_ge(mod_ready, 3 if l == 0 else 12)
                for i in range(2):
                    rows = slice(64 * i, 64 * i + 64)
                    for j in range(4):
                        last = MM(duo(4 + 2 * i + j // 2)[:, j % 2, :], SW[rows, WL + j * P:WL + (j + 1) * P], YA[rows, 0, :],
                                  start=True, stop=True)
                    last.then_inc(lora_mm, 1)
                product(l, 4, H)
                product(l, 5, H)
                pe.wait_ge(lora_act, 10 * l + 4)
                for j in range(4):
                    last = MM(duo(4 + j // 2)[:, j % 2, :], SW[:, WG + j * P:WG + (j + 1) * P], YA[:, 1, :], start=True, stop=True)
                last.then_inc(lora_mm, 1)
                product(l, 6, H)
                if l:
                    pe.wait_ge(s_v12, 32)
                    pe.wait_ge(lora_act, 10 * l + 8)
                    for i in range(KT):
                        last = MM(ps[0:32, 6, 0:S], V1[:, i, :], H[:, i, :], start=(i == 0), stop=(i == KT - 1))
                    last.then_inc(zv_up, 1)
                    product(l, LR, H)
                    pe.wait_ge(zv_ready, 1)
                    for j in range(4):
                        last = MM(duo(6 + j // 2)[:, j % 2, :], V2[0:32, j * P:(j + 1) * P], YB[0:32, 2, :], start=True, stop=True)
                    last.then_inc(zv_up, 1)
                    product(l, LR + 1, H)
                else:
                    product(l, LR, H)
                    product(l, LR + 1, H)
                pe.wait_ge(kk_sq, l + 1)
                pe.wait_ge(lora_act, 10 * l + 10)
                for b in range(2):
                    last = MM(ps[:, 4 + b, :], mat(BLOCKS), E[:, 2 * b:2 * b + 2, :], start=True, stop=True)
                last.then_inc(kk_mm, 1)
                product(l, LR + 2, H)
                product(l, LR + 3, H)
                pe.wait_ge(rk_ready, 4 * (l + 1))
                pe.wait_ge(lora_act, 10 * l + 8)
                if l:
                    pe.wait_ge(zv_up, 7)
                for b in range(2):
                    last = MM(ps[:, 6 + b, :], mat(BLOCKS), BON[:, 2 * b:2 * b + 2, :], start=True, stop=True)
                last.then_inc(bon_mm, 1)
                for k in range(AT, GA):
                    product(l, k, H)
                pe.wait_ge(kk_rt, 2 * (l + 1))
                pe.wait_ge(bon_ready, 2 * (l + 1))
                for b in range(4):
                    g = PAIRS * l + AT + b
                    pe.wait_ge(bank_free[g % 4], EMPTIED[g][g % 4] + 1)
                    MM(ps[:, 4 + b, :], mat(ROT), QK[:, 2 * b:2 * b + 2, :], start=True, stop=True).then_inc(rot_mm, 1)
                for t in range(2):
                    g = PAIRS * l + AT + 4 + t
                    pe.wait_ge(bank_free[g % 4], EMPTIED[g][g % 4] + 1)
                for t in range(2):
                    pe.wait_ge(rope_mul, 4 * l + t + 1)
                    for j in range(4):
                        last = nc.tensor.transpose(ps[:, 4 + t, j * P:(j + 1) * P], VR[:, j, t * P:(t + 1) * P], mat(IDENT))
                    last.then_inc(avt_mm, 1)
                for i in range(2):
                    for h in range(2):
                        pe.wait_ge(xc_ready, 4 * l + 2 * h + 2)
                        if i == 0:
                            pe.wait_ge(avt_ev, 2 * l + h + 1)
                        else:
                            pe.wait_ge(rope_mul, 4 * l + 4)
                        for j in (2 * h, 2 * h + 1):
                            last = MM(duo((4 if i == 0 else 6) + h)[:, j % 2, :], SW[:, WA + W * i + j * P:WA + W * i + (j + 1) * P],
                                      XC[:, j, :], start=True, stop=True)
                        last.then_inc(lr_mm, 1)
                filled = [0]

                def fill(point):
                    n = FILL[point] if point < len(FILL) else 192 - filled[0]
                    for _ in range(n):
                        k, r = divmod(filled[0], 16)
                        m, i = divmod(r, 8)
                        g = PAIRS * l + GA + k
                        if r == 0:
                            landed(g)
                            emptied(g, g % 4)
                        last = MM(ps[:, g % 4, m * S:(m + 1) * S], w_of(g, m, i), H[:, i, :], start=(i == 0), stop=(i == KT - 1))
                        if r == 15:
                            last.then_inc(pair_done, 1)
                        filled[0] += 1

                def scores(n):
                    t, c, h0, nh = SCORES[n]
                    rows = slice(64 * c, 64 * c + 64)
                    nk = P * (t + 1)
                    for i in range(nh):
                        h = h0 + i
                        last = MM(ps[:, SCORE_BANK[n], i * nk:(i + 1) * nk], QK[rows, h, t * P:(t + 1) * P], QK[rows, 4 + h, 0:nk],
                                  start=True, stop=True)
                    last.then_inc(sc_mm, 1)

                fill(0)
                pe.wait_ge(qk_ready, 4 * (l + 1))
                pe.wait_ge(lr_act, 8 * (l + 1))
                scores(0)
                scores(1)
                fill(1)
                scores(2)
                scores(3)
                pe.wait_ge(sc_read, 6 * l + 1)
                scores(4)
                pe.wait_ge(sc_read, 6 * l + 2)
                scores(5)
                fill(2)
                fill(3)
                fill(4)
                for n, (kt, qt) in enumerate(((0, 0), (0, 1), (1, 1))):
                    pe.wait_ge(sc_read, 6 * (l + 1))
                    for h in range(4):
                        pe.wait_ge(p_ready, 8 * l + 4 * qt + h + 1)
                        src = S0[:, 0, h, :] if qt == 0 else S1[:, 0, h, kt * P:(kt + 1) * P]
                        last = nc.tensor.transpose(ps[:, 4 + n, h * P:(h + 1) * P], src, mat(IDENT))
                    last.then_inc(pt_mm, 1)
                fill(5)
                for n, b in enumerate((7, 4)):
                    pe.wait_ge(pt_ev, 3 * (l + 1))
                    for h in (2 * n, 2 * n + 1):
                        MM(ps[:, b, (h % 2) * S:(h % 2 + 1) * S], AVT[:, 0, h * P:(h + 1) * P], PT[:, 0, h, :], start=True, stop=False)
                        last = MM(ps[:, b, (h % 2) * S + P:(h % 2 + 1) * S], AVT[:, 1, h * P:(h + 1) * P], PT[:, 1, h, P:S],
                                  start=False, stop=True)
                    last.then_inc(ao_mm, 1)
                for n in range(2):
                    pe.wait_ge(ao_sq, 2 * l + n + 1)
                    MM(ps[:, 5 + n, :], ones[:, :], E[:, 2 * n:2 * n + 2, :], start=True, stop=True).then_inc(as_mm, 1)
                fill(6)
                pe.wait_ge(feat, 4 * (l + 1))
                for n in range(8):
                    t = n % 2
                    src = (KK, AB, K_, V_)[n // 2]
                    pe.wait_ge(yb_ready, 2 * (l + 1))
                    if n >= 4:
                        pe.wait_ge(tk_ev, 8 * l + n - 3)
                    for j in range(4):
                        last = nc.tensor.transpose(ps[:, 4 + n % 4, j * P:(j + 1) * P], src[:, j, t * P:(t + 1) * P], mat(IDENT))
                    last.then_inc(tk_mm, 1)
                fill(7)
                for tt in range(2):
                    base = NSTEP * (2 * l + tt)
                    cols = slice(tt * P, (tt + 1) * P)
                    for n, (kind, par, v, b) in enumerate(STEPS):
                        rows = slice(64 * par, 64 * par + 64)
                        t_ = 2 * tt + par
                        if kind in ("ak", "n", "nt"):
                            if kind != "nt":
                                if tt == 0:
                                    pe.wait_ge(tk_ev, 8 * l + 8)
                                else:
                                    pe.wait_ge(t_ev, base)
                            else:
                                pe.wait_ge(t_ev, base + par + 1)
                            a, bb = {"ak": (K_, KK), "n": (KK, AB), "nt": (AB, KK)}[kind]
                            for j in range(4):
                                last = MM(quad(b)[:, j, :], a[rows, j, cols], bb[rows, j, cols], start=True, stop=True)
                        elif kind == "m":
                            if v == 0:
                                pe.wait_ge(t_init, 6 * (2 * l + tt) + 3 * par + 3)
                                pe.wait_ge(w1_ev, 2 * l + tt + 1)
                            else:
                                pe.wait_ge(t_ev, base + step_no("x", par, v - 1) + 1)
                            for j in range(4):
                                last = MM(quad(b)[:, j, :], Nm[:, par, j, :], TTm[:, t_, j, :], start=True, stop=True)
                        elif kind == "x":
                            pe.wait_ge(t_ev, base + step_no("m", par, v) + 1)
                            if v:
                                pe.wait_ge(t_ev, base + step_no("xt", par, v - 1) + 1)
                            for j in range(4):
                                last = MM(quad(b)[:, j, :], Tm[:, par, j, :], Mm[:, par, j, :], start=True, stop=True)
                        else:
                            for j in range(4):
                                last = MM(quad(b)[:, j, :], Mm[:, par, j, :], Tm[:, par, j, :], start=True, stop=True)
                        last.then_inc(t_mm, 1)
                        if n == 5:
                            pe.wait_ge(t_ev, base + 4)
                            for j in range(4):
                                for p2 in range(2):
                                    h = 2 * j + p2
                                    last = MM(ps[:, 6, h * 64:(h + 1) * 64], Mm[:, p2, j, :], VT_[:, tt, h * 64:(h + 1) * 64],
                                              start=True, stop=True)
                            last.then_inc(w1_mm, 1)
                        if kind == "x" and par == 1:
                            fill(8 + 5 * tt + v)
                pe.wait_ge(t_ev, NSTEP * 2 * (l + 1))
                for tt in range(2):
                    for j in range(4):
                        for p2 in range(2):
                            h = 2 * j + p2
                            last = MM(quad(4 + tt)[64 * p2:64 * p2 + 64, j, :], AT_[:, tt, h * 64:(h + 1) * 64], TTm[:, 2 * tt + p2, j, :],
                                      start=True, stop=True)
                    last.then_inc(zy_mm, 1)
                for tt in range(2):
                    for j in range(4):
                        for p2 in range(2):
                            h = 2 * j + p2
                            last = MM(ps[:, 6 + tt, h * 64:(h + 1) * 64], TTm[:, 2 * tt + p2, j, :], WY[:, tt, h * 64:(h + 1) * 64],
                                      start=True, stop=True)
                    last.then_inc(zy_mm, 1)
                for n in range(8):
                    tt, par = n // 4, (n // 2) % 2
                    rows, cols = slice(64 * par, 64 * par + 64), slice(tt * P, (tt + 1) * P)
                    if n < 4:
                        pe.wait_ge(zy_ev, 4 * l + n + 1)
                    else:
                        pe.wait_ge(rb_ev, 8 * l + n - 3)
                    a = K_ if n % 2 == 0 else AB
                    for j in range(4):
                        last = MM(quad(4 + n % 4)[:, j, :], a[rows, j, cols], R_[rows, j, cols], start=True, stop=True)
                    last.then_inc(rb_mm, 1)
                fill(99)

                def read_part(tt, m, tokm, first):
                    for j in range(4):
                        for p2 in range(2):
                            h = 2 * j + p2
                            last = MM(quad(6 + tt)[64 * p2:64 * p2 + 64, j, :], tokm[:, tt, h * 64:(h + 1) * 64], m[:, 2 * tt + p2, j, :],
                                      start=(first and j == 0), stop=False, skip_group_check=True)
                    return last

                pe.wait_ge(rb_ev, 8 * (l + 1))
                pe.wait_ge(zy_ev, 4 * (l + 1))
                read_part(0, RKm, VT_, True)
                read_part(1, RKm, VT_, True)
                for c in range(NCH):
                    tt, hf = c // 2, c % 2
                    rows = slice(64 * hf, 64 * hf + 64)
                    cols = slice(64 * c, 64 * c + 64)
                    if c < NCH - 1:
                        if c:
                            pe.wait_ge(st_ready, 3 * l + c)
                        for j in range(4):
                            MM(quad(5)[:, j, :], KT_[rows, tt, j * P:(j + 1) * P], VT_[rows, tt, j * P:(j + 1) * P],
                               start=(j == 0), stop=False, skip_group_check=True)
                    if c:
                        pe.wait_ge(st_ready, 3 * l + c)
                        for j in range(4):
                            last = MM(quad(4)[rows, j, :], KK[:, j, cols], ST[:, j, :], start=True, stop=True)
                        last.then_inc(u_mm, 1)
                        for j in range(4):
                            last = MM(quad(6 + tt)[:, j, rows], ST[:, j, :], R_[:, j, cols], start=False, stop=False, skip_group_check=True)
                        pe.wait_ge(u_ready, 3 * l + c)
                    if c < NCH - 1:
                        for j in range(4):
                            last = MM(quad(5)[:, j, :], BT_[rows, tt, j * P:(j + 1) * P], WY[rows, tt, j * P:(j + 1) * P],
                                      start=False, stop=(j == 3), skip_group_check=True)
                        last.then_inc(s_mm, 1)
                    if hf == 1:
                        read_part(tt, RBm, WY, False).then_inc(o_mm, 1)

                def merge(p, y):
                    g = PAIRS * l + MG + p
                    landed(g)
                    for i, b in enumerate(banks_of(g)):
                        emptied(g, b)
                        for m in (2 * i, 2 * i + 1):
                            for k in range(4):
                                last = MM(ps[:, b, (m % 2) * S:(m % 2 + 1) * S], w_of(g, m, k, 4), y[:, k, :], start=(k == 0), stop=(k == 3))
                    last.then_inc(pair_done, 1)

                pe.wait_ge(ya_ready, 4 * (l + 1))
                merge(0, YA)
                for b in range(2):
                    pe.wait_ge(o_ev, 2 * (l + 1))
                    MM(ps[:, 4 + b, :], mat(BLOCKS), AB[:, 2 * b:2 * b + 2, :], start=True, stop=True).then_inc(gn_mm, 1)
                merge(1, YA)
                pe.wait_ge(yb_ready, 2 * (l + 1))
                merge(2, YB)
                merge(3, YB)
                pe.wait_ge(gn_sq, l + 1)
                for b in range(2):
                    MM(ps[:, 6 + b, :], mat(BLOCKS), E[:, 2 * b:2 * b + 2, :], start=True, stop=True).then_inc(gn_mm, 1)
                if l == 0:
                    pe.wait_ge(gn_rt, 2 * (l + 1))
                    mod_sum(3)
                pe.wait_ge(yc_ready, l + 1)
                merge(4, AB)
                merge(5, AB)
                if l == 0:
                    mod_sum(4)
                pe.wait_ge(mg_ready, 8 * (l + 1))
                for j in range(4):
                    product(l, OU + j, H)
                ones_sum(2 * l + 1)
                g0 = PAIRS * l + UP

                def up(i, q, first=False):
                    g = g0 + q
                    b = g % 4
                    pe.wait_ge(s_w[b], i * 16 + 16 * (g // 4 + 1))
                    pe.wait_ge(bank_free[b], i + EMPTIED[g][b])
                    for m in range(2):
                        for k in range(KT):
                            if first and q == 0 and m == 0:
                                pe.wait_ge(h_ready, 8 * (2 * l + 1) + k + 1)
                            last = MM(ps[:, b, m * S:(m + 1) * S], w_of(g, m, k), H[:, k, :], start=(k == 0), stop=(k == KT - 1))
                    last.then_inc(pair_done, 1)

                for q in range(4):
                    up(0, q, True)
                if l == 0:
                    for q in range(4, 8):
                        up(0, q)
                    mod_sum(5)
                    with pe.Fori(1, 3) as i:
                        for q in range(8):
                            up(i * 2, q)
                        pe.wait_ge(mod_used, i * 8 + 48)
                        pe.wait_ge(mod_ready, i + 5)
                        for j in range(KT):
                            last = MM(ps[:, 7, j:j + 1], macc[:, j * P:(j + 1) * P], sm[:, ONE1:ONE1 + 1], start=True, stop=True)
                        last.then_inc(mod_mm, 1)
                else:
                    with pe.Fori(1, FT // 4) as i:
                        for q in range(4):
                            up(i, q)

                def down(i, q, first=False):
                    g = PAIRS * l + DN + q
                    b = g % 4
                    pe.wait_ge(s_w[b], i * 16 + 16 * (g // 4 + 1))
                    if first:
                        emptied(g, b)
                    for m in range(2):
                        for k in range(KT):
                            if first and q == 0 and m == 0:
                                pe.wait_ge(g_ready, FT * l + k + 1)
                            rhs = G[:, k, :] if first else G[:, bass.ds(i * 8 + k, 1), :]
                            last = MM(ps[:, b, m * S:(m + 1) * S], w_of(g, m, k), rhs, start=(first and m == 0 and k == 0), stop=False,
                                      skip_group_check=True)
                    last.then_inc(pair_done, 1)

                for q in range(4):
                    down(0, q, True)
                if l == 0:
                    mod_sum(8)
                pe.wait_ge(g_ready, FT * (l + 1))
                with pe.Fori(1, 3) as i:
                    for q in range(4):
                        down(i, q)
                    if l == 0:
                        pe.wait_ge(mod_used, i * 8 + 72)
                        pe.wait_ge(mod_ready, i + 8)
                        for j in range(KT):
                            last = MM(ps[:, 7, j:j + 1], macc[:, j * P:(j + 1) * P], sm[:, ONE1:ONE1 + 1], start=True, stop=True)
                        last.then_inc(mod_mm, 1)
            ones_sum(4)


def kernel(x, c, positions, w_mod, b_mod, norm1_g, norm2_g, final_g, w_in, w_merge_a, w_merge_b, w_merge_c, w_out,
           lru_conv_w, lru_conv_b, lru_wa, lru_ba, lru_wx, lru_bx, lru_lambda, diff_lq1, diff_lk1, diff_lq2, diff_lk2,
           diff_subln_g, rwkv_mu, rwkv_w0, rwkv_w2, rwkv_a0, rwkv_a2, rwkv_g2, rwkv_kk, rwkv_ka, rwkv_rk, rwkv_lnx_g,
           rwkv_lnx_b, rwkv_v0, rwkv_v1, rwkv_v2, rwkv_vmu, ffn_up, ffn_conv_w, ffn_conv_b, ffn_down):
    import concourse.bacc as bacc
    from concourse.bass_utils import run_bass_kernel_spmd

    f = np.ascontiguousarray

    def blocks(w):
        return w.reshape(w.shape[0] // P, P, w.shape[1] // P, P).transpose(2, 0, 1, 3)

    def pairs(b):
        return b.reshape(-1, 16, P, P).transpose(0, 2, 1, 3).reshape(-1, P, PAIR)

    def tiles(v):
        return v.reshape(-1, P).T

    wmain, wmod, small, prs = [], [], [], []
    zero = np.zeros
    for l in range(L):
        b = blocks(w_in[l])
        gate, lx, q, rw = b[0:24], b[24:32], b[32:44], b[44:58]
        rkv, lora = rw[0:12], rw[12:14]
        wmain.append(pairs(np.concatenate([lora, rkv[4:8], rkv[0:4], rkv[8:12], lx, q, gate])))
        for w in (w_merge_a, w_merge_b, w_merge_c):
            wmain.append(pairs(blocks(w[l])))
        wmain.append(pairs(blocks(w_out[l])))
        up = blocks(ffn_up[l])
        wmain.append(pairs(np.stack([up[0:FT], up[FT:]], axis=1)))
        dn = blocks(ffn_down[l])
        wmain.append(pairs(dn.reshape(KT, 3, KT, P, P).transpose(1, 0, 2, 3, 4)))
        vecs = w_mod[l].reshape(KT, P, 6, D)
        order = (1, 0, 2, 3, 4, 5)
        wmod.append(vecs[:, :, order].transpose(2, 0, 1, 3).reshape(6 * KT, P, D))
        bm = b_mod[l].reshape(6, D)[list(order)].reshape(-1)

        def bd(w):
            return w.reshape(4, 2, 64, 64).transpose(1, 2, 0, 3).reshape(P, 256)

        small.append(np.concatenate([np.concatenate([rwkv_w2[l], rwkv_a2[l]], axis=0), rwkv_g2[l], bd(lru_wa[l]), bd(lru_wx[l])], axis=1))
        mu = rwkv_mu[l]
        mu = np.concatenate([mu[3 * W:], mu[W:2 * W], mu[0:W], mu[2 * W:3 * W]])
        v0 = rwkv_v0[l - 1] if l else zero(W, np.float32)
        vmu = np.concatenate([rwkv_vmu[l - 1], zero(P - 32, np.float32)]) if l else zero(P, np.float32)
        parts = {"n1g": norm1_g[l], "n2g": norm2_g[l], "bmod": bm, "mu": mu, "w0": rwkv_w0[l], "a0": rwkv_a0[l], "v0": v0,
                 "ba": lru_ba[l].reshape(-1), "bx": lru_bx[l].reshape(-1), "kk": rwkv_kk[l], "ka": rwkv_ka[l],
                 "rk": rwkv_rk[l].reshape(-1), "lng": rwkv_lnx_g[l], "lnb": rwkv_lnx_b[l], "vmu": vmu, "sub": diff_subln_g[l],
                 "cw": lru_conv_w[l].reshape(-1), "cb": lru_conv_b[l], "lam": lru_lambda[l], "fw": ffn_conv_w[l].reshape(-1),
                 "fb": ffn_conv_b[l], "fg": final_g, "cc": c[0]}
        prs.append(np.concatenate([tiles(np.asarray(parts[n])) for n, _ in _NAMES], axis=1))
    v1v2 = np.concatenate([np.asarray(rwkv_v1[0]).reshape(KT, P, 32).transpose(1, 0, 2).reshape(P, 256),
                           np.concatenate([rwkv_v2[0], zero((P - 32, W), np.float32)])], axis=1)
    lqk = np.stack([diff_lq1, diff_lk1, diff_lq2, diff_lk2], axis=1).reshape(-1)

    i, j = np.arange(P)[:, None], np.arange(P)[None, :]
    same = i // CH == j // CH

    def level(s):
        return (i // (2 * s) == j // (2 * s)) & (i // s % 2 == 0) & (j // s % 2 == 1)

    rot = zero((P, P), np.float32)
    for p in range(P):
        if p % 64 < 8:
            rot[p + 8, p] = -1
        elif p % 64 < 16:
            rot[p - 8, p] = 1
    mats = [i == j, i // 64 == j // 64, same & (j < i), same & (j > i), same & (j >= i), level(1).T, level(1), level(2), level(4),
            level(8), level(16), level(32), rot]
    neg = np.where(np.arange(2 * P)[None, :] > P + i, np.float32(-1e30), np.float32(0))
    reset = np.broadcast_to((np.arange(S) % CH != 0)[None, :], (P, S))
    inv = (np.float32(500000.0) ** (-np.arange(0, 16, 2, dtype=np.float32) / np.float32(16))).astype(np.float32)
    freq = np.where(i % 64 < 16, inv[i % 8], np.float32(0))
    consts = np.concatenate([m.astype(np.float32) for m in mats] + [neg, reset.astype(np.float32), freq], axis=1).astype(np.float32)

    arrays = {
        "wmain": f(np.concatenate(wmain)), "wmod": f(np.concatenate(wmod)), "small": f(np.stack(small)), "v1v2": f(v1v2),
        "params": f(np.stack(prs, axis=1)), "consts": f(consts), "lqk": f(lqk),
        "x_t": f(np.asarray(x)[0].T.reshape(KT, P, S).transpose(1, 0, 2)), "positions": f(np.asarray(positions)[0]),
    }
    nc = bacc.Bacc("TRN2", target_bir_lowering=False, num_devices=1)
    args = [nc.dram_tensor(f"{n}_dram", a.shape, mybir.dt.from_np(a.dtype), kind="ExternalInput").ap() for n, a in arrays.items()]
    args.append(nc.dram_tensor("y_dram", (P, KT, S), F32, kind="ExternalOutput").ap())
    trunk_kernel(nc, *args)
    r = run_bass_kernel_spmd(nc, [{f"{n}_dram": a for n, a in arrays.items()}], core_ids=[0])
    y = r.results[0]["y_dram"]
    return y.transpose(1, 0, 2).reshape(D, S).T.reshape(1, S, D)
```

```python
import math
from contextlib import ExitStack

import numpy as np

import concourse.bass as bass
from concourse import mybir

ALU = mybir.AluOpType
ACT = mybir.ActivationFunctionType
F32 = mybir.dt.float32
F32R = mybir.dt.float32r
I32 = mybir.dt.int32
AX_X = mybir.AxisListType.X

P = 128
D = 1024
S = 256
L = 2
KT = D // P
W = 512
WT = W // P
FT = 3 * D // P
CH = 64
NCH = S // CH

RW, LR, AT, GA, MG, OU, UP, DN, PAIRS = 0, 7, 11, 17, 29, 35, 39, 63, 75
MLP = PAIRS - UP
FIRST = 16
SLOTS = 4
PAIR = 2048

_NAMES = [("n1g", 8), ("n2g", 8), ("bmod", 48), ("mu", 14), ("w0", 4), ("a0", 4), ("v0", 4), ("ba", 4), ("bx", 4),
          ("kk", 4), ("ka", 4), ("rk", 4), ("lng", 4), ("lnb", 4), ("vmu", 1), ("sub", 1), ("cw", 16), ("cb", 4),
          ("lam", 4), ("fw", 144), ("fb", 48), ("fg", 8), ("cc", 8)]
COL, NP = {}, 0
for _n, _w in _NAMES:
    COL[_n] = NP
    NP += _w

(IDENT, BLOCKS, M_LOW, M_UP, M_UPI, M_L1, M_U1, M_U2, M_U4, M_U8, M_U16, M_U32, ROT) = range(13)
NMAT = 13
NEG0 = NMAT * P
RESET = NEG0 + 256
FREQ = RESET + 256
NC_ = FREQ + 1

WL, WG, WA, WX = 0, 512, 1024, 1536

SQ2PI = 2.0 * math.pi
MAGIC = 1.5 * 2.0 ** 23
C1 = 6.28125
C2 = float(np.float32(SQ2PI - C1))
C3 = SQ2PI - C1 - C2
PI_IN = 3.1415925
EM05 = math.exp(-0.5)


def lambda_init(l):
    return 0.8 - 0.6 * math.exp(-0.3 * l)


def banks_of(g):
    l, k = divmod(g, PAIRS)
    if MG <= k < OU:
        return [(2 * (k - MG)) % 4, (2 * (k - MG) + 1) % 4]
    return [g % 4]


def _emptied():
    count, out = [0] * 4, []
    for g in range(L * PAIRS):
        out.append(list(count))
        if not DN <= g % PAIRS < PAIRS - 4:
            for b in banks_of(g):
                count[b] += 1
    return out


EMPTIED = _emptied()

FILL = [16] * 4 + [8] * 14
FILLED = np.cumsum(FILL) // 16

SCORES = [(0, 0, 0, 4), (0, 1, 0, 4), (1, 0, 0, 2), (1, 1, 0, 2), (1, 0, 2, 2), (1, 1, 2, 2)]
SCORE_BANK = [6, 7, 4, 5, 6, 7]
LEVELS = [M_U2, M_U4, M_U8, M_U16, M_U32]


def solve_steps():
    steps = [("ak", 0, 0, 4), ("ak", 1, 0, 5), ("n", 0, 0, 6), ("n", 1, 0, 7), ("nt", 0, 0, 4), ("nt", 1, 0, 5)]
    other = 6
    for v in range(len(LEVELS)):
        for kind in ("m", "x", "xt"):
            if kind == "xt" and v == len(LEVELS) - 1:
                continue
            for par in (0, 1):
                steps.append((kind, par, v, other + par))
            other = 10 - other
    return steps


STEPS = solve_steps()
NSTEP = len(STEPS)


def step_no(kind, par, v):
    return next(i for i, s in enumerate(STEPS) if s[:3] == (kind, par, v))


def trunk_kernel(nc, wmain, wmod, small, v1v2, params, consts, lqk, x_t, positions, y_t):
    ctx = ExitStack()
    with ctx:
        def sb(name, shape, dt=F32):
            return ctx.enter_context(nc.sbuf_tensor(name, shape, dt))

        def sem(name):
            return ctx.enter_context(nc.semaphore(name))

        X = sb("X", [P, KT, S])
        H = sb("H", [P, KT, S])
        ring = sb("ring", [P, SLOTS, PAIR])
        mring = sb("mring", [P, 2, D])
        macc = sb("macc", [P, D])
        C = sb("C", [P, NC_])
        PR = sb("PR", [P, L, NP])
        PH = sb("PH", [P, L, 20])
        SW = sb("SW", [P, 2048])
        COS = sb("COS", [P, S])
        SIN = sb("SIN", [P, S])
        at_g = nc.sbuf_base
        G = sb("G", [P, FT, S])
        at_r = nc.sbuf_base
        R = sb("R", [P, 24, S])
        at_k = nc.sbuf_base + WT * S * 4
        ZS = sb("ZS", [P, 12, S])
        AB = sb("AB", [P, WT, S])
        KK = sb("KK", [P, WT, S])
        GG = sb("GG", [P, WT, S])
        BON = sb("BON", [P, WT, S])
        E = sb("E", [P, WT, S])
        WY = sb("WY", [P, 2, W])
        at_y = nc.sbuf_base
        YA = sb("YA", [P, WT, S])
        YB = sb("YB", [P, WT, S])
        at_tk = nc.sbuf_base
        TK = sb("TK", [P, 16, S])
        WH = nc.alloc_sbuf_tensor_at("WH", [P, 2, PAIR], F32R, offset=at_k)
        WLO = nc.alloc_sbuf_tensor_at("WLO", [P, 2, PAIR], F32R, offset=at_k + 16 * S * 4)
        HH = nc.alloc_sbuf_tensor_at("HH", [P, KT, S], F32R, offset=at_y)
        HL = nc.alloc_sbuf_tensor_at("HL", [P, KT, S], F32R, offset=at_tk + 8 * S * 4)
        GH = nc.alloc_sbuf_tensor_at("GH", [P, FT, S], F32R, offset=at_g)
        GL = nc.alloc_sbuf_tensor_at("GL", [P, FT, S], F32R, offset=at_r)
        RT = sb("RT", [P, S])
        mod = sb("mod", [P, 12, KT])
        Acol = sb("Acol", [P, KT])
        ones = sb("ones", [P, P])
        sm = sb("sm", [P, 80])
        CSIL, NLAM, N8, SUBG, ONE1 = 0, 8, 10, 18, 20
        EPS6, EPS5, EPSG = 21, 22, 23
        MIDS, GF, MX, LSUM = 24, 40, 52, 60
        FH = 68

        ps = ctx.enter_context(nc.psum_tensor("ps", [P, 8, 512], F32))

        V_, K_, R_ = ZS[:, 0:4, :], ZS[:, 4:8, :], ZS[:, 8:12, :]
        LD, CUM = G[:, 14:18, :], G[:, 18:22, :]
        V1 = G[:, 22, :].rearrange("p (k m) -> p k m", k=KT)
        V2 = YB[:, 0:2, :].rearrange("p a b -> p (a b)")
        ZX, XC, LRA, LRI = TK[:, 0:4, :], TK[:, 4:8, :], TK[:, 8:12, :], TK[:, 12:16, :]
        QK, VR = R[:, 0:8, :], R[:, 8:12, :]
        VF = R[:, 0:4, :]
        AVT = R[:, 12:16, :].rearrange("p a b -> p (a b)").rearrange("p (t w) -> p t w", t=2)
        S0 = R[:, 16:20, :].rearrange("p a b -> p (a b)").rearrange("p (c h k) -> p c h k", c=2, h=4)
        S1 = TK[:, 8:16, :].rearrange("p (c h) k -> p c h k", c=2)
        PT = R[:, 0:8, :].rearrange("p (t h) q -> p t h q", t=2)

        def tok(i):
            return TK[:, 4 * i:4 * i + 4, :].rearrange("p a b -> p (a b)").rearrange("p (t w) -> p t w", t=2)

        AT_, BT_, KT_, VT_ = tok(0), tok(1), tok(2), tok(3)

        def mats(a, b):
            return R[:, a:b, :].rearrange("p a b -> p (a b)").rearrange("p (g j s) -> p g j s", j=4, s=P)

        TTm, Nm, Tm, Mm = mats(0, 8), mats(8, 12), mats(12, 16), mats(16, 20)
        RBm, RKm = mats(8, 16), mats(16, 24)
        ge = E[:, :, :].rearrange("p a b -> p (a b)").rearrange("p (c j s) -> p c j s", c=2, j=4)
        ga = TK[:, 0:4, :].rearrange("p a b -> p (a b)").rearrange("p (c j s) -> p c j s", c=2, j=4)
        GM = [ge[:, 0], ge[:, 1], ga[:, 0]]
        ST = ga[:, 1]
        UB = TK[:, 0:4, :].rearrange("p (u t) s -> p u t s", u=2)
        TP = TK[:, 4:6, :]

        def first_blocks(g):
            buf, i = ((G, g), (R, g - 3), (TK, g - 6))[(g >= 3) + (g >= 6)]
            return buf[:, 8 * i:8 * i + 8, :].rearrange("p (n a) b -> p n (a b)", n=2)

        def mat(i):
            return C[:, i * P:(i + 1) * P]

        def col(l, name, i=0, n=1):
            return PR[:, l, COL[name] + i:COL[name] + i + n]

        def flat(ap):
            return ap.rearrange("p a b -> p (a b)")

        def over(ap, n):
            return ap.unsqueeze(1).broadcast_to([ap.shape[0], n, ap.shape[1]])

        def along(ap, n):
            return ap.unsqueeze(2).broadcast_to([ap.shape[0], ap.shape[1], n])

        def quad(b):
            return ps[:, b, :].rearrange("p (j s) -> p j s", j=4)

        def duo(b):
            return ps[:, b, :].rearrange("p (t s) -> p t s", t=2)

        s_w = [sem(f"pair_landed{i}") for i in range(SLOTS)]
        s_m = [sem(f"mod_block_landed{i}") for i in range(2)]
        s_first = [sem(f"first_mod_blocks_landed{i}") for i in range(8)]
        s_pr, s_x = sem("parameters_landed"), sem("x_landed")
        s_par, s_sw, s_v12 = sem("constants_landed"), sem("small_weights_landed"), sem("value_lora_landed")
        s_out = sem("output_written")
        pair_done = sem("pair_done")
        bank_free = [sem(f"bank_free{i}") for i in range(4)]
        pre_act, pre_dve = sem("preamble_act"), sem("preamble_dve")
        bd_zero = sem("block_diagonals_zeroed")
        mod_used, mod_mm, mod_ready = sem("mod_block_used"), sem("mod_summed"), sem("mod_ready")
        x_sq, x_ss, x_rt = sem("x_squared"), sem("x_summed"), sem("x_rooted")
        h_pre, h_ready = sem("h_scaled"), sem("h_ready")
        step = sem("dve_step")
        astep = sem("act_step")
        zr_up = sem("rwkv_raw_ready")
        lora_z, lora_t, lora_mm, lora_act = sem("lora_shifted"), sem("lora_activated"), sem("lora_products"), sem("lora_read")
        zv_up, zv_ready, vf_moved, v_ready = sem("value_lora_up"), sem("value_lora_shifted"), sem("v_first_moved"), sem("v_ready")
        kk_raw, kk_sq, kk_mm, kk_rt = sem("kk_raw"), sem("kk_squared"), sem("kk_summed"), sem("kk_rooted")
        kk_used = sem("kk_root_used")
        rk_ready, bon_mm, bon_ready = sem("bonus_terms"), sem("bonus_summed"), sem("bonus_ready")
        cc_ready, cm_ready, exps = sem("log_decay_ready"), sem("log_decay_before_ready"), sem("decay_exps")
        feat = sem("rwkv_operands_ready")
        lr_up, xc_ready, lr_mm, lr_act = sem("lru_inputs_ready"), sem("lru_conv_ready"), sem("lru_gates_summed"), sem("lru_gates_ready")
        la_ready, la_act, lq_ready, lq_rt = sem("lru_log_a"), sem("lru_exps"), sem("lru_var"), sem("lru_root")
        ya_ready = sem("ya_ready")
        at_up, rot_mm, rope_mul, qk_ready = sem("qkv_ready"), sem("rotated"), sem("rotated_read"), sem("qk_ready")
        avt_mm, avt_ev = sem("v_turned"), sem("v_by_position")
        sc_mm, sc_read, mx_ready, p_exp, p_ready = (sem("scores_summed"), sem("scores_read"), sem("maxima_ready"),
                                                    sem("weights_exp"), sem("weights_ready"))
        pt_mm, pt_ev, ao_mm, ao_sq, as_mm, as_rt, yb_ready = (
            sem("weights_turned"), sem("weights_turned_read"), sem("heads_summed"), sem("heads_squared"),
            sem("head_squares_summed"), sem("head_roots"), sem("yb_ready"))
        tk_mm, tk_ev = sem("operands_turned"), sem("operands_by_position")
        t_mm, t_ev, t_init, w1_mm, w1_ev = (sem("solve_products"), sem("solve_read"), sem("solve_begun"),
                                            sem("akv_summed"), sem("akv_ready"))
        zy_mm, zy_ev, rb_mm, rb_ev = sem("zy_summed"), sem("zy_ready"), sem("read_products"), sem("read_ready")
        gm_ready = sem("state_factors_ready")
        u_mm, u_ready, s_mm, st_ready, o_mm, o_ev = (sem("u_summed"), sem("u_ready"), sem("state_summed"),
                                                     sem("state_ready"), sem("out_summed"), sem("out_ready"))
        gn_mm, gn_c, gn_sq, gn_rt, yc_ready = (sem("norm_summed"), sem("centred"), sem("centred_squared"),
                                               sem("norm_rooted"), sem("yc_ready"))
        gn_inv = sem("norm_inverse_root")
        mg_ready = sem("merged_ready")
        cv_step = sem("first_taps_done")
        u_begun, cv_done, gl_done, g_ready = sem("conv_begun"), sem("conv_done"), sem("gelu_done"), sem("hidden_split")
        hi_ready, lo_ready, half_done = sem("weights_high_ready"), sem("weights_low_ready"), sem("half_pair_done")
        hh_ready, hl_ready, g_prod, gh_ready = (sem("input_high_ready"), sem("input_low_ready"), sem("hidden_multiplied"),
                                                sem("hidden_high_ready"))

        n_step, n_astep = [0], [0]

        def tick(n):
            n[0] += 1
            return 1

        block = ctx.enter_context(nc.Block())

        @block.sync
        def _(sp):
            sp.dma_start(PR[:, :, :], params).then_inc(s_pr, 16)
            for g in range(8):
                sp.dma_start(first_blocks(g), wmod[2 * g:2 * g + 2].rearrange("n p d -> p n d")).then_inc(s_first[g], 16)
                if g == 1:
                    sp.dma_start(X[:, :, :], x_t).then_inc(s_x, 16)
            sp.dma_start(C[:, :], consts).then_inc(s_par, 16)
            sp.dma_start(E[:, 0:2, :].rearrange("p a b -> p (a b)"), lqk.partition_broadcast(P)).then_inc(s_par, 16)
            sp.dma_start(YA[:, 0, :].bitcast(I32), positions.partition_broadcast(P)).then_inc(s_par, 16)

            def pair(g):
                if g >= PAIRS and g < PAIRS + SLOTS:
                    sp.wait_ge(lo_ready, 2 * (g - UP - SLOTS + 1))
                elif g >= SLOTS:
                    sp.wait_ge(pair_done, g - SLOTS + 1)
                sp.dma_start(ring[:, g % SLOTS, :], wmain[g]).then_inc(s_w[g % SLOTS], 16)

            for l in range(L):
                for g in range(PAIRS * l, PAIRS * l + 4):
                    pair(g)
                if l:
                    sp.wait_ge(lr_mm, 4 * l)
                else:
                    sp.wait_ge(bd_zero, 1)
                sp.dma_start(SW[:, WL:WL + 1024], small[l, :, 0:1024]).then_inc(s_sw, 16)
                for i in range(2):
                    for par in range(2):
                        at = WA + W * i
                        sp.dma_start(SW[64 * par:64 * par + 64, at:at + W].rearrange("p (j m) -> p j m", j=4)
                                     [:, :, 64 * par:64 * par + 64],
                                     small[l, 64 * par:64 * par + 64, 1024 + 256 * i:1280 + 256 * i]
                                     .rearrange("p (j m) -> p j m", j=4)).then_inc(s_sw, 16)
                if l:
                    sp.wait_ge(pair_done, PAIRS * l)
                    sp.dma_start(V1, v1v2[:, 0:256].rearrange("p (k m) -> p k m", k=KT)).then_inc(s_v12, 16)
                    sp.dma_start(V2[0:32, :], v1v2[0:32, 256:768]).then_inc(s_v12, 16)
                for k in range(4, UP + 4):
                    pair(PAIRS * l + k)
                with sp.Fori(1, (PAIRS - UP) // 4) as i:
                    for q in range(4):
                        g0 = PAIRS * l + UP + q
                        sp.wait_ge(lo_ready, i * 8 + (2 * (MLP * l + q) - 6))
                        sp.dma_start(ring[:, g0 % SLOTS, :], wmain[i * 4 + g0]).then_inc(s_w[g0 % SLOTS], 16)
            sp.wait_ge(h_pre, 8 * 5)
            sp.dma_start(y_t, H[:, :, :]).then_inc(s_out, 16)
            sp.wait_ge(s_out, 16)

        @block.gpsimd
        def _(pool):
            pool.memset(SW[:, WA:WA + 2 * W], 0.0).then_inc(bd_zero, 1)
            pool.memset(sm[:, ONE1:ONE1 + 1], 1.0).then_inc(bd_zero, 1)
            pool.memset(sm[:, EPS6:EPS6 + 1], 1e-6).then_inc(bd_zero, 1)
            pool.memset(sm[:, EPS5:EPS5 + 1], 1e-5).then_inc(bd_zero, 1)
            pool.memset(sm[:, EPSG:EPSG + 1], 64e-5).then_inc(bd_zero, 1)
            pool.memset(ones[:, :], 1.0).then_inc(bd_zero, 1)

            def mod_blocks(a, b):
                for n in range(a, b):
                    if n >= FIRST + 2:
                        pool.wait_ge(mod_used, n - 1)
                    pool.dma_start(mring[:, n % 2, :], wmod[n]).then_inc(s_m[n % 2], 16)

            for l in range(L):
                if l == 0:
                    mod_blocks(FIRST, 34)
                for tt in range(2):
                    if l == 0 and tt:
                        mod_blocks(34, 38)
                    base = NSTEP * (2 * l + tt)
                    for par in range(2):
                        pool.wait_ge(t_ev, base + step_no("n", par, 0) + 1)
                        if tt:
                            pool.wait_ge(t_mm, base + step_no("n", par, 0) + 1)
                        pool.tensor_tensor(Tm[:, par], Nm[:, par], over(mat(M_L1), 4), ALU.mult).then_inc(t_init, 1)
                        pool.wait_ge(t_init, 6 * (2 * l + tt) + 3 * par + 1)
                        pool.tensor_tensor(Tm[:, par], Tm[:, par], over(mat(IDENT), 4), ALU.add).then_inc(t_init, 1)
                        pool.wait_ge(t_ev, base + step_no("nt", par, 0) + 1)
                        pool.tensor_tensor(TTm[:, 2 * tt + par], TTm[:, 2 * tt + par], over(mat(IDENT), 4),
                                           ALU.add).then_inc(t_init, 1)
                if l == 0:
                    mod_blocks(38, 40)
                pool.wait_ge(zy_ev, 4 * (l + 1))
                pool.wait_ge(yb_ready, 2 * (l + 1))
                for c in range(3):
                    gf = sm[:, GF:GF + 12].rearrange("p (j c) -> p j c", c=3)[:, :, c]
                    pool.tensor_tensor(GM[c], along(gf, P), over(mat(BLOCKS), 4), ALU.mult).then_inc(gm_ready, 1)
                if l == 0:
                    mod_blocks(40, 42)
                for n in range(8):
                    m = 2 * (n % 4)
                    br = 1 + n // 4
                    g = PAIRS * l + MG + 2 + n // 2
                    b = banks_of(g)[n % 2]
                    pool.wait_ge(bank_free[b], EMPTIED[g][b] + 1)
                    if n >= 4:
                        pool.wait_ge(mg_ready, 8 * l + n - 3)
                    pool.tensor_tensor(H[:, m:m + 2, :], H[:, m:m + 2, :], G[:, 8 * br + m:8 * br + m + 2, :],
                                       ALU.add).then_inc(mg_ready, 1)
                if l == 0:
                    mod_blocks(42, 88)
                else:
                    mod_blocks(88, 96)

        @block.scalar
        def _(act):
            A = nc.scalar.activation
            act.wait_ge(s_pr, 16)
            act.wait_ge(bd_zero, 6)
            A(sm[:, CSIL:CSIL + 8], PR[:, 0, COL["cc"]:COL["cc"] + 8], ACT.Tanh, scale=0.5).then_inc(pre_act, 1)
            def squares(n):
                for m in range(KT):
                    if n:
                        g = PAIRS * ((n - 1) // 2) + (OU if n % 2 else PAIRS - 4) + m // 2
                        act.wait_ge(bank_free[g % 4], EMPTIED[g][g % 4] + 1)
                    if m == 0 and n:
                        act.wait_ge(pair_done, PAIRS * ((n - 1) // 2) + (OU + 4 if n % 2 else PAIRS))
                    elif m == 0:
                        act.wait_ge(s_x, 16)
                    A(H[:, m, :], X[:, m, :], ACT.Square).then_inc(x_sq, 1)
                act.wait_ge(x_ss, n + 1)
                A(RT[:, :], ps[:, 4, 0:S], ACT.Ln, bias=sm[:, EPS6:EPS6 + 1], scale=1.0 / D).then_inc(astep, tick(n_astep))
                act.wait_ge(astep, n_astep[0])
                A(RT[:, :], RT[:, :], ACT.Exp, scale=-0.5).then_inc(x_rt, 1)

            def shifts(n, u):
                for m in range(KT):
                    act.wait_ge(h_pre, 8 * n + m + 1)
                    if m == 0:
                        act.wait_ge(mod_ready, u + 1)
                    if n % 2:
                        if m == 0:
                            act.wait_ge(pair_done, PAIRS * (n // 2) + OU)
                        A(HH[:, m, :], H[:, m, :], ACT.Identity, bias=mod[:, u, m:m + 1]).then_inc(hh_ready, 1)
                    A(H[:, m, :], H[:, m, :], ACT.Identity, bias=mod[:, u, m:m + 1]).then_inc(h_ready, 1)

            def evac(l, k, out, func=ACT.Identity, scale=1.0):
                g = PAIRS * l + k
                act.wait_ge(pair_done, g + 1)
                return A(out, duo(g % 4), func, scale=scale).then_inc(bank_free[g % 4], 1)

            for l in range(L):
                squares(2 * l)
                shifts(2 * l, 1 if l == 0 else 7)
                if l == 0:
                    act.wait_ge(pre_dve, 3)
                    A(sm[:, 24:28], sm[:, 24:28], ACT.Exp).then_inc(pre_act, 1)
                    A(sm[:, 40:48], sm[:, 40:48], ACT.Exp, scale=-1.0).then_inc(pre_act, 1)
                    act.wait_ge(pre_act, 3)
                    A(sm[:, 48:56], sm[:, 40:48], ACT.Ln, bias=sm[:, ONE1:ONE1 + 1]).then_inc(pre_act, 1)
                    act.wait_ge(pre_dve, 5)
                    A(SIN[:, :], RT[:, :], ACT.Sin).then_inc(pre_act, 1)
                    A(COS[:, :], YA[:, 1, :], ACT.Sin).then_inc(pre_act, 1)
                for k in range(0, 3):
                    evac(l, k, G[:, 2 * k:2 * k + 2, :])
                act.wait_ge(lora_z, 2 * l + 2)
                A(YA[0:64, 0, :], YA[0:64, 0, :], ACT.Tanh).then_inc(lora_t, 1)
                A(YA[:, 1, :], YA[:, 1, :], ACT.Tanh, scale=0.5).then_inc(lora_t, 1)
                act.wait_ge(lora_t, 3 * l + 2)
                A(YA[:, 1, :], YA[:, 1, :], ACT.Copy, scale=0.5, bias=0.5).then_inc(lora_t, 1)
                evac(l, 3, G[:, 6:8, :])
                base = 10 * l
                for i, (dst, h) in enumerate(((LD, 0), (AB, 4))):
                    act.wait_ge(lora_mm, 3 * l + i + 1)
                    for j in range(4):
                        A(dst[:, j, :], duo(4 + 2 * i + j // 2)[:, j % 2, :], ACT.Tanh, scale=0.5,
                          bias=PH[:, l, h + j:h + j + 1]).then_inc(lora_act, 1)
                evac(l, 4, G[:, 8:10, :])
                evac(l, 5, G[:, 10:12, :])
                act.wait_ge(lora_mm, 3 * l + 3)
                for b in range(2):
                    A(GG[:, 2 * b:2 * b + 2, :], duo(4 + b), ACT.Copy).then_inc(lora_act, 1)
                evac(l, 6, G[:, 12:14, :])
                if l:
                    act.wait_ge(zv_up, 1)
                    A(RT[0:32, :], ps[0:32, 6, 0:S], ACT.Copy).then_inc(zv_up, 1)
                    act.wait_ge(zv_up, 3)
                    for j in range(4):
                        A(E[:, j, :], duo(6 + j // 2)[:, j % 2, :], ACT.Tanh, scale=0.5,
                          bias=PH[:, l, 8 + j:9 + j]).then_inc(zv_up, 1)
                for k in (LR, LR + 1):
                    evac(l, k, ZX[:, 2 * (k - LR):2 * (k - LR) + 2, :])
                act.wait_ge(kk_raw, 4 * l + 4)
                if l:
                    act.wait_ge(v_ready, 2)
                A(E[:, :, :], KK[:, :, :], ACT.Square).then_inc(kk_sq, 1)
                act.wait_ge(kk_mm, l + 1)
                for b in range(2):
                    A(E[:, 2 * b:2 * b + 2, :], duo(4 + b), ACT.Sqrt).then_inc(kk_rt, 1)
                for k in (LR + 2, LR + 3):
                    if k == LR + 2:
                        act.wait_ge(lora_mm, 3 * l + 3)
                    evac(l, k, YA[:, 2 * (k - LR) - 4:2 * (k - LR) - 2, :], ACT.Gelu_apprx_tanh)
                act.wait_ge(cc_ready, l + 1)
                act.wait_ge(kk_used, l + 1)
                A(sm[:, GF:GF + 12], sm[:, GF:GF + 12], ACT.Exp).then_inc(exps, 1)
                A(E[:, :, :], CUM, ACT.Exp).then_inc(exps, 1)
                A(LRI, CUM, ACT.Exp, scale=-1.0).then_inc(exps, 1)
                act.wait_ge(cm_ready, l + 1)
                A(LRA, LRA, ACT.Exp).then_inc(exps, 1)
                for k in range(AT, AT + 6):
                    if l and k == AT:
                        act.wait_ge(v_ready, 2)
                    g = PAIRS * l + k
                    act.wait_ge(pair_done, g + 1)
                    A(R[:, 2 * (k - AT):2 * (k - AT) + 2, :], duo(g % 4), ACT.Identity).then_inc(bank_free[g % 4], 1)
                for t in range(2):
                    act.wait_ge(avt_mm, 2 * l + t + 1)
                    A(AVT[:, t, :], ps[:, 4 + t, :], ACT.Copy).then_inc(avt_ev, 1)
                act.wait_ge(feat, 4 * (l + 1))
                for i in range(2):
                    for j in range(4):
                        act.wait_ge(lr_mm, 4 * l + 2 * i + j // 2 + 1)
                        A((LRA if i == 0 else LRI)[:, j, :], duo((4 if i == 0 else 6) + j // 2)[:, j % 2, :], ACT.Tanh, scale=0.5,
                          bias=PH[:, l, 12 + 4 * i + j:13 + 4 * i + j]).then_inc(lr_act, 1)
                gates_out = [0]

                def gates(point):
                    done = int(FILLED[point]) if point < len(FILL) else 12
                    while gates_out[0] < done:
                        k = GA + gates_out[0]
                        g = PAIRS * l + k
                        act.wait_ge(pair_done, g + 1)
                        if k == GA:
                            act.wait_ge(feat, 4 * (l + 1))
                        A(G[:, 2 * (k - GA):2 * (k - GA) + 2, :], duo(g % 4), ACT.Tanh, scale=0.5).then_inc(bank_free[g % 4], 1)
                        gates_out[0] += 1

                gates(0)
                act.wait_ge(la_ready, 4 * (l + 1))
                A(E[:, :, :], LRA, ACT.Exp).then_inc(la_act, 1)
                A(ZX, LRA, ACT.Tanh).then_inc(la_act, 1)
                gates(1)
                act.wait_ge(lq_ready, l + 1)
                A(LRA, LRA, ACT.Sqrt, scale=-1.0).then_inc(lq_rt, 1)
                for tt in range(2):
                    gates(2 + tt)
                    act.wait_ge(mx_ready, 2 * l + tt + 1)
                    sc = S0 if tt == 0 else S1
                    for c in range(2):
                        for h in range(4):
                            A(sc[:, c, h, :], sc[:, c, h, :], ACT.Exp, scale=0.125, bias=sm[:, MX + 4 * c + h:MX + 4 * c + h + 1],
                              accum_out=sm[:, LSUM + 4 * c + h:LSUM + 4 * c + h + 1]).then_inc(p_exp, 1)
                gates(4)
                for n, (kt, qt) in enumerate(((0, 0), (0, 1), (1, 1))):
                    act.wait_ge(pt_mm, 3 * l + n + 1)
                    A(PT[:, kt, :, qt * P:(qt + 1) * P], quad(4 + n), ACT.Copy).then_inc(pt_ev, 1)
                gates(5)
                for n, b in enumerate((7, 4)):
                    act.wait_ge(ao_mm, 2 * l + n + 1)
                    A(E[:, 2 * n:2 * n + 2, :], duo(b), ACT.Square).then_inc(ao_sq, 1)
                for n in range(2):
                    act.wait_ge(as_mm, 2 * l + n + 1)
                    A(E[:, 2 * n:2 * n + 2, :], duo(5 + n), ACT.Ln, scale=1.0 / P, bias=sm[:, EPS5:EPS5 + 1]).then_inc(astep, tick(n_astep))
                for n in range(2):
                    act.wait_ge(astep, n_astep[0] - 1 + n)
                    A(E[:, 2 * n:2 * n + 2, :], E[:, 2 * n:2 * n + 2, :], ACT.Exp, scale=-0.5).then_inc(as_rt, 1)
                gates(6)
                for n in range(8):
                    act.wait_ge(tk_mm, 8 * l + n + 1)
                    if n == 0:
                        act.wait_ge(ya_ready, 4 * (l + 1))
                        act.wait_ge(pt_mm, 3 * (l + 1))
                    A(tok(n // 2)[:, n % 2, :], ps[:, 4 + n % 4, :], ACT.Copy).then_inc(tk_ev, 1)
                gates(7)
                for tt in range(2):
                    act.wait_ge(w1_mm, 2 * l + tt + 1)
                    A(WY[:, tt, :], ps[:, 6, :], ACT.Copy).then_inc(w1_ev, 1)
                    for v in range(5):
                        gates(8 + 5 * tt + v)
                for n in range(4):
                    act.wait_ge(zy_mm, 4 * l + n + 1)
                    if n < 2:
                        A(KK[:, :, n * P:(n + 1) * P], quad(4 + n), ACT.Copy).then_inc(zy_ev, 1)
                    else:
                        A(WY[:, n - 2, :], ps[:, 4 + n, :], ACT.Copy).then_inc(zy_ev, 1)
                gates(99)
                for tt in range(2):
                    act.wait_ge(o_mm, 2 * l + tt + 1)
                    A(AB[:, :, tt * P:(tt + 1) * P], quad(6 + tt), ACT.Copy).then_inc(o_ev, 1)
                act.wait_ge(gn_c, 2 * l + 2)
                A(E[:, :, :], AB[:, :, :], ACT.Square).then_inc(gn_sq, 1)
                for b in range(2):
                    act.wait_ge(gn_mm, 4 * l + 3 + b)
                    A(E[:, 2 * b:2 * b + 2, :], duo(6 + b), ACT.Ln, scale=1.0 / 64, bias=sm[:, EPSG:EPSG + 1]).then_inc(gn_rt, 1)
                for b in range(2):
                    act.wait_ge(gn_rt, 2 * l + 1 + b)
                    A(E[:, 2 * b:2 * b + 2, :], E[:, 2 * b:2 * b + 2, :], ACT.Exp, scale=-0.5).then_inc(gn_inv, 1)
                g0 = PAIRS * l + UP

                def high(i, n, early=False):
                    b = (g0 + n) % 4
                    act.wait_ge(s_w[b], i * 16 + 16 * ((g0 + n) // 4 + 1))
                    for h in range(2):
                        part = slice(h * D, h * D + D)
                        if early:
                            act.wait_ge(pair_done, PAIRS * l + OU)
                        elif h == 0:
                            act.wait_ge(half_done, i * 4 + (MLP * l + n - 1))
                        else:
                            act.wait_ge(pair_done, i * 4 + (g0 + n - 1))
                        A(WH[:, n % 2, part], ring[:, b, part], ACT.Copy).then_inc(hi_ready, 1)

                high(0, 0, True)
                high(0, 1, True)
                squares(2 * l + 1)
                shifts(2 * l + 1, 3 if l == 0 else 9)

                def begin(i, q, first=False):
                    b = (g0 + q) % 4
                    act.wait_ge(pair_done, i * 4 + (g0 + q + 1))
                    if not (first and q < 2):
                        act.wait_ge(g_prod, i * 4 + (FT * l + q - 1))
                    for t in range(2):
                        j = i * 4 + (q + FT * t)
                        A(UB[:, q % 2, t, :], duo(b)[:, t, :], ACT.Identity, scale=PR[:, l, bass.ds(j + (COL["fw"] + 96), 1)],
                          bias=PR[:, l, bass.ds(j + COL["fb"], 1)]).then_inc(u_begun, 1)

                def gelu(i, q):
                    act.wait_ge(cv_done, i * 4 + (FT * l + q + 1))
                    A(UB[:, q % 2, 0, :], UB[:, q % 2, 0, :], ACT.Gelu_apprx_tanh).then_inc(gl_done, 1)

                def hidden_high(i, q):
                    act.wait_ge(g_prod, i * 4 + (FT * l + q + 1))
                    A(GH[:, bass.ds(i * 4 + q, 1), :], TP[:, q % 2:q % 2 + 1, :], ACT.Copy).then_inc(gh_ready, 1)

                def act_tile(i, q, first=False):
                    high(i, q + 2)
                    begin(i, q, first)
                    if not (first and q < 1):
                        gelu(i, q - 1)
                    if not (first and q < 2):
                        hidden_high(i, q - 2)

                for q in range(4):
                    act_tile(0, q, True)
                with act.Fori(1, FT // 4) as i:
                    for q in range(4):
                        act_tile(i, q)
                gelu(0, FT - 1)
                hidden_high(0, FT - 2)
                hidden_high(0, FT - 1)
                with act.Fori(FT // 4, MLP // 4 - 1) as i:
                    for q in range(4):
                        high(i, q + 2)
                high(0, MLP - 2)
                high(0, MLP - 1)
            squares(4)

        @block.vector
        def _(dve):
            V = nc.vector

            def after():
                dve.wait_ge(step, n_step[0])

            dve.wait_ge(s_pr, 16)
            dve.wait_ge(bd_zero, 6)
            dve.wait_ge(pre_act, 1)
            V.scalar_tensor_tensor(sm[:, CSIL:CSIL + 8], sm[:, CSIL:CSIL + 8], 1.0, PR[:, 0, COL["cc"]:COL["cc"] + 8],
                                   ALU.add, ALU.mult).then_inc(step, tick(n_step))
            after()
            V.tensor_scalar(sm[:, CSIL:CSIL + 8], sm[:, CSIL:CSIL + 8], 0.5, None, ALU.mult).then_inc(step, tick(n_step))
            after()

            def derived():
                dve.wait_ge(s_par, 48)
                for n in range(L):
                    V.tensor_scalar(PH[:, n, :], PR[:, n, COL["w0"]:COL["w0"] + 20], 0.5, None, ALU.mult).then_inc(step, tick(n_step))
                lq = E[:, 0:2, :].rearrange("p a b -> p (a b)").rearrange("p (n two d) -> p n two d", n=4, two=2)
                V.tensor_tensor(E[:, 2, :].rearrange("p (n d) -> p n d", n=4), lq[:, :, 0, :], lq[:, :, 1, :], ALU.mult).then_inc(step, tick(n_step))
                after()
                V.reduce_sum(sm[:, 24:28], E[:, 2, :].rearrange("p (n d) -> p n d", n=4), AX_X).then_inc(pre_dve, 1)
                for n in range(L):
                    lam = col(n, "lam", 0, 4)
                    V.scalar_tensor_tensor(sm[:, 40 + 4 * n:44 + 4 * n], lam, -1.0, lam, ALU.mult, ALU.max).then_inc(pre_dve, 1)
                ang, k1, red = YA[:, 2, :], YA[:, 3, :], RT[:, :]
                V.tensor_copy(YA[:, 1, :], YA[:, 0, :].bitcast(I32)).then_inc(step, tick(n_step))
                after()
                V.tensor_scalar(ang, YA[:, 1, :], C[:, FREQ:FREQ + 1], None, ALU.mult).then_inc(step, tick(n_step))
                for n, out in enumerate((red, YA[:, 1, :])):
                    after()
                    V.tensor_scalar(k1, ang, 1.0 / SQ2PI, 0.25 * n, ALU.mult, ALU.add).then_inc(step, tick(n_step))
                    after()
                    V.tensor_scalar(k1, k1, MAGIC, None, ALU.add).then_inc(step, tick(n_step))
                    after()
                    V.tensor_scalar(k1, k1, -MAGIC, None, ALU.add).then_inc(step, tick(n_step))
                    after()
                    V.scalar_tensor_tensor(out, k1, -C1, ang, ALU.mult, ALU.add).then_inc(step, tick(n_step))
                    after()
                    V.scalar_tensor_tensor(out, k1, -C2, out, ALU.mult, ALU.add).then_inc(step, tick(n_step))
                    after()
                    V.scalar_tensor_tensor(out, k1, -C3, out, ALU.mult, ALU.add).then_inc(step, tick(n_step))
                    after()
                    V.tensor_scalar(out, out, 0.5 * math.pi * n, PI_IN, ALU.add, ALU.min).then_inc(step, tick(n_step))
                    after()
                    V.tensor_scalar(out, out, -PI_IN, None, ALU.max).then_inc(pre_dve, 1)
                dve.wait_ge(pre_act, 4)
                for n in range(L):
                    lam = col(n, "lam", 0, 4)
                    V.tensor_tensor(sm[:, NLAM + n:NLAM + n + 1], sm[:, 25 + 2 * n:26 + 2 * n], sm[:, 24 + 2 * n:25 + 2 * n],
                                    ALU.subtract).then_inc(step, tick(n_step))
                    after()
                    V.tensor_scalar(sm[:, NLAM + n:NLAM + n + 1], sm[:, NLAM + n:NLAM + n + 1], -lambda_init(n), None,
                                    ALU.add).then_inc(step, tick(n_step))
                    V.tensor_scalar(sm[:, SUBG + n:SUBG + n + 1], col(n, "sub"), 1.0 - lambda_init(n), None, ALU.mult).then_inc(step, tick(n_step))
                    V.tensor_scalar(sm[:, N8 + 4 * n:N8 + 4 * n + 4], lam, -1.0, 0.0, ALU.mult, ALU.max).then_inc(step, tick(n_step))
                    after()
                    V.tensor_tensor(sm[:, N8 + 4 * n:N8 + 4 * n + 4], sm[:, N8 + 4 * n:N8 + 4 * n + 4], sm[:, 48 + 4 * n:52 + 4 * n],
                                    ALU.add).then_inc(step, tick(n_step))
                    after()
                    V.tensor_scalar(sm[:, N8 + 4 * n:N8 + 4 * n + 4], sm[:, N8 + 4 * n:N8 + 4 * n + 4], -4.0, None,
                                    ALU.mult).then_inc(step, tick(n_step))
                after()
                dve.wait_ge(pre_act, 6)

            def mod_loop_block(i, kt):
                dve.wait_ge(s_m[kt % 2], i * 64 + 16 * (20 - FIRST // 2 + kt // 2 + 1))
                if kt == 0:
                    dve.wait_ge(mod_mm, i + 5)
                    V.tensor_scalar(macc[:, :], mring[:, 0, :], sm[:, CSIL:CSIL + 1], None, ALU.mult).then_inc(mod_used, 1)
                else:
                    dve.wait_ge(mod_used, i * 8 + (40 + kt))
                    V.scalar_tensor_tensor(macc[:, :], mring[:, kt % 2, :], sm[:, CSIL + kt:CSIL + kt + 1], macc[:, :],
                                           ALU.mult, ALU.add).then_inc(mod_used, 1)

            def mod_block(n):
                u, kt = divmod(n, 8)
                if n < FIRST:
                    dve.wait_ge(s_first[n // 2], 16)
                    block = first_blocks(n // 2)[:, n % 2, :]
                else:
                    dve.wait_ge(s_m[n % 2], 16 * ((n - FIRST) // 2 + 1))
                    block = mring[:, n % 2, :]
                if kt == 0:
                    if u:
                        dve.wait_ge(mod_mm, u)
                    V.tensor_scalar(macc[:, :], block, sm[:, CSIL:CSIL + 1], None, ALU.mult).then_inc(mod_used, 1)
                else:
                    dve.wait_ge(mod_used, n)
                    V.scalar_tensor_tensor(macc[:, :], block, sm[:, CSIL + kt:CSIL + kt + 1], macc[:, :],
                                           ALU.mult, ALU.add).then_inc(mod_used, 1)

            def mod_vector(u):
                dve.wait_ge(mod_mm, u + 1)
                lay = 0 if u < 6 else 1
                V.tensor_tensor(mod[:, u, :], ps[:, 7, 0:8], col(lay, "bmod", 8 * (u % 6), 8), ALU.add).then_inc(mod_ready, 1)

            def mod_unit(u):
                for kt in range(8):
                    mod_block(8 * u + kt)
                mod_vector(u)

            mod_unit(0)
            mod_unit(1)
            beside = [FIRST]

            def mod_beside(n):
                for _ in range(n if beside[0] < 40 else 0):
                    mod_block(beside[0])
                    beside[0] += 1

            def norm(n, gain, u):
                if u is None:
                    A_ = gain
                else:
                    dve.wait_ge(mod_ready, u + 1)
                    V.scalar_tensor_tensor(Acol[:, :], mod[:, u, :], 1.0, gain, ALU.add, ALU.mult).then_inc(step, tick(n_step))
                    A_ = Acol
                    after()
                dve.wait_ge(x_rt, n + 1)
                for m in range(KT):
                    V.scalar_tensor_tensor(H[:, m, :], X[:, m, :], A_[:, m:m + 1], RT[:, :], ALU.mult, ALU.mult).then_inc(h_pre, 1)

            def shift(src, dst, n, l, mu, out=None):
                V.tensor_tensor(dst[:, :, 1:S], src[:, :, 0:S - 1], src[:, :, 1:S], ALU.subtract).then_inc(step, tick(n_step))
                V.tensor_scalar(dst[:, :, 0:1], src[:, :, 0:1], -1.0, None, ALU.mult).then_inc(step, tick(n_step))
                after()
                for j in range(n):
                    i = V.scalar_tensor_tensor(dst[:, j, :], dst[:, j, :], col(l, "mu", mu + j), src[:, j, :], ALU.mult, ALU.add)
                    if out is None:
                        i.then_inc(step, tick(n_step))
                    else:
                        i.then_inc(out, 1)

            for l in range(L):
                norm(2 * l, col(l, "n1g", 0, 8), 0 if l == 0 else 6)
                if l == 0:
                    derived()
                dve.wait_ge(bank_free[(PAIRS * l) % 4], EMPTIED[PAIRS * l][(PAIRS * l) % 4] + 1)
                shift(G[:, 0:2, :], YA[:, 0:2, :], 2, l, 0, lora_z)
                if l == 0:
                    mod_beside(2)
                for k in (1, 2):
                    g = PAIRS * l + k
                    dve.wait_ge(bank_free[g % 4], EMPTIED[g][g % 4] + 1)
                shift(G[:, 2:6, :], K_, 4, l, 2)
                after()
                for j in range(4):
                    V.tensor_scalar(KK[:, j, :], K_[:, j, :], col(l, "kk", j), None, ALU.mult).then_inc(kk_raw, 1)
                if l:
                    V.tensor_copy(VF, V_).then_inc(vf_moved, 1)
                if l == 0:
                    mod_beside(2)
                dve.wait_ge(lora_act, 10 * l + 8)
                V.tensor_scalar(AB[:, :, :], AB[:, :, :], 0.5, 0.5, ALU.mult, ALU.add).then_inc(step, tick(n_step))
                V.tensor_scalar(LD, LD, -0.5 * EM05, -0.5 * EM05, ALU.mult, ALU.add).then_inc(step, tick(n_step))
                after()
                for j in range(4):
                    V.tensor_tensor_scan(CUM[:, j, :], C[:, RESET:RESET + S], LD[:, j, :], 0.0, ALU.mult, ALU.add).then_inc(step, tick(n_step))
                for k in (3, 4):
                    g = PAIRS * l + k
                    dve.wait_ge(bank_free[g % 4], EMPTIED[g][g % 4] + 1)
                shift(G[:, 6:10, :], R_, 4, l, 6)
                if l == 0:
                    mod_beside(2)
                after()
                cum4 = CUM.rearrange("p j (c t) -> p (j c) t", t=CH)
                mids = sm[:, MIDS:MIDS + 16]
                V.tensor_copy(mids, cum4[:, :, CH // 2 - 1]).then_inc(step, tick(n_step))
                after()
                V.tensor_tensor(cum4, cum4, along(mids, CH), ALU.subtract).then_inc(step, tick(n_step))
                after()
                V.tensor_tensor(sm[:, GF:GF + 12].rearrange("p (j c) -> p j c", c=3),
                                cum4.rearrange("p (j c) t -> p j c t", c=NCH)[:, :, 0:3, CH - 1],
                                mids.rearrange("p (j c) -> p j c", c=NCH)[:, :, 1:4], ALU.add).then_inc(cc_ready, 1)
                for j in range(4):
                    V.tensor_scalar(BON[:, j, :], AB[:, j, :], -1.0, col(l, "ka", j), ALU.add, ALU.mult).then_inc(step, tick(n_step))
                after()
                V.scalar_tensor_tensor(K_, BON[:, :, :], 1.0, K_, ALU.add, ALU.mult).then_inc(step, tick(n_step))
                after()
                if l == 0:
                    mod_beside(2)
                for k in (5, 6):
                    g = PAIRS * l + k
                    dve.wait_ge(bank_free[g % 4], EMPTIED[g][g % 4] + 1)
                if l:
                    dve.wait_ge(vf_moved, 1)
                shift(G[:, 10:14, :], V_, 4, l, 10)
                after()
                for j in range(4):
                    V.scalar_tensor_tensor(BON[:, j, :], R_[:, j, :], col(l, "rk", j), K_[:, j, :], ALU.mult, ALU.mult).then_inc(rk_ready, 1)
                if l:
                    dve.wait_ge(zv_up, 2)
                    zv, zd = RT[0:32, :], Acol
                    V.tensor_tensor(YB[0:32, 2, 1:S], zv[:, 0:S - 1], zv[:, 1:S], ALU.subtract).then_inc(step, tick(n_step))
                    V.tensor_scalar(YB[0:32, 2, 0:1], zv[:, 0:1], -1.0, None, ALU.mult).then_inc(step, tick(n_step))
                    after()
                    V.scalar_tensor_tensor(YB[0:32, 2, :], YB[0:32, 2, :], PR[0:32, l, COL["vmu"]:COL["vmu"] + 1], zv,
                                           ALU.mult, ALU.add).then_inc(zv_ready, 1)
                    V.tensor_tensor(VF, VF, V_, ALU.subtract).then_inc(step, tick(n_step))
                    dve.wait_ge(zv_up, 7)
                    V.tensor_scalar(E[:, :, :], E[:, :, :], 0.5, 0.5, ALU.mult, ALU.add).then_inc(step, tick(n_step))
                    after()
                    V.tensor_tensor(E[:, :, :], E[:, :, :], VF, ALU.mult).then_inc(v_ready, 1)
                    dve.wait_ge(v_ready, 1)
                    V.tensor_tensor(V_, V_, E[:, :, :], ALU.add).then_inc(v_ready, 1)
                if l == 0:
                    mod_vector(2)
                    mod_beside(2)
                dve.wait_ge(kk_rt, 2 * (l + 1))
                V.tensor_scalar(E[:, :, :], E[:, :, :], 1e-12, None, ALU.max).then_inc(step, tick(n_step))
                after()
                V.reciprocal(E[:, :, :], E[:, :, :]).then_inc(step, tick(n_step))
                after()
                V.tensor_tensor(KK[:, :, :], KK[:, :, :], E[:, :, :], ALU.mult).then_inc(kk_used, 1)
                V.tensor_tensor(LRA, CUM, LD, ALU.subtract).then_inc(cm_ready, 1)
                dve.wait_ge(kk_used, l + 1)
                V.tensor_tensor(AB[:, :, :], AB[:, :, :], KK[:, :, :], ALU.mult).then_inc(step, tick(n_step))
                if l:
                    dve.wait_ge(v_ready, 2)
                dve.wait_ge(bon_mm, l + 1)
                for b in range(2):
                    V.tensor_tensor(BON[:, 2 * b:2 * b + 2, :], duo(6 + b), V_[:, 2 * b:2 * b + 2, :], ALU.mult).then_inc(bon_ready, 1)
                dve.wait_ge(exps, 4 * l + 2)
                V.tensor_tensor(R_, R_, E[:, :, :], ALU.mult).then_inc(feat, 1)
                dve.wait_ge(exps, 4 * l + 3)
                V.tensor_tensor(K_, K_, LRI, ALU.mult).then_inc(feat, 1)
                after()
                V.tensor_tensor(AB[:, :, :], AB[:, :, :], LRI, ALU.mult).then_inc(feat, 1)
                dve.wait_ge(exps, 4 * l + 4)
                V.scalar_tensor_tensor(KK[:, :, :], KK[:, :, :], -1.0, LRA, ALU.mult, ALU.mult).then_inc(feat, 1)
                if l == 0:
                    mod_beside(2)
                for b in range(4):
                    g = PAIRS * l + AT + b
                    dve.wait_ge(bank_free[g % 4], EMPTIED[g][g % 4] + 1)
                    dve.wait_ge(rot_mm, 4 * l + b + 1)
                    tmp = R[:, 16 + 2 * b:18 + 2 * b, :]
                    qk = QK[:, 2 * b:2 * b + 2, :]
                    V.tensor_tensor(tmp, duo(4 + b), over(SIN[:, :], 2), ALU.mult).then_inc(rope_mul, 1)
                    V.tensor_tensor(qk, qk, over(COS[:, :], 2), ALU.mult).then_inc(step, tick(n_step))
                    after()
                    dve.wait_ge(rope_mul, 4 * l + b + 1)
                    V.tensor_tensor(qk, qk, tmp, ALU.add).then_inc(qk_ready, 1)
                for k in (LR, LR + 1):
                    g = PAIRS * l + k
                    dve.wait_ge(bank_free[g % 4], EMPTIED[g][g % 4] + 1)
                for j in range(4):
                    V.tensor_scalar(XC[:, j, :], ZX[:, j, :], col(l, "cw", 12 + j), col(l, "cb", j), ALU.mult, ALU.add).then_inc(step, tick(n_step))
                for d in (1, 2, 3):
                    after()
                    for j in range(4):
                        i = V.scalar_tensor_tensor(XC[:, j, d:S], ZX[:, j, 0:S - d], col(l, "cw", 4 * (3 - d) + j), XC[:, j, d:S],
                                                   ALU.mult, ALU.add)
                        if d == 3:
                            i.then_inc(xc_ready, 1)
                        else:
                            i.then_inc(step, tick(n_step))

                def read_scores(tt):
                    sc = S0 if tt == 0 else S1
                    for n, (t, c, h0, nh) in enumerate(SCORES):
                        if t != tt:
                            continue
                        dve.wait_ge(sc_mm, 6 * l + n + 1)
                        b = SCORE_BANK[n]
                        if tt == 0:
                            V.tensor_tensor(sc[:, c], quad(b), over(C[:, NEG0 + P:NEG0 + 2 * P], 4), ALU.add).then_inc(sc_read, 1)
                        else:
                            V.tensor_tensor(sc[:, c, h0:h0 + 2, :], duo(b), over(C[:, NEG0:NEG0 + 2 * P], 2), ALU.add).then_inc(sc_read, 1)
                    dve.wait_ge(sc_read, 6 * l + (2 if tt == 0 else 6))
                    if tt:
                        dve.wait_ge(p_exp, 16 * l + 8)
                    V.reduce_max(sm[:, MX:MX + 8].rearrange("p (c h) -> p c h", c=2), sc, AX_X).then_inc(step, tick(n_step))
                    after()
                    V.tensor_scalar(sm[:, MX:MX + 8], sm[:, MX:MX + 8], -0.125, None, ALU.mult).then_inc(mx_ready, 1)

                def weights(tt):
                    sc = S0 if tt == 0 else S1
                    dve.wait_ge(p_exp, 16 * l + 8 * (tt + 1))
                    V.reciprocal(sm[:, LSUM:LSUM + 8], sm[:, LSUM:LSUM + 8]).then_inc(step, tick(n_step))
                    after()
                    V.tensor_scalar(sm[:, LSUM + 4:LSUM + 8], sm[:, LSUM + 4:LSUM + 8], sm[:, NLAM + l:NLAM + l + 1], None,
                                    ALU.mult).then_inc(step, tick(n_step))
                    for h in range(4):
                        V.tensor_scalar(sc[:, 0, h, :], sc[:, 0, h, :], sm[:, LSUM + h:LSUM + h + 1], None, ALU.mult).then_inc(step, tick(n_step))
                    after()
                    for h in range(4):
                        V.scalar_tensor_tensor(sc[:, 0, h, :], sc[:, 1, h, :], sm[:, LSUM + 4 + h:LSUM + 5 + h], sc[:, 0, h, :],
                                               ALU.mult, ALU.add).then_inc(p_ready, 1)

                if l == 0:
                    mod_beside(2)
                read_scores(0)
                for j in range(4):
                    dve.wait_ge(lr_act, 8 * l + j + 1)
                    V.tensor_scalar(LRA[:, j, :], LRA[:, j, :], 1.0, sm[:, N8 + 4 * l + j:N8 + 4 * l + j + 1], ALU.add, ALU.mult).then_inc(la_ready, 1)
                dve.wait_ge(lr_act, 8 * (l + 1))
                dve.wait_ge(xc_ready, 4 * (l + 1))
                V.scalar_tensor_tensor(XC, LRI, 1.0, XC, ALU.add, ALU.mult).then_inc(step, tick(n_step))
                dve.wait_ge(la_act, 2 * (l + 1))
                V.tensor_tensor(LRA, E[:, :, :], E[:, :, :], ALU.mult).then_inc(step, tick(n_step))
                after()
                V.scalar_tensor_tensor(LRA, LRA, 1.0, ZX, ALU.add, ALU.mult).then_inc(lq_ready, 1)
                weights(0)
                dve.wait_ge(lq_rt, l + 1)
                V.scalar_tensor_tensor(LRI, LRA, 0.5, XC, ALU.mult, ALU.mult).then_inc(step, tick(n_step))
                after()
                for j in range(4):
                    V.tensor_tensor_scan(ZX[:, j, :], E[:, j, :], LRI[:, j, :], 0.0, ALU.mult, ALU.add).then_inc(step, tick(n_step))
                after()
                for k in (LR + 2, LR + 3):
                    g = PAIRS * l + k
                    dve.wait_ge(bank_free[g % 4], EMPTIED[g][g % 4] + 1)
                for j in range(4):
                    V.tensor_tensor(YA[:, j, :], YA[:, j, :], ZX[:, j, :], ALU.mult).then_inc(ya_ready, 1)
                read_scores(1)
                if l == 0:
                    mod_beside(2)
                weights(1)
                for n, b in enumerate((7, 4)):
                    dve.wait_ge(as_rt, 2 * l + n + 1)
                    e = E[:, 2 * n:2 * n + 2, :]
                    V.scalar_tensor_tensor(YB[:, 2 * n:2 * n + 2, :], duo(b), sm[:, SUBG + l:SUBG + l + 1], e,
                                           ALU.mult, ALU.mult).then_inc(yb_ready, 1)
                if l == 0:
                    mod_vector(3)
                for tt in range(2):
                    base = NSTEP * (2 * l + tt)
                    for n, (kind, par, v, b) in enumerate(STEPS):
                        dve.wait_ge(t_mm, base + n + 1)
                        if kind == "ak":
                            V.tensor_tensor(Mm[:, par], quad(b), over(mat(M_UP), 4), ALU.mult).then_inc(t_ev, 1)
                        elif kind == "n":
                            V.tensor_tensor(Nm[:, par], quad(b), over(mat(M_LOW), 4), ALU.mult).then_inc(t_ev, 1)
                        elif kind == "nt":
                            V.tensor_tensor(TTm[:, 2 * tt + par], quad(b), over(mat(M_U1), 4), ALU.mult).then_inc(t_ev, 1)
                        elif kind == "m":
                            V.tensor_tensor(Mm[:, par], quad(b), over(mat(LEVELS[v]), 4), ALU.mult).then_inc(t_ev, 1)
                        elif kind == "x":
                            T_ = TTm[:, 2 * tt + par]
                            V.tensor_tensor(T_, T_, quad(b), ALU.add).then_inc(t_ev, 1)
                            if l == 0 and par == 1 and v:
                                mod_beside(1)
                        else:
                            T_ = Tm[:, par]
                            V.tensor_tensor(T_, T_, quad(b), ALU.add).then_inc(t_ev, 1)
                for n in range(8):
                    dst = (RKm if n % 2 == 0 else RBm)[:, n // 2]
                    dve.wait_ge(rb_mm, 8 * l + n + 1)
                    V.tensor_tensor(dst, quad(4 + n % 4), over(mat(M_UPI), 4), ALU.mult).then_inc(rb_ev, 1)
                for c in range(NCH):
                    tt, rows = c // 2, slice(64 * (c % 2), 64 * (c % 2) + 64)
                    if c:
                        dve.wait_ge(u_mm, 3 * l + c)
                        V.tensor_tensor(WY[rows, tt, :], ps[rows, 4, :], WY[rows, tt, :], ALU.add).then_inc(u_ready, 1)
                    if c < NCH - 1:
                        dve.wait_ge(s_mm, 3 * l + c + 1)
                        dve.wait_ge(gm_ready, 3 * l + c + 1)
                        if c == 0:
                            V.tensor_tensor(ST, quad(5), GM[c], ALU.mult).then_inc(st_ready, 1)
                        else:
                            dve.wait_ge(st_ready, 3 * l + c)
                            V.tensor_tensor(ST, ST, quad(5), ALU.add).then_inc(step, tick(n_step))
                            after()
                            V.tensor_tensor(ST, ST, GM[c], ALU.mult).then_inc(st_ready, 1)

                def gated(p):
                    br, half = p // 2, p % 2
                    g = PAIRS * l + MG + p
                    dve.wait_ge(pair_done, g + 1)
                    for i, b in enumerate(banks_of(g)):
                        m = 4 * half + 2 * i
                        gate = G[:, 8 * br + m:8 * br + m + 2, :]
                        dst = H[:, m:m + 2, :] if br == 0 else gate
                        V.scalar_tensor_tensor(dst, gate, 1.0, duo(b), ALU.add, ALU.mult).then_inc(bank_free[b], 1)

                gk = PAIRS * l + GA
                for k in range(8, 12):
                    dve.wait_ge(bank_free[(gk + k) % 4], EMPTIED[gk + k][(gk + k) % 4] + 1)
                for p in range(4):
                    gated(p)
                for b in range(2):
                    dve.wait_ge(gn_mm, 4 * l + 1 + b)
                    o = AB[:, 2 * b:2 * b + 2, :]
                    V.scalar_tensor_tensor(o, duo(4 + b), -1.0 / 64, o, ALU.mult, ALU.add).then_inc(gn_c, 1)
                dve.wait_ge(gn_inv, 2 * (l + 1))
                V.tensor_tensor(AB[:, :, :], AB[:, :, :], E[:, :, :], ALU.mult).then_inc(step, tick(n_step))
                after()
                for j in range(4):
                    V.tensor_scalar(AB[:, j, :], AB[:, j, :], col(l, "lng", j), col(l, "lnb", j), ALU.mult, ALU.add).then_inc(step, tick(n_step))
                after()
                V.tensor_tensor(AB[:, :, :], AB[:, :, :], BON[:, :, :], ALU.add).then_inc(step, tick(n_step))
                after()
                V.tensor_tensor(AB[:, :, :], AB[:, :, :], GG[:, :, :], ALU.mult).then_inc(yc_ready, 1)
                if l == 0:
                    mod_vector(4)
                for p in (4, 5):
                    gated(p)
                u = 2 if l == 0 else 8
                dve.wait_ge(mod_ready, u + 1)
                V.tensor_scalar(sm[:, FH:FH + 8], mod[:, u, :], 0.5, None, ALU.mult).then_inc(step, tick(n_step))
                after()

                def residuals(g0, scale):
                    for g in range(g0, g0 + 4):
                        dve.wait_ge(pair_done, g + 1)
                        for i in range(2):
                            m = 2 * (g - g0) + i
                            ins = V.scalar_tensor_tensor(X[:, m, :], duo(g % 4)[:, i, :], scale[:, m:m + 1], X[:, m, :],
                                                         ALU.mult, ALU.add)
                        ins.then_inc(bank_free[g % 4], 1)

                g0 = PAIRS * l + UP

                def low(i, n):
                    b = (g0 + n) % 4
                    for h in range(2):
                        part = slice(h * D, h * D + D)
                        dve.wait_ge(hi_ready, i * 8 + (2 * (MLP * l + n) + h + 1))
                        V.tensor_tensor(WLO[:, n % 2, part], ring[:, b, part], WH[:, n % 2, part].bitcast(F32),
                                        ALU.subtract).then_inc(lo_ready, 1)

                low(0, 0)
                low(0, 1)
                residuals(PAIRS * l + OU, sm[:, FH:FH + 8])
                norm(2 * l + 1, col(l, "n2g", 0, 8), 4 if l == 0 else 10)
                for m in range(KT):
                    dve.wait_ge(hh_ready, KT * l + m + 1)
                    dve.wait_ge(h_ready, KT * (2 * l + 1) + m + 1)
                    V.tensor_tensor(HL[:, m, :], H[:, m, :], HH[:, m, :].bitcast(F32), ALU.subtract).then_inc(hl_ready, 1)
                def conv_read(i, q):
                    if q < 0:
                        return i + EMPTIED[g0 + q + 4][(g0 + q) % 4]
                    return i + (EMPTIED[g0 + q][(g0 + q) % 4] + 1)

                def taps(i, q):
                    b = (g0 + q) % 4
                    for d in (1, 2):
                        for t in range(2):
                            j = i * 4 + (q + FT * t)
                            dve.wait_ge(u_begun if d == 1 else cv_step, i * 8 + (2 * (FT * l + q) + (2 if d == 1 else 1 + t)))
                            ins = V.scalar_tensor_tensor(UB[:, q % 2, t, d:S], duo(b)[:, t, 0:S - d],
                                                         PR[:, l, bass.ds(j + (COL["fw"] + 48 * (2 - d)), 1)], UB[:, q % 2, t, d:S],
                                                         ALU.mult, ALU.add)
                            ins.then_inc(cv_step if d == 1 else (cv_done, bank_free[b])[t], 1)

                def product(i, q):
                    dve.wait_ge(gl_done, i * 4 + (FT * l + q + 1))
                    dve.wait_ge(bank_free[(g0 + q) % 4], conv_read(i, q))
                    V.tensor_tensor(TP[:, q % 2, :], UB[:, q % 2, 0, :], UB[:, q % 2, 1, :], ALU.mult).then_inc(g_prod, 1)

                def hidden_low(i, q):
                    dve.wait_ge(gh_ready, i * 4 + (FT * l + q + 1))
                    V.tensor_tensor(GL[:, bass.ds(i * 4 + q, 1), :], TP[:, q % 2:q % 2 + 1, :],
                                    GH[:, bass.ds(i * 4 + q, 1), :].bitcast(F32), ALU.subtract).then_inc(g_ready, 1)

                def up_tile(i, q, first=False):
                    low(i, q + 2)
                    taps(i, q)
                    if not (first and q < 2):
                        hidden_low(i, q - 2)
                    if not (first and q < 1):
                        product(i, q - 1)

                if l == 0:
                    beside = [(0, 1), (2, 3), (4,), (5,), (6,), (7,), (), ()]
                    for q in range(8):
                        up_tile(0, q, True)
                        for kt in beside[q]:
                            mod_block(40 + kt)
                    mod_vector(5)
                    with dve.Fori(1, 3) as i:
                        for q in range(8):
                            up_tile(i * 2, q)
                            for kt in beside[q]:
                                mod_loop_block(i, kt)
                        dve.wait_ge(mod_mm, i + 6)
                        V.tensor_tensor(mod[:, bass.ds(i + 5, 1), :], ps[:, 7, 0:8].unsqueeze(1),
                                        PR[:, 1, bass.ds(i * 8 + (COL["bmod"] - 8), 8)].unsqueeze(1), ALU.add).then_inc(mod_ready, 1)
                else:
                    for q in range(4):
                        up_tile(0, q, True)
                    with dve.Fori(1, FT // 4) as i:
                        for q in range(4):
                            up_tile(i, q)
                hidden_low(0, FT - 2)
                product(0, FT - 1)
                hidden_low(0, FT - 1)
                for r in range(3):
                    for q in range(4):
                        n = FT + 4 * r + q + 2
                        if n < MLP:
                            low(0, n)
                        if l == 0:
                            if q == 0 and r:
                                mod_vector(7 + r)
                            mod_block(8 * (8 + r) + 2 * q)
                            mod_block(8 * (8 + r) + 2 * q + 1)
                        elif r < 2:
                            mod_block(88 + 4 * r + q)
                mod_vector(10 if l == 0 else 11)
                u = 5 if l == 0 else 11
                dve.wait_ge(mod_ready, u + 1)
                g1 = PAIRS * l + PAIRS - 4
                residuals(g1, mod[:, u, :])
            norm(4, col(0, "fg", 0, 8), None)

        @block.tensor
        def _(pe):
            MM = nc.tensor.matmul

            def mod_sum(u):
                pe.wait_ge(mod_used, 8 * (u + 1))
                if u:
                    pe.wait_ge(mod_ready, u)
                for j in range(KT):
                    i = MM(ps[:, 7, j:j + 1], macc[:, j * P:(j + 1) * P], sm[:, ONE1:ONE1 + 1], start=True, stop=True)
                i.then_inc(mod_mm, 1)

            def ones_sum(n):
                for m in range(KT):
                    pe.wait_ge(x_sq, 8 * n + m + 1)
                    i = MM(ps[:, 4, 0:S], ones[:, :], H[:, m, :], start=(m == 0), stop=(m == KT - 1))
                i.then_inc(x_ss, 1)

            def landed(g):
                pe.wait_ge(s_w[g % 4], 16 * (g // 4 + 1))

            def emptied(g, b):
                if EMPTIED[g][b]:
                    pe.wait_ge(bank_free[b], EMPTIED[g][b])

            def w_of(g, m, k, n=KT):
                return ring[:, g % 4, (m * n + k) * P:(m * n + k + 1) * P]

            def product(l, k, rhs, wait_h=None):
                g = PAIRS * l + k
                landed(g)
                emptied(g, g % 4)
                for m in range(2):
                    for i in range(KT):
                        if wait_h is not None and m == 0:
                            pe.wait_ge(h_ready, wait_h + i + 1)
                        last = MM(ps[:, g % 4, m * S:(m + 1) * S], w_of(g, m, i), rhs[:, i, :], start=(i == 0), stop=(i == KT - 1))
                last.then_inc(pair_done, 1)

            pe.wait_ge(bd_zero, 6)
            for l in range(L):
                ones_sum(2 * l)
                if l == 0:
                    mod_sum(0)
                    mod_sum(1)
                product(l, 0, H, wait_h=16 * l)
                for k in range(1, 4):
                    product(l, k, H)
                pe.wait_ge(s_par, 48)
                pe.wait_ge(s_sw, 80 * (l + 1))
                pe.wait_ge(lora_t, 3 * l + 3)
                pe.wait_ge(x_rt, 2 * l + 1)
                pe.wait_ge(mod_ready, 2 if l == 0 else 11)
                for i in range(2):
                    rows = slice(64 * i, 64 * i + 64)
                    for j in range(4):
                        last = MM(duo(4 + 2 * i + j // 2)[:, j % 2, :], SW[rows, WL + j * P:WL + (j + 1) * P], YA[rows, 0, :],
                                  start=True, stop=True)
                    last.then_inc(lora_mm, 1)
                product(l, 4, H)
                product(l, 5, H)
                pe.wait_ge(lora_act, 10 * l + 4)
                for j in range(4):
                    last = MM(duo(4 + j // 2)[:, j % 2, :], SW[:, WG + j * P:WG + (j + 1) * P], YA[:, 1, :], start=True, stop=True)
                last.then_inc(lora_mm, 1)
                product(l, 6, H)
                if l == 0:
                    pe.wait_ge(lora_act, 8)
                    mod_sum(2)
                if l:
                    pe.wait_ge(s_v12, 32)
                    pe.wait_ge(lora_act, 10 * l + 8)
                    for i in range(KT):
                        last = MM(ps[0:32, 6, 0:S], V1[:, i, :], H[:, i, :], start=(i == 0), stop=(i == KT - 1))
                    last.then_inc(zv_up, 1)
                    product(l, LR, H)
                    pe.wait_ge(zv_ready, 1)
                    for j in range(4):
                        last = MM(duo(6 + j // 2)[:, j % 2, :], V2[0:32, j * P:(j + 1) * P], YB[0:32, 2, :], start=True, stop=True)
                    last.then_inc(zv_up, 1)
                    product(l, LR + 1, H)
                else:
                    product(l, LR, H)
                    product(l, LR + 1, H)
                pe.wait_ge(kk_sq, l + 1)
                pe.wait_ge(lora_act, 10 * l + 10)
                for b in range(2):
                    last = MM(ps[:, 4 + b, :], mat(BLOCKS), E[:, 2 * b:2 * b + 2, :], start=True, stop=True)
                last.then_inc(kk_mm, 1)
                product(l, LR + 2, H)
                product(l, LR + 3, H)
                pe.wait_ge(rk_ready, 4 * (l + 1))
                pe.wait_ge(lora_act, 10 * l + 8)
                if l:
                    pe.wait_ge(zv_up, 7)
                else:
                    pe.wait_ge(mod_ready, 3)
                for b in range(2):
                    last = MM(ps[:, 6 + b, :], mat(BLOCKS), BON[:, 2 * b:2 * b + 2, :], start=True, stop=True)
                last.then_inc(bon_mm, 1)
                for k in range(AT, GA):
                    product(l, k, H)
                pe.wait_ge(kk_rt, 2 * (l + 1))
                pe.wait_ge(bon_ready, 2 * (l + 1))
                for b in range(4):
                    g = PAIRS * l + AT + b
                    pe.wait_ge(bank_free[g % 4], EMPTIED[g][g % 4] + 1)
                    MM(ps[:, 4 + b, :], mat(ROT), QK[:, 2 * b:2 * b + 2, :], start=True, stop=True).then_inc(rot_mm, 1)
                for t in range(2):
                    g = PAIRS * l + AT + 4 + t
                    pe.wait_ge(bank_free[g % 4], EMPTIED[g][g % 4] + 1)
                for t in range(2):
                    pe.wait_ge(rope_mul, 4 * l + t + 1)
                    for j in range(4):
                        last = nc.tensor.transpose(ps[:, 4 + t, j * P:(j + 1) * P], VR[:, j, t * P:(t + 1) * P], mat(IDENT))
                    last.then_inc(avt_mm, 1)
                for i in range(2):
                    for h in range(2):
                        pe.wait_ge(xc_ready, 4 * l + 2 * h + 2)
                        if i == 0:
                            pe.wait_ge(avt_ev, 2 * l + h + 1)
                        else:
                            pe.wait_ge(rope_mul, 4 * l + 4)
                        for j in (2 * h, 2 * h + 1):
                            last = MM(duo((4 if i == 0 else 6) + h)[:, j % 2, :], SW[:, WA + W * i + j * P:WA + W * i + (j + 1) * P],
                                      XC[:, j, :], start=True, stop=True)
                        last.then_inc(lr_mm, 1)
                filled = [0]

                def fill(point):
                    n = FILL[point] if point < len(FILL) else 192 - filled[0]
                    for _ in range(n):
                        k, r = divmod(filled[0], 16)
                        m, i = divmod(r, 8)
                        g = PAIRS * l + GA + k
                        if r == 0:
                            landed(g)
                            emptied(g, g % 4)
                        last = MM(ps[:, g % 4, m * S:(m + 1) * S], w_of(g, m, i), H[:, i, :], start=(i == 0), stop=(i == KT - 1))
                        if r == 15:
                            last.then_inc(pair_done, 1)
                        filled[0] += 1

                def scores(n):
                    t, c, h0, nh = SCORES[n]
                    rows = slice(64 * c, 64 * c + 64)
                    nk = P * (t + 1)
                    for i in range(nh):
                        h = h0 + i
                        last = MM(ps[:, SCORE_BANK[n], i * nk:(i + 1) * nk], QK[rows, h, t * P:(t + 1) * P], QK[rows, 4 + h, 0:nk],
                                  start=True, stop=True)
                    last.then_inc(sc_mm, 1)

                fill(0)
                pe.wait_ge(qk_ready, 4 * (l + 1))
                pe.wait_ge(lr_act, 8 * (l + 1))
                scores(0)
                scores(1)
                fill(1)
                scores(2)
                scores(3)
                pe.wait_ge(sc_read, 6 * l + 1)
                scores(4)
                pe.wait_ge(sc_read, 6 * l + 2)
                scores(5)
                fill(2)
                fill(3)
                fill(4)
                for n, (kt, qt) in enumerate(((0, 0), (0, 1), (1, 1))):
                    pe.wait_ge(sc_read, 6 * (l + 1))
                    for h in range(4):
                        pe.wait_ge(p_ready, 8 * l + 4 * qt + h + 1)
                        src = S0[:, 0, h, :] if qt == 0 else S1[:, 0, h, kt * P:(kt + 1) * P]
                        last = nc.tensor.transpose(ps[:, 4 + n, h * P:(h + 1) * P], src, mat(IDENT))
                    last.then_inc(pt_mm, 1)
                fill(5)
                for n, b in enumerate((7, 4)):
                    pe.wait_ge(pt_ev, 3 * (l + 1))
                    for h in (2 * n, 2 * n + 1):
                        MM(ps[:, b, (h % 2) * S:(h % 2 + 1) * S], AVT[:, 0, h * P:(h + 1) * P], PT[:, 0, h, :], start=True, stop=False)
                        last = MM(ps[:, b, (h % 2) * S + P:(h % 2 + 1) * S], AVT[:, 1, h * P:(h + 1) * P], PT[:, 1, h, P:S],
                                  start=False, stop=True)
                    last.then_inc(ao_mm, 1)
                for n in range(2):
                    pe.wait_ge(ao_sq, 2 * l + n + 1)
                    MM(ps[:, 5 + n, :], ones[:, :], E[:, 2 * n:2 * n + 2, :], start=True, stop=True).then_inc(as_mm, 1)
                fill(6)
                pe.wait_ge(feat, 4 * (l + 1))
                for n in range(8):
                    t = n % 2
                    src = (KK, AB, K_, V_)[n // 2]
                    pe.wait_ge(yb_ready, 2 * (l + 1))
                    if l == 0 and n == 0:
                        mod_sum(3)
                    if l == 0 and n == 3:
                        pe.wait_ge(mod_ready, 4)
                    if n >= 4:
                        pe.wait_ge(tk_ev, 8 * l + n - 3)
                    for j in range(4):
                        last = nc.tensor.transpose(ps[:, 4 + n % 4, j * P:(j + 1) * P], src[:, j, t * P:(t + 1) * P], mat(IDENT))
                    last.then_inc(tk_mm, 1)
                fill(7)
                for tt in range(2):
                    base = NSTEP * (2 * l + tt)
                    cols = slice(tt * P, (tt + 1) * P)
                    for n, (kind, par, v, b) in enumerate(STEPS):
                        rows = slice(64 * par, 64 * par + 64)
                        t_ = 2 * tt + par
                        if kind in ("ak", "n", "nt"):
                            if kind != "nt":
                                if tt == 0:
                                    pe.wait_ge(tk_ev, 8 * l + 8)
                                else:
                                    pe.wait_ge(t_ev, base)
                            else:
                                pe.wait_ge(t_ev, base + par + 1)
                            a, bb = {"ak": (K_, KK), "n": (KK, AB), "nt": (AB, KK)}[kind]
                            for j in range(4):
                                last = MM(quad(b)[:, j, :], a[rows, j, cols], bb[rows, j, cols], start=True, stop=True)
                        elif kind == "m":
                            if v == 0:
                                pe.wait_ge(t_init, 6 * (2 * l + tt) + 3 * par + 3)
                                pe.wait_ge(w1_ev, 2 * l + tt + 1)
                            else:
                                pe.wait_ge(t_ev, base + step_no("x", par, v - 1) + 1)
                            for j in range(4):
                                last = MM(quad(b)[:, j, :], Nm[:, par, j, :], TTm[:, t_, j, :], start=True, stop=True)
                        elif kind == "x":
                            pe.wait_ge(t_ev, base + step_no("m", par, v) + 1)
                            if v:
                                pe.wait_ge(t_ev, base + step_no("xt", par, v - 1) + 1)
                            for j in range(4):
                                last = MM(quad(b)[:, j, :], Tm[:, par, j, :], Mm[:, par, j, :], start=True, stop=True)
                        else:
                            for j in range(4):
                                last = MM(quad(b)[:, j, :], Mm[:, par, j, :], Tm[:, par, j, :], start=True, stop=True)
                        last.then_inc(t_mm, 1)
                        if n == 5:
                            pe.wait_ge(t_ev, base + 4)
                            for j in range(4):
                                for p2 in range(2):
                                    h = 2 * j + p2
                                    last = MM(ps[:, 6, h * 64:(h + 1) * 64], Mm[:, p2, j, :], VT_[:, tt, h * 64:(h + 1) * 64],
                                              start=True, stop=True)
                            last.then_inc(w1_mm, 1)
                        if kind == "x" and par == 1:
                            fill(8 + 5 * tt + v)
                pe.wait_ge(t_ev, NSTEP * 2 * (l + 1))
                for tt in range(2):
                    for j in range(4):
                        for p2 in range(2):
                            h = 2 * j + p2
                            last = MM(quad(4 + tt)[64 * p2:64 * p2 + 64, j, :], AT_[:, tt, h * 64:(h + 1) * 64], TTm[:, 2 * tt + p2, j, :],
                                      start=True, stop=True)
                    last.then_inc(zy_mm, 1)
                for tt in range(2):
                    for j in range(4):
                        for p2 in range(2):
                            h = 2 * j + p2
                            last = MM(ps[:, 6 + tt, h * 64:(h + 1) * 64], TTm[:, 2 * tt + p2, j, :], WY[:, tt, h * 64:(h + 1) * 64],
                                      start=True, stop=True)
                    last.then_inc(zy_mm, 1)
                for n in range(8):
                    tt, par = n // 4, (n // 2) % 2
                    rows, cols = slice(64 * par, 64 * par + 64), slice(tt * P, (tt + 1) * P)
                    if n < 4:
                        pe.wait_ge(zy_ev, 4 * l + n + 1)
                    else:
                        pe.wait_ge(rb_ev, 8 * l + n - 3)
                    a = K_ if n % 2 == 0 else AB
                    for j in range(4):
                        last = MM(quad(4 + n % 4)[:, j, :], a[rows, j, cols], R_[rows, j, cols], start=True, stop=True)
                    last.then_inc(rb_mm, 1)
                fill(99)

                def read_part(tt, m, tokm, first):
                    for j in range(4):
                        for p2 in range(2):
                            h = 2 * j + p2
                            last = MM(quad(6 + tt)[64 * p2:64 * p2 + 64, j, :], tokm[:, tt, h * 64:(h + 1) * 64], m[:, 2 * tt + p2, j, :],
                                      start=(first and j == 0), stop=False, skip_group_check=True)
                    return last

                pe.wait_ge(rb_ev, 8 * (l + 1))
                pe.wait_ge(zy_ev, 4 * (l + 1))
                read_part(0, RKm, VT_, True)
                read_part(1, RKm, VT_, True)
                for c in range(NCH):
                    tt, hf = c // 2, c % 2
                    rows = slice(64 * hf, 64 * hf + 64)
                    cols = slice(64 * c, 64 * c + 64)
                    if c < NCH - 1:
                        if c:
                            pe.wait_ge(st_ready, 3 * l + c)
                        for j in range(4):
                            MM(quad(5)[:, j, :], KT_[rows, tt, j * P:(j + 1) * P], VT_[rows, tt, j * P:(j + 1) * P],
                               start=(j == 0), stop=False, skip_group_check=True)
                    if c:
                        pe.wait_ge(st_ready, 3 * l + c)
                        for j in range(4):
                            last = MM(quad(4)[rows, j, :], KK[:, j, cols], ST[:, j, :], start=True, stop=True)
                        last.then_inc(u_mm, 1)
                        for j in range(4):
                            last = MM(quad(6 + tt)[:, j, rows], ST[:, j, :], R_[:, j, cols], start=False, stop=False, skip_group_check=True)
                        pe.wait_ge(u_ready, 3 * l + c)
                    if c < NCH - 1:
                        for j in range(4):
                            last = MM(quad(5)[:, j, :], BT_[rows, tt, j * P:(j + 1) * P], WY[rows, tt, j * P:(j + 1) * P],
                                      start=False, stop=(j == 3), skip_group_check=True)
                        last.then_inc(s_mm, 1)
                    if hf == 1:
                        read_part(tt, RBm, WY, False).then_inc(o_mm, 1)

                def merge(p, y):
                    g = PAIRS * l + MG + p
                    landed(g)
                    for i, b in enumerate(banks_of(g)):
                        emptied(g, b)
                        for m in (2 * i, 2 * i + 1):
                            for k in range(4):
                                last = MM(ps[:, b, (m % 2) * S:(m % 2 + 1) * S], w_of(g, m, k, 4), y[:, k, :], start=(k == 0), stop=(k == 3))
                    last.then_inc(pair_done, 1)

                pe.wait_ge(ya_ready, 4 * (l + 1))
                merge(0, YA)
                for b in range(2):
                    pe.wait_ge(o_ev, 2 * (l + 1))
                    MM(ps[:, 4 + b, :], mat(BLOCKS), AB[:, 2 * b:2 * b + 2, :], start=True, stop=True).then_inc(gn_mm, 1)
                merge(1, YA)
                pe.wait_ge(yb_ready, 2 * (l + 1))
                merge(2, YB)
                merge(3, YB)
                pe.wait_ge(gn_sq, l + 1)
                for b in range(2):
                    MM(ps[:, 6 + b, :], mat(BLOCKS), E[:, 2 * b:2 * b + 2, :], start=True, stop=True).then_inc(gn_mm, 1)
                if l == 0:
                    pe.wait_ge(gn_rt, 2 * (l + 1))
                    mod_sum(4)
                pe.wait_ge(yc_ready, l + 1)
                merge(4, AB)
                merge(5, AB)
                pe.wait_ge(mg_ready, 8 * (l + 1))
                for j in range(4):
                    product(l, OU + j, H)
                ones_sum(2 * l + 1)
                g0 = PAIRS * l + UP

                def passes(out, n, m, k, high, low, start, stop):
                    at = slice((m * KT + k) * P, (m * KT + k + 1) * P)
                    MM(out, WH[:, n % 2, at], high, start=start, stop=False, skip_group_check=True)
                    MM(out, WH[:, n % 2, at], low, start=False, stop=False, skip_group_check=True)
                    return MM(out, WLO[:, n % 2, at], high, start=False, stop=stop, skip_group_check=True)

                def up(i, q, first=False):
                    g = g0 + q
                    b = g % 4
                    pe.wait_ge(bank_free[b], i + EMPTIED[g][b])
                    for m in range(2):
                        pe.wait_ge(lo_ready, i * 8 + (2 * (MLP * l + q) + m + 1))
                        for k in range(KT):
                            if first and q == 0 and m == 0:
                                pe.wait_ge(hl_ready, KT * l + k + 1)
                            last = passes(ps[:, b, m * S:(m + 1) * S], q, m, k, HH[:, k, :], HL[:, k, :], k == 0, k == KT - 1)
                        last.then_inc((half_done, pair_done)[m], 1)

                for q in range(4):
                    up(0, q, True)
                if l == 0:
                    for q in range(4, 8):
                        up(0, q)
                    mod_sum(5)
                    with pe.Fori(1, 3) as i:
                        for q in range(8):
                            up(i * 2, q)
                        pe.wait_ge(mod_used, i * 8 + 48)
                        pe.wait_ge(mod_ready, i + 5)
                        for j in range(KT):
                            last = MM(ps[:, 7, j:j + 1], macc[:, j * P:(j + 1) * P], sm[:, ONE1:ONE1 + 1], start=True, stop=True)
                        last.then_inc(mod_mm, 1)
                else:
                    with pe.Fori(1, FT // 4) as i:
                        for q in range(4):
                            up(i, q)

                def down(i, q, first=False):
                    g = PAIRS * l + DN + q
                    b = g % 4
                    if first:
                        emptied(g, b)
                    for m in range(2):
                        pe.wait_ge(lo_ready, i * 8 + (2 * (MLP * l + FT + q) + m + 1))
                        for k in range(KT):
                            if first and q == 0 and m == 0:
                                pe.wait_ge(g_ready, FT * l + k + 1)
                            at = k if first else bass.ds(i * 8 + k, 1)
                            last = passes(ps[:, b, m * S:(m + 1) * S], q, m, k, GH[:, at, :], GL[:, at, :],
                                          first and m == 0 and k == 0, False)
                        last.then_inc((half_done, pair_done)[m], 1)

                for q in range(4):
                    down(0, q, True)
                if l == 0:
                    mod_sum(8)
                pe.wait_ge(g_ready, FT * (l + 1))
                with pe.Fori(1, 3) as i:
                    for q in range(4):
                        down(i, q)
                    if l == 0:
                        pe.wait_ge(mod_used, i * 8 + 72)
                        pe.wait_ge(mod_ready, i + 8)
                        for j in range(KT):
                            last = MM(ps[:, 7, j:j + 1], macc[:, j * P:(j + 1) * P], sm[:, ONE1:ONE1 + 1], start=True, stop=True)
                        last.then_inc(mod_mm, 1)
                if l == 1:
                    mod_sum(11)
            ones_sum(4)


def kernel(x, c, positions, w_mod, b_mod, norm1_g, norm2_g, final_g, w_in, w_merge_a, w_merge_b, w_merge_c, w_out,
           lru_conv_w, lru_conv_b, lru_wa, lru_ba, lru_wx, lru_bx, lru_lambda, diff_lq1, diff_lk1, diff_lq2, diff_lk2,
           diff_subln_g, rwkv_mu, rwkv_w0, rwkv_w2, rwkv_a0, rwkv_a2, rwkv_g2, rwkv_kk, rwkv_ka, rwkv_rk, rwkv_lnx_g,
           rwkv_lnx_b, rwkv_v0, rwkv_v1, rwkv_v2, rwkv_vmu, ffn_up, ffn_conv_w, ffn_conv_b, ffn_down):
    import concourse.bacc as bacc
    from concourse.bass_utils import run_bass_kernel_spmd

    f = np.ascontiguousarray

    def blocks(w):
        return w.reshape(w.shape[0] // P, P, w.shape[1] // P, P).transpose(2, 0, 1, 3)

    def pairs(b):
        return b.reshape(-1, 16, P, P).transpose(0, 2, 1, 3).reshape(-1, P, PAIR)

    def tiles(v):
        return v.reshape(-1, P).T

    wmain, wmod, small, prs = [], [], [], []
    zero = np.zeros
    for l in range(L):
        b = blocks(w_in[l])
        gate, lx, q, rw = b[0:24], b[24:32], b[32:44], b[44:58]
        rkv, lora = rw[0:12], rw[12:14]
        wmain.append(pairs(np.concatenate([lora, rkv[4:8], rkv[0:4], rkv[8:12], lx, q, gate])))
        for w in (w_merge_a, w_merge_b, w_merge_c):
            wmain.append(pairs(blocks(w[l])))
        wmain.append(pairs(blocks(w_out[l])))
        up = blocks(ffn_up[l])
        wmain.append(pairs(np.stack([up[0:FT], up[FT:]], axis=1)))
        dn = blocks(ffn_down[l])
        wmain.append(pairs(dn.reshape(KT, 3, KT, P, P).transpose(1, 0, 2, 3, 4)))
        vecs = w_mod[l].reshape(KT, P, 6, D)
        order = (1, 0, 2, 3, 4, 5)
        wmod.append(vecs[:, :, order].transpose(2, 0, 1, 3).reshape(6 * KT, P, D))
        bm = b_mod[l].reshape(6, D)[list(order)].reshape(-1)

        def bd(w):
            return w.reshape(4, 2, 64, 64).transpose(1, 2, 0, 3).reshape(P, 256)

        small.append(np.concatenate([np.concatenate([rwkv_w2[l], rwkv_a2[l]], axis=0), rwkv_g2[l], bd(lru_wa[l]), bd(lru_wx[l])], axis=1))
        mu = rwkv_mu[l]
        mu = np.concatenate([mu[3 * W:], mu[W:2 * W], mu[0:W], mu[2 * W:3 * W]])
        v0 = rwkv_v0[l - 1] if l else zero(W, np.float32)
        vmu = np.concatenate([rwkv_vmu[l - 1], zero(P - 32, np.float32)]) if l else zero(P, np.float32)
        parts = {"n1g": norm1_g[l], "n2g": norm2_g[l], "bmod": bm, "mu": mu, "w0": rwkv_w0[l], "a0": rwkv_a0[l], "v0": v0,
                 "ba": lru_ba[l].reshape(-1), "bx": lru_bx[l].reshape(-1), "kk": rwkv_kk[l], "ka": rwkv_ka[l],
                 "rk": rwkv_rk[l].reshape(-1), "lng": rwkv_lnx_g[l], "lnb": rwkv_lnx_b[l], "vmu": vmu, "sub": diff_subln_g[l],
                 "cw": lru_conv_w[l].reshape(-1), "cb": lru_conv_b[l], "lam": lru_lambda[l], "fw": ffn_conv_w[l].reshape(-1),
                 "fb": ffn_conv_b[l], "fg": final_g, "cc": c[0]}
        prs.append(np.concatenate([tiles(np.asarray(parts[n])) for n, _ in _NAMES], axis=1))
    v1v2 = np.concatenate([np.asarray(rwkv_v1[0]).reshape(KT, P, 32).transpose(1, 0, 2).reshape(P, 256),
                           np.concatenate([rwkv_v2[0], zero((P - 32, W), np.float32)])], axis=1)
    lqk = np.stack([diff_lq1, diff_lk1, diff_lq2, diff_lk2], axis=1).reshape(-1)

    i, j = np.arange(P)[:, None], np.arange(P)[None, :]
    same = i // CH == j // CH

    def level(s):
        return (i // (2 * s) == j // (2 * s)) & (i // s % 2 == 0) & (j // s % 2 == 1)

    rot = zero((P, P), np.float32)
    for p in range(P):
        if p % 64 < 8:
            rot[p + 8, p] = -1
        elif p % 64 < 16:
            rot[p - 8, p] = 1
    mats = [i == j, i // 64 == j // 64, same & (j < i), same & (j > i), same & (j >= i), level(1).T, level(1), level(2), level(4),
            level(8), level(16), level(32), rot]
    neg = np.where(np.arange(2 * P)[None, :] > P + i, np.float32(-1e30), np.float32(0))
    reset = np.broadcast_to((np.arange(S) % CH != 0)[None, :], (P, S))
    inv = (np.float32(500000.0) ** (-np.arange(0, 16, 2, dtype=np.float32) / np.float32(16))).astype(np.float32)
    freq = np.where(i % 64 < 16, inv[i % 8], np.float32(0))
    consts = np.concatenate([m.astype(np.float32) for m in mats] + [neg, reset.astype(np.float32), freq], axis=1).astype(np.float32)

    arrays = {
        "wmain": f(np.concatenate(wmain)), "wmod": f(np.concatenate(wmod)), "small": f(np.stack(small)), "v1v2": f(v1v2),
        "params": f(np.stack(prs, axis=1)), "consts": f(consts), "lqk": f(lqk),
        "x_t": f(np.asarray(x)[0].T.reshape(KT, P, S).transpose(1, 0, 2)), "positions": f(np.asarray(positions)[0]),
    }
    nc = bacc.Bacc("TRN2", target_bir_lowering=False, num_devices=1)
    args = [nc.dram_tensor(f"{n}_dram", a.shape, mybir.dt.from_np(a.dtype), kind="ExternalInput").ap() for n, a in arrays.items()]
    args.append(nc.dram_tensor("y_dram", (P, KT, S), F32, kind="ExternalOutput").ap())
    trunk_kernel(nc, *args)
    r = run_bass_kernel_spmd(nc, [{f"{n}_dram": a for n, a in arrays.items()}], core_ids=[0])
    y = r.results[0]["y_dram"]
    return y.transpose(1, 0, 2).reshape(D, S).T.reshape(1, S, D)
```

```python
import math
from contextlib import ExitStack

import numpy as np

import concourse.bass as bass
from concourse import mybir

ALU = mybir.AluOpType
ACT = mybir.ActivationFunctionType
F32 = mybir.dt.float32
F32R = mybir.dt.float32r
I32 = mybir.dt.int32
AX_X = mybir.AxisListType.X

P = 128
D = 1024
S = 256
L = 2
KT = D // P
W = 512
WT = W // P
FT = 3 * D // P
CH = 64
NCH = S // CH

RW, LR, AT, GA, OU, UP, DN, PAIRS = 0, 7, 11, 17, 35, 39, 63, 75
GATES, MERGE = 12, GA + 12
MLP = PAIRS - UP
FIRST = 16
SLOTS = 4
PAIR = 2048

_NAMES = [("n1g", 8), ("n2g", 8), ("bmod", 48), ("mu", 14), ("w0", 4), ("a0", 4), ("v0", 4), ("ba", 4), ("bx", 4),
          ("kk", 4), ("ka", 4), ("rk", 4), ("lng", 4), ("lnb", 4), ("vmu", 1), ("sub", 1), ("cw", 16), ("cb", 4),
          ("lam", 4), ("fw", 144), ("fb", 48), ("fg", 8), ("cc", 8)]
COL, NP = {}, 0
for _n, _w in _NAMES:
    COL[_n] = NP
    NP += _w

(IDENT, BLOCKS, M_LOW, M_UP, M_UPI, M_L1, M_U1, M_U2, M_U4, M_U8, M_U16, M_U32, ROT) = range(13)
NMAT = 13
NEG0 = NMAT * P
RESET = NEG0 + 256
FREQ = RESET + 256
NC_ = FREQ + 1

WL, WG, WA, WX = 0, 512, 1024, 1536

SQ2PI = 2.0 * math.pi
MAGIC = 1.5 * 2.0 ** 23
C1 = 6.28125
C2 = float(np.float32(SQ2PI - C1))
C3 = SQ2PI - C1 - C2
PI_IN = 3.1415925
EM05 = math.exp(-0.5)


def lambda_init(l):
    return 0.8 - 0.6 * math.exp(-0.3 * l)


def banks_of(g):
    l, k = divmod(g, PAIRS)
    if MERGE <= k < OU:
        return [(2 * (k - MERGE)) % 4, (2 * (k - MERGE) + 1) % 4]
    return [g % 4]


def _emptied():
    count, out = [0] * 4, []
    for g in range(L * PAIRS):
        out.append(list(count))
        if not DN <= g % PAIRS < PAIRS - 4:
            for b in banks_of(g):
                count[b] += 1
    return out


EMPTIED = _emptied()

FILL = [4, 16, 24, 16, 16, 4, 12, 8] + [8, 6, 6, 6, 8] * 2
FILL_CHAIN = 4
FILLED = np.cumsum(FILL) // 16

SCORES = [(0, 0, 0, 4), (0, 1, 0, 4), (1, 0, 0, 2), (1, 1, 0, 2), (1, 0, 2, 2), (1, 1, 2, 2)]
SCORE_BANK = [6, 7, 4, 5, 6, 7]
DN_BLOCKS = [2, 2, 2, 1, 1, 0, 1, 2, 2, 2, 1, 0]
DN_SUM = 6
LEVELS = [M_U2, M_U4, M_U8, M_U16, M_U32]


def solve_steps():
    steps = [("ak", 0, 0, 4), ("ak", 1, 0, 5), ("n", 0, 0, 6), ("n", 1, 0, 7), ("nt", 0, 0, 4), ("nt", 1, 0, 5)]
    other = 6
    for v in range(len(LEVELS)):
        for kind in ("m", "x", "xt"):
            if kind == "xt" and v == len(LEVELS) - 1:
                continue
            for par in (0, 1):
                steps.append((kind, par, v, other + par))
            other = 10 - other
    return steps


STEPS = solve_steps()
NSTEP = len(STEPS)


def step_no(kind, par, v):
    return next(i for i, s in enumerate(STEPS) if s[:3] == (kind, par, v))


def trunk_kernel(nc, wmain, wmod, small, v1v2, params, consts, lqk, x_t, positions, y_t):
    ctx = ExitStack()
    with ctx:
        def sb(name, shape, dt=F32):
            return ctx.enter_context(nc.sbuf_tensor(name, shape, dt))

        def sem(name):
            return ctx.enter_context(nc.semaphore(name))

        X = sb("X", [P, KT, S])
        H = sb("H", [P, KT, S])
        ring = sb("ring", [P, SLOTS, PAIR])
        mring = sb("mring", [P, 2, D])
        macc = sb("macc", [P, D])
        C = sb("C", [P, NC_])
        PR = sb("PR", [P, L, NP])
        PH = sb("PH", [P, L, 20])
        SW = sb("SW", [P, 2048])
        COS = sb("COS", [P, S])
        SIN = sb("SIN", [P, S])
        at_g = nc.sbuf_base
        G = sb("G", [P, FT, S])
        at_r = nc.sbuf_base
        R = sb("R", [P, 24, S])
        at_k = nc.sbuf_base + WT * S * 4
        ZS = sb("ZS", [P, 12, S])
        AB = sb("AB", [P, WT, S])
        KK = sb("KK", [P, WT, S])
        GG = sb("GG", [P, WT, S])
        BON = sb("BON", [P, WT, S])
        E = sb("E", [P, WT, S])
        WY = sb("WY", [P, 2, W])
        at_y = nc.sbuf_base
        YA = sb("YA", [P, WT, S])
        YB = sb("YB", [P, WT, S])
        at_tk = nc.sbuf_base
        TK = sb("TK", [P, 16, S])
        WH = nc.alloc_sbuf_tensor_at("WH", [P, 2, PAIR], F32R, offset=at_k)
        WLO = nc.alloc_sbuf_tensor_at("WLO", [P, 2, PAIR], F32R, offset=at_k + 16 * S * 4)
        HH = nc.alloc_sbuf_tensor_at("HH", [P, KT, S], F32R, offset=at_y)
        HL = nc.alloc_sbuf_tensor_at("HL", [P, KT, S], F32R, offset=at_tk + 8 * S * 4)
        GH = nc.alloc_sbuf_tensor_at("GH", [P, FT, S], F32R, offset=at_g)
        GL = nc.alloc_sbuf_tensor_at("GL", [P, FT, S], F32R, offset=at_r)
        OWH = nc.alloc_sbuf_tensor_at("OWH", [P, 2, PAIR], F32R, offset=at_r)
        OWL = nc.alloc_sbuf_tensor_at("OWL", [P, 2, PAIR], F32R, offset=at_tk)
        MH, ML = GH[:, 8:16, :], GH[:, 16:24, :]
        RT = sb("RT", [P, S])
        mod = sb("mod", [P, 12, KT])
        Acol = sb("Acol", [P, KT])
        ones = sb("ones", [P, P])
        sm = sb("sm", [P, 80])
        CSIL, NLAM, N8, SUBG, ONE1 = 0, 8, 10, 18, 20
        EPS6, EPS5, EPSG = 21, 22, 23
        MIDS, GF, MX, LSUM = 24, 40, 52, 60
        FH = 68

        ps = ctx.enter_context(nc.psum_tensor("ps", [P, 8, 512], F32))

        V_, K_, R_ = ZS[:, 0:4, :], ZS[:, 4:8, :], ZS[:, 8:12, :]
        LD, CUM = G[:, 14:18, :], G[:, 18:22, :]
        V1 = G[:, 22, :].rearrange("p (k m) -> p k m", k=KT)
        V2 = YB[:, 0:2, :].rearrange("p a b -> p (a b)")
        ZX, XC, LRA, LRI = TK[:, 0:4, :], TK[:, 4:8, :], TK[:, 8:12, :], TK[:, 12:16, :]
        QK, VR = R[:, 0:8, :], R[:, 8:12, :]
        VF = R[:, 0:4, :]
        AVT = R[:, 12:16, :].rearrange("p a b -> p (a b)").rearrange("p (t w) -> p t w", t=2)
        S0 = R[:, 16:20, :].rearrange("p a b -> p (a b)").rearrange("p (c h k) -> p c h k", c=2, h=4)
        S1 = TK[:, 8:16, :].rearrange("p (c h) k -> p c h k", c=2)
        PT = R[:, 0:8, :].rearrange("p (t h) q -> p t h q", t=2)

        def tok(i):
            return TK[:, 4 * i:4 * i + 4, :].rearrange("p a b -> p (a b)").rearrange("p (t w) -> p t w", t=2)

        AT_, BT_, KT_, VT_ = tok(0), tok(1), tok(2), tok(3)

        def mats(a, b):
            return R[:, a:b, :].rearrange("p a b -> p (a b)").rearrange("p (g j s) -> p g j s", j=4, s=P)

        TTm, Nm, Tm, Mm = mats(0, 8), mats(8, 12), mats(12, 16), mats(16, 20)
        RBm, RKm = mats(8, 16), mats(16, 24)
        ge = E[:, :, :].rearrange("p a b -> p (a b)").rearrange("p (c j s) -> p c j s", c=2, j=4)
        ga = TK[:, 0:4, :].rearrange("p a b -> p (a b)").rearrange("p (c j s) -> p c j s", c=2, j=4)
        GM = [ge[:, 0], ge[:, 1], ga[:, 0]]
        ST = ga[:, 1]
        UB = TK[:, 0:4, :].rearrange("p (u t) s -> p u t s", u=2)
        TP = TK[:, 4:6, :]

        def first_blocks(g):
            buf, i = ((G, g), (R, g - 3), (TK, g - 6))[(g >= 3) + (g >= 6)]
            return buf[:, 8 * i:8 * i + 8, :].rearrange("p (n a) b -> p n (a b)", n=2)

        def mat(i):
            return C[:, i * P:(i + 1) * P]

        def col(l, name, i=0, n=1):
            return PR[:, l, COL[name] + i:COL[name] + i + n]

        def flat(ap):
            return ap.rearrange("p a b -> p (a b)")

        def over(ap, n):
            return ap.unsqueeze(1).broadcast_to([ap.shape[0], n, ap.shape[1]])

        def along(ap, n):
            return ap.unsqueeze(2).broadcast_to([ap.shape[0], ap.shape[1], n])

        def quad(b):
            return ps[:, b, :].rearrange("p (j s) -> p j s", j=4)

        def every_other(ap, odd):
            if len(ap.shape) == 2:
                return ap.rearrange("p (n two) -> p n two", two=2)[:, :, odd]
            return ap.rearrange("p j (n two) -> p j n two", two=2)[:, :, :, odd]

        def duo(b):
            return ps[:, b, :].rearrange("p (t s) -> p t s", t=2)

        s_w = [sem(f"pair_landed{i}") for i in range(SLOTS)]
        s_m = [sem(f"mod_block_landed{i}") for i in range(2)]
        s_first = [sem(f"first_mod_blocks_landed{i}") for i in range(8)]
        s_pr, s_x = sem("parameters_landed"), sem("x_landed")
        s_par, s_sw, s_v12 = sem("constants_landed"), sem("small_weights_landed"), sem("value_lora_landed")
        s_out = sem("output_written")
        pair_done = sem("pair_done")
        bank_free = [sem(f"bank_free{i}") for i in range(4)]
        pre_act, pre_dve = sem("preamble_act"), sem("preamble_dve")
        bd_zero = sem("block_diagonals_zeroed")
        mod_used, mod_mm, mod_ready = sem("mod_block_used"), sem("mod_summed"), sem("mod_ready")
        x_sq, x_ss, x_rt = sem("x_squared"), sem("x_summed"), sem("x_rooted")
        h_pre, h_ready = sem("h_scaled"), sem("h_ready")
        step = sem("dve_step")
        astep = sem("act_step")
        lora_z, lora_t, lora_mm, lora_act = sem("lora_shifted"), sem("lora_activated"), sem("lora_products"), sem("lora_read")
        zv_up, zv_ready, vf_moved, v_ready = sem("value_lora_up"), sem("value_lora_shifted"), sem("v_first_moved"), sem("v_ready")
        kk_raw, kk_sq, kk_mm, kk_rt = sem("kk_raw"), sem("kk_squared"), sem("kk_summed"), sem("kk_rooted")
        kk_used = sem("kk_root_used")
        rk_ready, bon_mm, bon_ready = sem("bonus_terms"), sem("bonus_summed"), sem("bonus_ready")
        cc_ready, cm_ready, exps = sem("log_decay_ready"), sem("log_decay_before_ready"), sem("decay_exps")
        feat = sem("rwkv_operands_ready")
        xc_ready, lr_mm, lr_act = sem("lru_conv_ready"), sem("lru_gates_summed"), sem("lru_gates_ready")
        la_ready, la_act, lq_ready, lq_rt = sem("lru_log_a"), sem("lru_exps"), sem("lru_var"), sem("lru_root")
        ya_ready = sem("ya_ready")
        rot_mm, rope_mul, qk_ready = sem("rotated"), sem("rotated_read"), sem("qk_ready")
        avt_mm, avt_ev = sem("v_turned"), sem("v_by_position")
        sc_mm, sc_read, mx_ready, p_exp, p_ready = (sem("scores_summed"), sem("scores_read"), sem("maxima_ready"),
                                                    sem("weights_exp"), sem("weights_ready"))
        pt_mm, pt_ev, ao_mm, ao_sq, as_mm, as_rt, yb_ready = (
            sem("weights_turned"), sem("weights_turned_read"), sem("heads_summed"), sem("heads_squared"),
            sem("head_squares_summed"), sem("head_roots"), sem("yb_ready"))
        tk_mm, tk_ev = sem("operands_turned"), sem("operands_by_position")
        t_mm, t_ev, t_init, w1_mm, w1_ev = (sem("solve_products"), sem("solve_read"), sem("solve_begun"),
                                            sem("akv_summed"), sem("akv_ready"))
        zy_mm, zy_ev, rb_mm, rb_ev = sem("zy_summed"), sem("zy_ready"), sem("read_products"), sem("read_ready")
        gm_ready = sem("state_factors_ready")
        u_mm, u_ready, s_mm, st_ready, o_mm, o_ev = (sem("u_summed"), sem("u_ready"), sem("state_summed"),
                                                     sem("state_ready"), sem("out_summed"), sem("out_ready"))
        gn_mm, gn_c, gn_sq, gn_rt, yc_ready = (sem("norm_summed"), sem("centred"), sem("centred_squared"),
                                               sem("norm_rooted"), sem("yc_ready"))
        oh_ready, ol_ready, mh_ready, ml_ready = (sem("out_weights_high"), sem("out_weights_low"), sem("merged_high"),
                                                  sem("merged_low"))
        i_ready = sem("identities_ready")
        gn_inv = sem("norm_inverse_root")
        mg_ready, merged = sem("two_branches_merged"), sem("merged_ready")
        cv_step = sem("first_taps_done")
        u_begun, cv_done, gl_done, g_ready = sem("conv_begun"), sem("conv_done"), sem("gelu_done"), sem("hidden_split")
        hi_ready, lo_ready, half_done = sem("weights_high_ready"), sem("weights_low_ready"), sem("half_pair_done")
        hh_ready, hl_ready, g_prod, gh_ready = (sem("input_high_ready"), sem("input_low_ready"), sem("hidden_multiplied"),
                                                sem("hidden_high_ready"))

        n_step, n_astep = [0], [0]

        def tick(n):
            n[0] += 1
            return 1

        block = ctx.enter_context(nc.Block())

        @block.sync
        def _(sp):
            sp.dma_start(PR[:, :, :], params).then_inc(s_pr, 16)
            for g in range(8):
                sp.dma_start(first_blocks(g), wmod[2 * g:2 * g + 2].rearrange("n p d -> p n d")).then_inc(s_first[g], 16)
                if g == 1:
                    sp.dma_start(X[:, :, :], x_t).then_inc(s_x, 16)
            sp.dma_start(C[:, :], consts).then_inc(s_par, 16)
            sp.dma_start(E[:, 0:2, :].rearrange("p a b -> p (a b)"), lqk.partition_broadcast(P)).then_inc(s_par, 16)
            sp.dma_start(YA[:, 0, :].bitcast(I32), positions.partition_broadcast(P)).then_inc(s_par, 16)

            def pair(g):
                if g >= PAIRS and g < PAIRS + SLOTS:
                    sp.wait_ge(lo_ready, 2 * (g - UP - SLOTS + 1))
                elif g >= SLOTS:
                    sp.wait_ge(pair_done, g - SLOTS + 1)
                sp.dma_start(ring[:, g % SLOTS, :], wmain[g]).then_inc(s_w[g % SLOTS], 16)

            for l in range(L):
                for g in range(PAIRS * l, PAIRS * l + 4):
                    pair(g)
                if l:
                    sp.wait_ge(lr_mm, 4 * l)
                else:
                    sp.wait_ge(bd_zero, 1)
                sp.dma_start(SW[:, WL:WL + 1024], small[l, :, 0:1024]).then_inc(s_sw, 16)
                for i in range(2):
                    for par in range(2):
                        at = WA + W * i
                        sp.dma_start(SW[64 * par:64 * par + 64, at:at + W].rearrange("p (j m) -> p j m", j=4)
                                     [:, :, 64 * par:64 * par + 64],
                                     small[l, 64 * par:64 * par + 64, 1024 + 256 * i:1280 + 256 * i]
                                     .rearrange("p (j m) -> p j m", j=4)).then_inc(s_sw, 16)
                if l:
                    sp.wait_ge(pair_done, PAIRS * l)
                    sp.dma_start(V1, v1v2[:, 0:256].rearrange("p (k m) -> p k m", k=KT)).then_inc(s_v12, 16)
                    sp.dma_start(V2[0:32, :], v1v2[0:32, 256:768]).then_inc(s_v12, 16)
                for k in range(4, UP + 4):
                    pair(PAIRS * l + k)
                with sp.Fori(1, (PAIRS - UP) // 4) as i:
                    for q in range(4):
                        g0 = PAIRS * l + UP + q
                        sp.wait_ge(lo_ready, i * 8 + (2 * (MLP * l + q) - 6))
                        sp.dma_start(ring[:, g0 % SLOTS, :], wmain[i * 4 + g0]).then_inc(s_w[g0 % SLOTS], 16)
            sp.wait_ge(h_pre, 8 * 5)
            sp.dma_start(y_t, H[:, :, :]).then_inc(s_out, 16)
            sp.wait_ge(s_out, 16)

        @block.gpsimd
        def _(pool):
            pool.memset(SW[:, WA:WA + 2 * W], 0.0).then_inc(bd_zero, 1)
            pool.memset(sm[:, ONE1:ONE1 + 1], 1.0).then_inc(bd_zero, 1)
            pool.memset(sm[:, EPS6:EPS6 + 1], 1e-6).then_inc(bd_zero, 1)
            pool.memset(sm[:, EPS5:EPS5 + 1], 1e-5).then_inc(bd_zero, 1)
            pool.memset(sm[:, EPSG:EPSG + 1], 64e-5).then_inc(bd_zero, 1)
            pool.memset(ones[:, :], 1.0).then_inc(bd_zero, 1)

            def mod_blocks(a, b):
                for n in range(a, b):
                    if n >= FIRST + 2:
                        pool.wait_ge(mod_used, n - 1)
                    pool.dma_start(mring[:, n % 2, :], wmod[n]).then_inc(s_m[n % 2], 16)

            for l in range(L):
                m0 = FIRST + 48 * l
                mod_blocks(m0 + 2 * l, m0 + 18)
                mod_blocks(m0 + 18, m0 + 32)
                pool.wait_ge(zy_ev, 4 * (l + 1))
                pool.wait_ge(yb_ready, 2 * (l + 1))
                for c in range(3):
                    gf = sm[:, GF:GF + 12].rearrange("p (j c) -> p j c", c=3)[:, :, c]
                    pool.tensor_tensor(GM[c], along(gf, P), over(mat(BLOCKS), 4), ALU.mult).then_inc(gm_ready, 1)
                for n in range(4):
                    m = 2 * (n % 4)
                    br = 1 + n // 4
                    g = PAIRS * l + MERGE + 2 + n // 2
                    b = banks_of(g)[n % 2]
                    pool.wait_ge(bank_free[b], EMPTIED[g][b] + 1)
                    pool.tensor_tensor(G[:, m:m + 2, :], G[:, m:m + 2, :], G[:, 8 * br + m:8 * br + m + 2, :],
                                       ALU.add).then_inc(mg_ready, 1)
                if l == 0:
                    mod_blocks(48, 66)

        @block.scalar
        def _(act):
            A = nc.scalar.activation
            act.wait_ge(s_pr, 16)
            act.wait_ge(bd_zero, 6)
            A(sm[:, CSIL:CSIL + 8], PR[:, 0, COL["cc"]:COL["cc"] + 8], ACT.Tanh, scale=0.5).then_inc(pre_act, 1)
            def squares(n):
                for m in range(KT):
                    if n:
                        g = PAIRS * ((n - 1) // 2) + (OU if n % 2 else PAIRS - 4) + m // 2
                        act.wait_ge(bank_free[g % 4], EMPTIED[g][g % 4] + 1)
                    if m == 0 and n:
                        act.wait_ge(pair_done, PAIRS * ((n - 1) // 2) + (OU + 4 if n % 2 else PAIRS))
                    elif m == 0:
                        act.wait_ge(s_x, 16)
                    A(H[:, m, :], X[:, m, :], ACT.Square).then_inc(x_sq, 1)
                act.wait_ge(x_ss, n + 1)
                A(RT[:, :], ps[:, 4, 0:S], ACT.Ln, bias=sm[:, EPS6:EPS6 + 1], scale=1.0 / D).then_inc(astep, tick(n_astep))
                act.wait_ge(astep, n_astep[0])
                A(RT[:, :], RT[:, :], ACT.Exp, scale=-0.5).then_inc(x_rt, 1)

            def shifts(n, u):
                for m in range(KT):
                    act.wait_ge(h_pre, 8 * n + m + 1)
                    if m == 0:
                        act.wait_ge(mod_ready, u + 1)
                    if n % 2:
                        if m == 0:
                            act.wait_ge(pair_done, PAIRS * (n // 2) + OU)
                        A(HH[:, m, :], H[:, m, :], ACT.Identity, bias=mod[:, u, m:m + 1]).then_inc(hh_ready, 1)
                    A(H[:, m, :], H[:, m, :], ACT.Identity, bias=mod[:, u, m:m + 1]).then_inc(h_ready, 1)

            def evac(l, k, out, func=ACT.Identity, scale=1.0):
                g = PAIRS * l + k
                act.wait_ge(pair_done, g + 1)
                return A(out, duo(g % 4), func, scale=scale).then_inc(bank_free[g % 4], 1)

            for l in range(L):
                squares(2 * l)
                shifts(2 * l, 1 if l == 0 else 7)
                if l == 0:
                    act.wait_ge(pre_dve, 3)
                    A(sm[:, 24:28], sm[:, 24:28], ACT.Exp).then_inc(pre_act, 1)
                    A(sm[:, 40:48], sm[:, 40:48], ACT.Exp, scale=-1.0).then_inc(pre_act, 1)
                    act.wait_ge(pre_act, 3)
                    A(sm[:, 48:56], sm[:, 40:48], ACT.Ln, bias=sm[:, ONE1:ONE1 + 1]).then_inc(pre_act, 1)
                    act.wait_ge(pre_dve, 5)
                    A(SIN[:, :], RT[:, :], ACT.Sin).then_inc(pre_act, 1)
                    A(COS[:, :], YA[:, 1, :], ACT.Sin).then_inc(pre_act, 1)
                for k in range(0, 3):
                    evac(l, k, G[:, 2 * k:2 * k + 2, :])
                act.wait_ge(lora_z, 2 * l + 2)
                A(YA[0:64, 0, :], YA[0:64, 0, :], ACT.Tanh).then_inc(lora_t, 1)
                A(YA[:, 1, :], YA[:, 1, :], ACT.Tanh, scale=0.5).then_inc(lora_t, 1)
                act.wait_ge(lora_t, 3 * l + 2)
                A(YA[:, 1, :], YA[:, 1, :], ACT.Copy, scale=0.5, bias=0.5).then_inc(lora_t, 1)
                evac(l, 3, G[:, 6:8, :])
                base = 10 * l
                for i, (dst, h) in enumerate(((LD, 0), (AB, 4))):
                    act.wait_ge(lora_mm, 3 * l + i + 1)
                    for j in range(4):
                        A(dst[:, j, :], duo(4 + 2 * i + j // 2)[:, j % 2, :], ACT.Tanh, scale=0.5,
                          bias=PH[:, l, h + j:h + j + 1]).then_inc(lora_act, 1)
                evac(l, 4, G[:, 8:10, :])
                evac(l, 5, G[:, 10:12, :])
                act.wait_ge(lora_mm, 3 * l + 3)
                for b in range(2):
                    A(GG[:, 2 * b:2 * b + 2, :], duo(4 + b), ACT.Copy).then_inc(lora_act, 1)
                evac(l, 6, G[:, 12:14, :])
                if l:
                    act.wait_ge(zv_up, 1)
                    A(RT[0:32, :], ps[0:32, 6, 0:S], ACT.Copy).then_inc(zv_up, 1)
                    act.wait_ge(zv_up, 3)
                    for j in range(4):
                        A(E[:, j, :], duo(6 + j // 2)[:, j % 2, :], ACT.Tanh, scale=0.5,
                          bias=PH[:, l, 8 + j:9 + j]).then_inc(zv_up, 1)
                for k in (LR, LR + 1):
                    evac(l, k, ZX[:, 2 * (k - LR):2 * (k - LR) + 2, :])
                act.wait_ge(kk_raw, 4 * l + 4)
                if l:
                    act.wait_ge(v_ready, 2)
                A(E[:, :, :], KK[:, :, :], ACT.Square).then_inc(kk_sq, 1)
                act.wait_ge(kk_mm, l + 1)
                for b in range(2):
                    A(E[:, 2 * b:2 * b + 2, :], duo(4 + b), ACT.Sqrt).then_inc(kk_rt, 1)
                for k in (LR + 2, LR + 3):
                    if k == LR + 2:
                        act.wait_ge(lora_mm, 3 * l + 3)
                    evac(l, k, YA[:, 2 * (k - LR) - 4:2 * (k - LR) - 2, :], ACT.Gelu_apprx_tanh)
                act.wait_ge(cc_ready, l + 1)
                act.wait_ge(kk_used, l + 1)
                A(sm[:, GF:GF + 12], sm[:, GF:GF + 12], ACT.Exp).then_inc(exps, 1)
                A(E[:, :, :], CUM, ACT.Exp).then_inc(exps, 1)
                A(LRI, CUM, ACT.Exp, scale=-1.0).then_inc(exps, 1)
                act.wait_ge(cm_ready, l + 1)
                A(LRA, LRA, ACT.Exp).then_inc(exps, 1)
                for k in range(AT, AT + 6):
                    if l and k == AT:
                        act.wait_ge(v_ready, 2)
                    g = PAIRS * l + k
                    act.wait_ge(pair_done, g + 1)
                    A(R[:, 2 * (k - AT):2 * (k - AT) + 2, :], duo(g % 4), ACT.Identity).then_inc(bank_free[g % 4], 1)
                act.wait_ge(feat, 4 * (l + 1))
                for i in range(2):
                    for j in range(4):
                        act.wait_ge(lr_mm, 4 * l + 2 * i + j // 2 + 1)
                        A((LRA if i == 0 else LRI)[:, j, :], duo((4 if i == 0 else 6) + j // 2)[:, j % 2, :], ACT.Tanh, scale=0.5,
                          bias=PH[:, l, 12 + 4 * i + j:13 + 4 * i + j]).then_inc(lr_act, 1)
                for t in range(2):
                    act.wait_ge(avt_mm, 2 * l + t + 1)
                    A(AVT[:, t, :], ps[:, 4 + t, :], ACT.Copy).then_inc(avt_ev, 1)
                gates_out = [0]

                def gates(point):
                    done = int(FILLED[point]) if point < len(FILL) else GATES
                    while gates_out[0] < done:
                        k = gates_out[0]
                        g = PAIRS * l + GA + k
                        act.wait_ge(pair_done, g + 1)
                        if k == 0:
                            act.wait_ge(feat, 4 * (l + 1))
                        A(G[:, 2 * k:2 * k + 2, :], duo(g % 4), ACT.Tanh, scale=0.5).then_inc(bank_free[g % 4], 1)
                        gates_out[0] += 1

                gates(0)
                act.wait_ge(la_ready, 4 * (l + 1))
                A(E[:, :, :], LRA, ACT.Exp).then_inc(la_act, 1)
                A(ZX, LRA, ACT.Tanh).then_inc(la_act, 1)
                gates(1)
                act.wait_ge(lq_ready, l + 1)
                A(LRA, LRA, ACT.Sqrt, scale=-1.0).then_inc(lq_rt, 1)
                for tt in range(2):
                    act.wait_ge(mx_ready, 2 * l + tt + 1)
                    sc = S0 if tt == 0 else S1
                    for c in range(2):
                        for h in range(4):
                            A(sc[:, c, h, :], sc[:, c, h, :], ACT.Exp, scale=0.125, bias=sm[:, MX + 4 * c + h:MX + 4 * c + h + 1],
                              accum_out=sm[:, LSUM + 4 * c + h:LSUM + 4 * c + h + 1]).then_inc(p_exp, 1)
                    gates(2 + tt)
                gates(4)
                for n, (kt, qt) in enumerate(((0, 0), (0, 1), (1, 1))):
                    act.wait_ge(pt_mm, 3 * l + n + 1)
                    A(PT[:, kt, :, qt * P:(qt + 1) * P], quad(4 + n), ACT.Copy).then_inc(pt_ev, 1)
                gates(5)
                for n, b in enumerate((7, 4)):
                    act.wait_ge(ao_mm, 2 * l + n + 1)
                    A(E[:, 2 * n:2 * n + 2, :], duo(b), ACT.Square).then_inc(ao_sq, 1)
                for n in range(2):
                    act.wait_ge(as_mm, 2 * l + n + 1)
                    A(E[:, 2 * n:2 * n + 2, :], duo(5 + n), ACT.Ln, scale=1.0 / P, bias=sm[:, EPS5:EPS5 + 1]).then_inc(astep, tick(n_astep))
                for n in range(2):
                    act.wait_ge(astep, n_astep[0] - 1 + n)
                    A(E[:, 2 * n:2 * n + 2, :], E[:, 2 * n:2 * n + 2, :], ACT.Exp, scale=-0.5).then_inc(as_rt, 1)
                A(TTm.rearrange("p g j s -> p (g j) s"), over(mat(IDENT), 16), ACT.Copy).then_inc(i_ready, 1)
                A(Tm.rearrange("p g j s -> p (g j) s"), over(mat(IDENT), 8), ACT.Copy).then_inc(i_ready, 1)
                gates(6)
                for n in range(8):
                    act.wait_ge(tk_mm, 8 * l + n + 1)
                    if n == 0:
                        act.wait_ge(ya_ready, 4 * (l + 1))
                        act.wait_ge(pt_mm, 3 * (l + 1))
                    A(tok(n // 2)[:, n % 2, :], ps[:, 4 + n % 4, :], ACT.Copy).then_inc(tk_ev, 1)
                gates(7)
                for tt in range(2):
                    if tt:
                        act.wait_ge(t_mm, NSTEP * (2 * l + 1))
                        A(Tm.rearrange("p g j s -> p (g j) s"), over(mat(IDENT), 8), ACT.Copy).then_inc(i_ready, 1)
                    act.wait_ge(w1_mm, 2 * l + tt + 1)
                    A(WY[:, tt, :], ps[:, 6, :], ACT.Copy).then_inc(w1_ev, 1)
                    for v in range(5):
                        gates(8 + 5 * tt + v)
                for n in range(4):
                    act.wait_ge(zy_mm, 4 * l + n + 1)
                    if n < 2:
                        A(KK[:, :, n * P:(n + 1) * P], quad(4 + n), ACT.Copy).then_inc(zy_ev, 1)
                    else:
                        A(WY[:, n - 2, :], ps[:, 4 + n, :], ACT.Copy).then_inc(zy_ev, 1)
                gates(99)
                for tt in range(2):
                    act.wait_ge(o_mm, 2 * l + tt + 1)
                    A(AB[:, :, tt * P:(tt + 1) * P], quad(6 + tt), ACT.Copy).then_inc(o_ev, 1)
                act.wait_ge(gn_c, 2 * l + 2)
                A(E[:, :, :], AB[:, :, :], ACT.Square).then_inc(gn_sq, 1)
                for b in range(2):
                    act.wait_ge(gn_mm, 4 * l + 3 + b)
                    A(E[:, 2 * b:2 * b + 2, :], duo(6 + b), ACT.Ln, scale=1.0 / 64, bias=sm[:, EPSG:EPSG + 1]).then_inc(gn_rt, 1)
                for b in range(2):
                    act.wait_ge(gn_rt, 2 * l + 1 + b)
                    A(E[:, 2 * b:2 * b + 2, :], E[:, 2 * b:2 * b + 2, :], ACT.Exp, scale=-0.5).then_inc(gn_inv, 1)
                def out_high(j):
                    g = PAIRS * l + OU + j
                    act.wait_ge(s_w[g % 4], 16 * (g // 4 + 1))
                    if j >= 2:
                        act.wait_ge(pair_done, g - 1)
                    A(OWH[:, j % 2, :], ring[:, g % 4, :], ACT.Copy).then_inc(oh_ready, 1)

                out_high(0)
                out_high(1)
                for k in range(4):
                    act.wait_ge(merged, 4 * l + k + 1)
                    A(MH[:, 2 * k:2 * k + 2, :], G[:, 2 * k:2 * k + 2, :], ACT.Copy).then_inc(mh_ready, 1)
                out_high(2)
                out_high(3)
                g0 = PAIRS * l + UP

                def high(i, n, early=False):
                    b = (g0 + n) % 4
                    act.wait_ge(s_w[b], i * 16 + 16 * ((g0 + n) // 4 + 1))
                    for h in range(2):
                        part = slice(h * D, h * D + D)
                        if early:
                            act.wait_ge(pair_done, PAIRS * l + OU)
                        elif h == 0:
                            act.wait_ge(half_done, i * 4 + (MLP * l + n - 1))
                        else:
                            act.wait_ge(pair_done, i * 4 + (g0 + n - 1))
                        A(WH[:, n % 2, part], ring[:, b, part], ACT.Copy).then_inc(hi_ready, 1)

                high(0, 0, True)
                high(0, 1, True)
                squares(2 * l + 1)
                shifts(2 * l + 1, 3 if l == 0 else 9)

                def begin(i, q, first=False):
                    b = (g0 + q) % 4
                    act.wait_ge(pair_done, i * 4 + (g0 + q + 1))
                    if not (first and q < 2):
                        act.wait_ge(g_prod, i * 4 + (FT * l + q - 1))
                    for t in range(2):
                        j = i * 4 + (q + FT * t)
                        A(UB[:, q % 2, t, :], duo(b)[:, t, :], ACT.Identity, scale=PR[:, l, bass.ds(j + (COL["fw"] + 96), 1)],
                          bias=PR[:, l, bass.ds(j + COL["fb"], 1)]).then_inc(u_begun, 1)

                def gelu(i, q):
                    act.wait_ge(cv_done, i * 4 + (FT * l + q + 1))
                    A(UB[:, q % 2, 0, :], UB[:, q % 2, 0, :], ACT.Gelu_apprx_tanh).then_inc(gl_done, 1)

                def hidden_high(i, q):
                    act.wait_ge(g_prod, i * 4 + (FT * l + q + 1))
                    A(GH[:, bass.ds(i * 4 + q, 1), :], TP[:, q % 2:q % 2 + 1, :], ACT.Copy).then_inc(gh_ready, 1)

                def act_tile(i, q, first=False):
                    high(i, q + 2)
                    begin(i, q, first)
                    if not (first and q < 1):
                        gelu(i, q - 1)
                    if not (first and q < 2):
                        hidden_high(i, q - 2)

                for q in range(4):
                    act_tile(0, q, True)
                with act.Fori(1, FT // 4) as i:
                    for q in range(4):
                        act_tile(i, q)
                gelu(0, FT - 1)
                hidden_high(0, FT - 2)
                hidden_high(0, FT - 1)
                with act.Fori(FT // 4, MLP // 4 - 1) as i:
                    for q in range(4):
                        high(i, q + 2)
                high(0, MLP - 2)
                high(0, MLP - 1)
            squares(4)

        @block.vector
        def _(dve):
            V = nc.vector

            def after():
                dve.wait_ge(step, n_step[0])

            dve.wait_ge(s_pr, 16)
            dve.wait_ge(bd_zero, 6)
            dve.wait_ge(pre_act, 1)
            V.scalar_tensor_tensor(sm[:, CSIL:CSIL + 8], sm[:, CSIL:CSIL + 8], 1.0, PR[:, 0, COL["cc"]:COL["cc"] + 8],
                                   ALU.add, ALU.mult).then_inc(step, tick(n_step))
            after()
            V.tensor_scalar(sm[:, CSIL:CSIL + 8], sm[:, CSIL:CSIL + 8], 0.5, None, ALU.mult).then_inc(step, tick(n_step))
            after()

            def derived():
                dve.wait_ge(s_par, 48)
                for n in range(L):
                    V.tensor_scalar(PH[:, n, :], PR[:, n, COL["w0"]:COL["w0"] + 20], 0.5, None, ALU.mult).then_inc(step, tick(n_step))
                lq = E[:, 0:2, :].rearrange("p a b -> p (a b)").rearrange("p (n two d) -> p n two d", n=4, two=2)
                V.tensor_tensor(E[:, 2, :].rearrange("p (n d) -> p n d", n=4), lq[:, :, 0, :], lq[:, :, 1, :], ALU.mult).then_inc(step, tick(n_step))
                after()
                V.reduce_sum(sm[:, 24:28], E[:, 2, :].rearrange("p (n d) -> p n d", n=4), AX_X).then_inc(pre_dve, 1)
                for n in range(L):
                    lam = col(n, "lam", 0, 4)
                    V.scalar_tensor_tensor(sm[:, 40 + 4 * n:44 + 4 * n], lam, -1.0, lam, ALU.mult, ALU.max).then_inc(pre_dve, 1)
                ang, k1, red = YA[:, 2, :], YA[:, 3, :], RT[:, :]
                V.tensor_copy(YA[:, 1, :], YA[:, 0, :].bitcast(I32)).then_inc(step, tick(n_step))
                after()
                V.tensor_scalar(ang, YA[:, 1, :], C[:, FREQ:FREQ + 1], None, ALU.mult).then_inc(step, tick(n_step))
                for n, out in enumerate((red, YA[:, 1, :])):
                    after()
                    V.tensor_scalar(k1, ang, 1.0 / SQ2PI, 0.25 * n, ALU.mult, ALU.add).then_inc(step, tick(n_step))
                    after()
                    V.tensor_scalar(k1, k1, MAGIC, None, ALU.add).then_inc(step, tick(n_step))
                    after()
                    V.tensor_scalar(k1, k1, -MAGIC, None, ALU.add).then_inc(step, tick(n_step))
                    after()
                    V.scalar_tensor_tensor(out, k1, -C1, ang, ALU.mult, ALU.add).then_inc(step, tick(n_step))
                    after()
                    V.scalar_tensor_tensor(out, k1, -C2, out, ALU.mult, ALU.add).then_inc(step, tick(n_step))
                    after()
                    V.scalar_tensor_tensor(out, k1, -C3, out, ALU.mult, ALU.add).then_inc(step, tick(n_step))
                    after()
                    V.tensor_scalar(out, out, 0.5 * math.pi * n, PI_IN, ALU.add, ALU.min).then_inc(step, tick(n_step))
                    after()
                    V.tensor_scalar(out, out, -PI_IN, None, ALU.max).then_inc(pre_dve, 1)
                dve.wait_ge(pre_act, 4)
                for n in range(L):
                    lam = col(n, "lam", 0, 4)
                    V.tensor_tensor(sm[:, NLAM + n:NLAM + n + 1], sm[:, 25 + 2 * n:26 + 2 * n], sm[:, 24 + 2 * n:25 + 2 * n],
                                    ALU.subtract).then_inc(step, tick(n_step))
                    after()
                    V.tensor_scalar(sm[:, NLAM + n:NLAM + n + 1], sm[:, NLAM + n:NLAM + n + 1], -lambda_init(n), None,
                                    ALU.add).then_inc(step, tick(n_step))
                    V.tensor_scalar(sm[:, SUBG + n:SUBG + n + 1], col(n, "sub"), 1.0 - lambda_init(n), None, ALU.mult).then_inc(step, tick(n_step))
                    V.tensor_scalar(sm[:, N8 + 4 * n:N8 + 4 * n + 4], lam, -1.0, 0.0, ALU.mult, ALU.max).then_inc(step, tick(n_step))
                    after()
                    V.tensor_tensor(sm[:, N8 + 4 * n:N8 + 4 * n + 4], sm[:, N8 + 4 * n:N8 + 4 * n + 4], sm[:, 48 + 4 * n:52 + 4 * n],
                                    ALU.add).then_inc(step, tick(n_step))
                    after()
                    V.tensor_scalar(sm[:, N8 + 4 * n:N8 + 4 * n + 4], sm[:, N8 + 4 * n:N8 + 4 * n + 4], -4.0, None,
                                    ALU.mult).then_inc(step, tick(n_step))
                after()
                dve.wait_ge(pre_act, 6)

            def mod_block(n):
                u, kt = divmod(n, 8)
                if n < FIRST:
                    dve.wait_ge(s_first[n // 2], 16)
                    block = first_blocks(n // 2)[:, n % 2, :]
                else:
                    dve.wait_ge(s_m[n % 2], 16 * ((n - FIRST) // 2 + 1))
                    block = mring[:, n % 2, :]
                if kt == 0:
                    if u:
                        dve.wait_ge(mod_mm, u)
                    V.tensor_scalar(macc[:, :], block, sm[:, CSIL:CSIL + 1], None, ALU.mult).then_inc(mod_used, 1)
                else:
                    dve.wait_ge(mod_used, n)
                    V.scalar_tensor_tensor(macc[:, :], block, sm[:, CSIL + kt:CSIL + kt + 1], macc[:, :],
                                           ALU.mult, ALU.add).then_inc(mod_used, 1)

            def mod_vector(u):
                dve.wait_ge(mod_mm, u + 1)
                lay = 0 if u < 6 else 1
                V.tensor_tensor(mod[:, u, :], ps[:, 7, 0:8], col(lay, "bmod", 8 * (u % 6), 8), ALU.add).then_inc(mod_ready, 1)

            def mod_unit(u):
                for kt in range(8):
                    mod_block(8 * u + kt)
                mod_vector(u)

            mod_unit(0)
            mod_unit(1)
            beside = [FIRST]

            def mod_beside(n):
                for _ in range(n):
                    mod_block(beside[0])
                    beside[0] += 1

            def norm(n, gain, u):
                if u is None:
                    A_ = gain
                else:
                    dve.wait_ge(mod_ready, u + 1)
                    V.scalar_tensor_tensor(Acol[:, :], mod[:, u, :], 1.0, gain, ALU.add, ALU.mult).then_inc(step, tick(n_step))
                    A_ = Acol
                    after()
                dve.wait_ge(x_rt, n + 1)
                for m in range(KT):
                    V.scalar_tensor_tensor(H[:, m, :], X[:, m, :], A_[:, m:m + 1], RT[:, :], ALU.mult, ALU.mult).then_inc(h_pre, 1)

            def shift(src, dst, n, l, mu, out=None):
                V.tensor_tensor(dst[:, :, 1:S], src[:, :, 0:S - 1], src[:, :, 1:S], ALU.subtract).then_inc(step, tick(n_step))
                V.tensor_scalar(dst[:, :, 0:1], src[:, :, 0:1], -1.0, None, ALU.mult).then_inc(step, tick(n_step))
                after()
                for j in range(n):
                    i = V.scalar_tensor_tensor(dst[:, j, :], dst[:, j, :], col(l, "mu", mu + j), src[:, j, :], ALU.mult, ALU.add)
                    if out is None:
                        i.then_inc(step, tick(n_step))
                    else:
                        i.then_inc(out, 1)

            for l in range(L):
                norm(2 * l, col(l, "n1g", 0, 8), 0 if l == 0 else 6)
                if l == 0:
                    derived()
                dve.wait_ge(bank_free[(PAIRS * l) % 4], EMPTIED[PAIRS * l][(PAIRS * l) % 4] + 1)
                shift(G[:, 0:2, :], YA[:, 0:2, :], 2, l, 0, lora_z)
                mod_beside(2)
                for k in (1, 2):
                    g = PAIRS * l + k
                    dve.wait_ge(bank_free[g % 4], EMPTIED[g][g % 4] + 1)
                shift(G[:, 2:6, :], K_, 4, l, 2)
                after()
                for j in range(4):
                    V.tensor_scalar(KK[:, j, :], K_[:, j, :], col(l, "kk", j), None, ALU.mult).then_inc(kk_raw, 1)
                if l:
                    V.tensor_copy(VF, V_).then_inc(vf_moved, 1)
                mod_beside(2)
                dve.wait_ge(lora_act, 10 * l + 8)
                V.tensor_scalar(AB[:, :, :], AB[:, :, :], 0.5, 0.5, ALU.mult, ALU.add).then_inc(step, tick(n_step))
                V.tensor_scalar(LD, LD, -0.5 * EM05, -0.5 * EM05, ALU.mult, ALU.add).then_inc(step, tick(n_step))
                after()
                for j in range(4):
                    V.tensor_tensor_scan(CUM[:, j, :], C[:, RESET:RESET + S], LD[:, j, :], 0.0, ALU.mult, ALU.add).then_inc(step, tick(n_step))
                for k in (3, 4):
                    g = PAIRS * l + k
                    dve.wait_ge(bank_free[g % 4], EMPTIED[g][g % 4] + 1)
                shift(G[:, 6:10, :], R_, 4, l, 6)
                mod_beside(2)
                after()
                cum4 = CUM.rearrange("p j (c t) -> p (j c) t", t=CH)
                mids = sm[:, MIDS:MIDS + 16]
                V.tensor_copy(mids, cum4[:, :, CH // 2 - 1]).then_inc(step, tick(n_step))
                after()
                V.tensor_tensor(cum4, cum4, along(mids, CH), ALU.subtract).then_inc(step, tick(n_step))
                after()
                V.tensor_tensor(sm[:, GF:GF + 12].rearrange("p (j c) -> p j c", c=3),
                                cum4.rearrange("p (j c) t -> p j c t", c=NCH)[:, :, 0:3, CH - 1],
                                mids.rearrange("p (j c) -> p j c", c=NCH)[:, :, 1:4], ALU.add).then_inc(cc_ready, 1)
                for j in range(4):
                    V.tensor_scalar(BON[:, j, :], AB[:, j, :], -1.0, col(l, "ka", j), ALU.add, ALU.mult).then_inc(step, tick(n_step))
                after()
                V.scalar_tensor_tensor(K_, BON[:, :, :], 1.0, K_, ALU.add, ALU.mult).then_inc(step, tick(n_step))
                after()
                mod_beside(2)
                for k in (5, 6):
                    g = PAIRS * l + k
                    dve.wait_ge(bank_free[g % 4], EMPTIED[g][g % 4] + 1)
                if l:
                    dve.wait_ge(vf_moved, 1)
                shift(G[:, 10:14, :], V_, 4, l, 10)
                after()
                for j in range(4):
                    V.scalar_tensor_tensor(BON[:, j, :], R_[:, j, :], col(l, "rk", j), K_[:, j, :], ALU.mult, ALU.mult).then_inc(rk_ready, 1)
                mod_vector(6 * l + 2)
                if l:
                    dve.wait_ge(zv_up, 2)
                    zv, zd = RT[0:32, :], Acol
                    V.tensor_tensor(YB[0:32, 2, 1:S], zv[:, 0:S - 1], zv[:, 1:S], ALU.subtract).then_inc(step, tick(n_step))
                    V.tensor_scalar(YB[0:32, 2, 0:1], zv[:, 0:1], -1.0, None, ALU.mult).then_inc(step, tick(n_step))
                    after()
                    V.scalar_tensor_tensor(YB[0:32, 2, :], YB[0:32, 2, :], PR[0:32, l, COL["vmu"]:COL["vmu"] + 1], zv,
                                           ALU.mult, ALU.add).then_inc(zv_ready, 1)
                    V.tensor_tensor(VF, VF, V_, ALU.subtract).then_inc(step, tick(n_step))
                    dve.wait_ge(zv_up, 7)
                    V.tensor_scalar(E[:, :, :], E[:, :, :], 0.5, 0.5, ALU.mult, ALU.add).then_inc(step, tick(n_step))
                    after()
                    V.tensor_tensor(E[:, :, :], E[:, :, :], VF, ALU.mult).then_inc(v_ready, 1)
                    dve.wait_ge(v_ready, 1)
                    V.tensor_tensor(V_, V_, E[:, :, :], ALU.add).then_inc(v_ready, 1)
                mod_beside(2)
                dve.wait_ge(kk_rt, 2 * (l + 1))
                V.tensor_scalar(E[:, :, :], E[:, :, :], 1e-12, None, ALU.max).then_inc(step, tick(n_step))
                after()
                V.reciprocal(E[:, :, :], E[:, :, :]).then_inc(step, tick(n_step))
                after()
                V.tensor_tensor(KK[:, :, :], KK[:, :, :], E[:, :, :], ALU.mult).then_inc(kk_used, 1)
                V.tensor_tensor(LRA, CUM, LD, ALU.subtract).then_inc(cm_ready, 1)
                dve.wait_ge(kk_used, l + 1)
                V.tensor_tensor(AB[:, :, :], AB[:, :, :], KK[:, :, :], ALU.mult).then_inc(step, tick(n_step))
                if l:
                    dve.wait_ge(v_ready, 2)
                dve.wait_ge(bon_mm, l + 1)
                for b in range(2):
                    V.tensor_tensor(BON[:, 2 * b:2 * b + 2, :], duo(6 + b), V_[:, 2 * b:2 * b + 2, :], ALU.mult).then_inc(bon_ready, 1)
                dve.wait_ge(exps, 4 * l + 2)
                V.tensor_tensor(R_, R_, E[:, :, :], ALU.mult).then_inc(feat, 1)
                dve.wait_ge(exps, 4 * l + 3)
                V.tensor_tensor(K_, K_, LRI, ALU.mult).then_inc(feat, 1)
                after()
                V.tensor_tensor(AB[:, :, :], AB[:, :, :], LRI, ALU.mult).then_inc(feat, 1)
                dve.wait_ge(exps, 4 * l + 4)
                V.scalar_tensor_tensor(KK[:, :, :], KK[:, :, :], -1.0, LRA, ALU.mult, ALU.mult).then_inc(feat, 1)
                mod_beside(2)
                for k in (LR, LR + 1):
                    g = PAIRS * l + k
                    dve.wait_ge(bank_free[g % 4], EMPTIED[g][g % 4] + 1)
                for j in range(4):
                    V.tensor_scalar(XC[:, j, :], ZX[:, j, :], col(l, "cw", 12 + j), col(l, "cb", j), ALU.mult, ALU.add).then_inc(step, tick(n_step))
                for d in (1, 2, 3):
                    after()
                    for j in range(4):
                        i = V.scalar_tensor_tensor(XC[:, j, d:S], ZX[:, j, 0:S - d], col(l, "cw", 4 * (3 - d) + j), XC[:, j, d:S],
                                                   ALU.mult, ALU.add)
                        if d == 3:
                            i.then_inc(xc_ready, 1)
                        else:
                            i.then_inc(step, tick(n_step))
                for b in range(4):
                    g = PAIRS * l + AT + b
                    dve.wait_ge(bank_free[g % 4], EMPTIED[g][g % 4] + 1)
                    dve.wait_ge(rot_mm, 4 * l + b + 1)
                    tmp = R[:, 16 + 2 * b:18 + 2 * b, :]
                    qk = QK[:, 2 * b:2 * b + 2, :]
                    V.tensor_tensor(tmp, duo(4 + b), over(SIN[:, :], 2), ALU.mult).then_inc(rope_mul, 1)
                    V.tensor_tensor(qk, qk, over(COS[:, :], 2), ALU.mult).then_inc(step, tick(n_step))
                    after()
                    dve.wait_ge(rope_mul, 4 * l + b + 1)
                    V.tensor_tensor(qk, qk, tmp, ALU.add).then_inc(qk_ready, 1)
                def read_scores(tt):
                    sc = S0 if tt == 0 else S1
                    for n, (t, c, h0, nh) in enumerate(SCORES):
                        if t != tt:
                            continue
                        dve.wait_ge(sc_mm, 6 * l + n + 1)
                        b = SCORE_BANK[n]
                        if tt == 0:
                            V.tensor_tensor(sc[:, c], quad(b), over(C[:, NEG0 + P:NEG0 + 2 * P], 4), ALU.add).then_inc(sc_read, 1)
                        else:
                            V.tensor_tensor(sc[:, c, h0:h0 + 2, :], duo(b), over(C[:, NEG0:NEG0 + 2 * P], 2), ALU.add).then_inc(sc_read, 1)
                    dve.wait_ge(sc_read, 6 * l + (2 if tt == 0 else 6))
                    if tt:
                        dve.wait_ge(p_exp, 16 * l + 8)
                    V.reduce_max(sm[:, MX:MX + 8].rearrange("p (c h) -> p c h", c=2), sc, AX_X).then_inc(step, tick(n_step))
                    after()
                    V.tensor_scalar(sm[:, MX:MX + 8], sm[:, MX:MX + 8], -0.125, None, ALU.mult).then_inc(mx_ready, 1)

                def weights(tt):
                    sc = S0 if tt == 0 else S1
                    dve.wait_ge(p_exp, 16 * l + 8 * (tt + 1))
                    V.reciprocal(sm[:, LSUM:LSUM + 8], sm[:, LSUM:LSUM + 8]).then_inc(step, tick(n_step))
                    after()
                    V.tensor_scalar(sm[:, LSUM + 4:LSUM + 8], sm[:, LSUM + 4:LSUM + 8], sm[:, NLAM + l:NLAM + l + 1], None,
                                    ALU.mult).then_inc(step, tick(n_step))
                    for h in range(4):
                        V.tensor_scalar(sc[:, 0, h, :], sc[:, 0, h, :], sm[:, LSUM + h:LSUM + h + 1], None, ALU.mult).then_inc(step, tick(n_step))
                    after()
                    for h in range(4):
                        V.scalar_tensor_tensor(sc[:, 0, h, :], sc[:, 1, h, :], sm[:, LSUM + 4 + h:LSUM + 5 + h], sc[:, 0, h, :],
                                               ALU.mult, ALU.add).then_inc(p_ready, 1)

                mod_beside(2)
                read_scores(0)
                for j in range(4):
                    dve.wait_ge(lr_act, 8 * l + j + 1)
                    V.tensor_scalar(LRA[:, j, :], LRA[:, j, :], 1.0, sm[:, N8 + 4 * l + j:N8 + 4 * l + j + 1], ALU.add, ALU.mult).then_inc(la_ready, 1)
                dve.wait_ge(lr_act, 8 * (l + 1))
                dve.wait_ge(xc_ready, 4 * (l + 1))
                V.scalar_tensor_tensor(XC, LRI, 1.0, XC, ALU.add, ALU.mult).then_inc(step, tick(n_step))
                dve.wait_ge(la_act, 2 * (l + 1))
                V.tensor_tensor(LRA, E[:, :, :], E[:, :, :], ALU.mult).then_inc(step, tick(n_step))
                after()
                V.scalar_tensor_tensor(LRA, LRA, 1.0, ZX, ALU.add, ALU.mult).then_inc(lq_ready, 1)
                weights(0)
                dve.wait_ge(lq_rt, l + 1)
                V.scalar_tensor_tensor(LRI, LRA, 0.5, XC, ALU.mult, ALU.mult).then_inc(step, tick(n_step))
                after()
                for j in range(4):
                    V.tensor_tensor_scan(ZX[:, j, :], E[:, j, :], LRI[:, j, :], 0.0, ALU.mult, ALU.add).then_inc(step, tick(n_step))
                after()
                for k in (LR + 2, LR + 3):
                    g = PAIRS * l + k
                    dve.wait_ge(bank_free[g % 4], EMPTIED[g][g % 4] + 1)
                for j in range(4):
                    V.tensor_tensor(YA[:, j, :], YA[:, j, :], ZX[:, j, :], ALU.mult).then_inc(ya_ready, 1)
                read_scores(1)
                mod_beside(2)
                weights(1)
                for n, b in enumerate((7, 4)):
                    dve.wait_ge(as_rt, 2 * l + n + 1)
                    e = E[:, 2 * n:2 * n + 2, :]
                    V.scalar_tensor_tensor(YB[:, 2 * n:2 * n + 2, :], duo(b), sm[:, SUBG + l:SUBG + l + 1], e,
                                           ALU.mult, ALU.mult).then_inc(yb_ready, 1)
                mod_vector(6 * l + 3)
                def blocks_of_two(at, src, mask, odd):
                    m = every_other(mat(mask), odd).unsqueeze(1).broadcast_to([P, 4, 64])
                    return V.tensor_tensor(E[:, at, :].rearrange("p (j n) -> p j n", j=4), every_other(src, odd), m, ALU.mult)

                for tt in range(2):
                    base = NSTEP * (2 * l + tt)
                    if tt:
                        mod_vector(6 * l + 4)
                    for n, (kind, par, v, b) in enumerate(STEPS):
                        dve.wait_ge(t_mm, base + n + 1)
                        if kind == "ak":
                            V.tensor_tensor(Mm[:, par], quad(b), over(mat(M_UP), 4), ALU.mult).then_inc(t_ev, 1)
                        elif kind == "n":
                            V.tensor_tensor(Nm[:, par], quad(b), over(mat(M_LOW), 4), ALU.mult).then_inc(t_ev, 1)
                        elif kind == "nt":
                            blocks_of_two(par, quad(b), M_U1, 1).then_inc(t_ev, 1)
                            if par:
                                for p2 in range(2):
                                    dve.wait_ge(t_ev, base + step_no("n", p2, 0) + 1)
                                    blocks_of_two(2 + p2, Nm[:, p2], M_L1, 0).then_inc(step, tick(n_step))
                                dve.wait_ge(i_ready, 3 * l + 2 + tt)
                                dve.wait_ge(t_ev, base + n + 1)
                                for p2 in range(2):
                                    for at, T_, odd in ((p2, TTm[:, 2 * tt + p2], 1), (2 + p2, Tm[:, p2], 0)):
                                        if at >= 2:
                                            dve.wait_ge(step, n_step[0] - 1 + p2)
                                        V.tensor_tensor(every_other(T_, odd), every_other(T_, odd),
                                                        E[:, at, :].rearrange("p (j n) -> p j n", j=4), ALU.add).then_inc(t_init, 1)
                        elif kind == "m":
                            V.tensor_tensor(Mm[:, par], quad(b), over(mat(LEVELS[v]), 4), ALU.mult).then_inc(t_ev, 1)
                        elif kind == "x":
                            T_ = TTm[:, 2 * tt + par]
                            V.tensor_tensor(T_, T_, quad(b), ALU.add).then_inc(t_ev, 1)
                            if par == 1 and v:
                                mod_beside(2)
                        else:
                            T_ = Tm[:, par]
                            V.tensor_tensor(T_, T_, quad(b), ALU.add).then_inc(t_ev, 1)
                for n in range(8):
                    dst = (RKm if n % 2 == 0 else RBm)[:, n // 2]
                    dve.wait_ge(rb_mm, 8 * l + n + 1)
                    V.tensor_tensor(dst, quad(4 + n % 4), over(mat(M_UPI), 4), ALU.mult).then_inc(rb_ev, 1)
                for c in range(NCH):
                    tt, rows = c // 2, slice(64 * (c % 2), 64 * (c % 2) + 64)
                    if c:
                        dve.wait_ge(u_mm, 3 * l + c)
                        V.tensor_tensor(WY[rows, tt, :], ps[rows, 4, :], WY[rows, tt, :], ALU.add).then_inc(u_ready, 1)
                    if c < NCH - 1:
                        dve.wait_ge(s_mm, 3 * l + c + 1)
                        dve.wait_ge(gm_ready, 3 * l + c + 1)
                        if c == 0:
                            V.tensor_tensor(ST, quad(5), GM[c], ALU.mult).then_inc(st_ready, 1)
                        else:
                            dve.wait_ge(st_ready, 3 * l + c)
                            V.tensor_tensor(ST, ST, quad(5), ALU.add).then_inc(step, tick(n_step))
                            after()
                            V.tensor_tensor(ST, ST, GM[c], ALU.mult).then_inc(st_ready, 1)

                def gated(p):
                    br, half = p // 2, p % 2
                    g = PAIRS * l + MERGE + p
                    dve.wait_ge(pair_done, g + 1)
                    for i, b in enumerate(banks_of(g)):
                        m = 4 * half + 2 * i
                        gate = G[:, 8 * br + m:8 * br + m + 2, :]
                        V.scalar_tensor_tensor(gate, gate, 1.0, duo(b), ALU.add, ALU.mult).then_inc(bank_free[b], 1)
                    if br == 2:
                        for i, b in enumerate(banks_of(g)):
                            m = 4 * half + 2 * i
                            dve.wait_ge(mg_ready, 4 * l + m // 2 + 1)
                            dve.wait_ge(bank_free[b], EMPTIED[g][b] + 1)
                            V.tensor_tensor(G[:, m:m + 2, :], G[:, m:m + 2, :], G[:, 16 + m:18 + m, :], ALU.add).then_inc(merged, 1)

                def gates_in(a, b):
                    for k in range(a, b):
                        g = PAIRS * l + GA + k
                        dve.wait_ge(bank_free[g % 4], EMPTIED[g][g % 4] + 1)

                for b in range(2):
                    dve.wait_ge(gn_mm, 4 * l + 1 + b)
                    o = AB[:, 2 * b:2 * b + 2, :]
                    V.scalar_tensor_tensor(o, duo(4 + b), -1.0 / 64, o, ALU.mult, ALU.add).then_inc(gn_c, 1)
                gates_in(4, 8)
                gated(0)
                dve.wait_ge(gn_inv, 2 * (l + 1))
                V.tensor_tensor(AB[:, :, :], AB[:, :, :], E[:, :, :], ALU.mult).then_inc(step, tick(n_step))
                after()
                for j in range(4):
                    V.tensor_scalar(AB[:, j, :], AB[:, j, :], col(l, "lng", j), col(l, "lnb", j), ALU.mult, ALU.add).then_inc(step, tick(n_step))
                after()
                V.tensor_tensor(AB[:, :, :], AB[:, :, :], BON[:, :, :], ALU.add).then_inc(step, tick(n_step))
                after()
                V.tensor_tensor(AB[:, :, :], AB[:, :, :], GG[:, :, :], ALU.mult).then_inc(yc_ready, 1)
                for p in (1, 2, 3):
                    gated(p)
                mod_vector(6 * l + 5)
                gates_in(8, 12)
                def out_low(j):
                    dve.wait_ge(oh_ready, 4 * l + j + 1)
                    V.tensor_tensor(OWL[:, j % 2, :], ring[:, (PAIRS * l + OU + j) % 4, :], OWH[:, j % 2, :].bitcast(F32),
                                    ALU.subtract).then_inc(ol_ready, 1)

                def merged_low(k):
                    dve.wait_ge(mh_ready, 4 * l + k + 1)
                    V.tensor_tensor(ML[:, 2 * k:2 * k + 2, :], G[:, 2 * k:2 * k + 2, :],
                                    MH[:, 2 * k:2 * k + 2, :].bitcast(F32), ALU.subtract).then_inc(ml_ready, 1)

                out_low(0)
                gated(4)
                out_low(1)
                merged_low(0)
                merged_low(1)
                gated(5)
                merged_low(2)
                merged_low(3)
                u = 2 if l == 0 else 8
                dve.wait_ge(mod_ready, u + 1)
                V.tensor_scalar(sm[:, FH:FH + 8], mod[:, u, :], 0.5, None, ALU.mult).then_inc(step, tick(n_step))
                after()

                def residual(g, j, scale):
                    dve.wait_ge(pair_done, g + 1)
                    for i in range(2):
                        m = 2 * j + i
                        ins = V.scalar_tensor_tensor(X[:, m, :], duo(g % 4)[:, i, :], scale[:, m:m + 1], X[:, m, :],
                                                     ALU.mult, ALU.add)
                    ins.then_inc(bank_free[g % 4], 1)

                g0 = PAIRS * l + UP

                def low(i, n):
                    b = (g0 + n) % 4
                    for h in range(2):
                        part = slice(h * D, h * D + D)
                        dve.wait_ge(hi_ready, i * 8 + (2 * (MLP * l + n) + h + 1))
                        V.tensor_tensor(WLO[:, n % 2, part], ring[:, b, part], WH[:, n % 2, part].bitcast(F32),
                                        ALU.subtract).then_inc(lo_ready, 1)

                for j in range(4):
                    if j < 2:
                        out_low(j + 2)
                    else:
                        low(0, j - 2)
                    residual(PAIRS * l + OU + j, j, sm[:, FH:FH + 8])
                norm(2 * l + 1, col(l, "n2g", 0, 8), 4 if l == 0 else 10)
                for m in range(KT):
                    dve.wait_ge(hh_ready, KT * l + m + 1)
                    dve.wait_ge(h_ready, KT * (2 * l + 1) + m + 1)
                    V.tensor_tensor(HL[:, m, :], H[:, m, :], HH[:, m, :].bitcast(F32), ALU.subtract).then_inc(hl_ready, 1)
                def conv_read(i, q):
                    if q < 0:
                        return i + EMPTIED[g0 + q + 4][(g0 + q) % 4]
                    return i + (EMPTIED[g0 + q][(g0 + q) % 4] + 1)

                def taps(i, q):
                    b = (g0 + q) % 4
                    for d in (1, 2):
                        for t in range(2):
                            j = i * 4 + (q + FT * t)
                            dve.wait_ge(u_begun if d == 1 else cv_step, i * 8 + (2 * (FT * l + q) + (2 if d == 1 else 1 + t)))
                            ins = V.scalar_tensor_tensor(UB[:, q % 2, t, d:S], duo(b)[:, t, 0:S - d],
                                                         PR[:, l, bass.ds(j + (COL["fw"] + 48 * (2 - d)), 1)], UB[:, q % 2, t, d:S],
                                                         ALU.mult, ALU.add)
                            ins.then_inc(cv_step if d == 1 else (cv_done, bank_free[b])[t], 1)

                def product(i, q):
                    dve.wait_ge(gl_done, i * 4 + (FT * l + q + 1))
                    dve.wait_ge(bank_free[(g0 + q) % 4], conv_read(i, q))
                    V.tensor_tensor(TP[:, q % 2, :], UB[:, q % 2, 0, :], UB[:, q % 2, 1, :], ALU.mult).then_inc(g_prod, 1)

                def hidden_low(i, q):
                    dve.wait_ge(gh_ready, i * 4 + (FT * l + q + 1))
                    V.tensor_tensor(GL[:, bass.ds(i * 4 + q, 1), :], TP[:, q % 2:q % 2 + 1, :],
                                    GH[:, bass.ds(i * 4 + q, 1), :].bitcast(F32), ALU.subtract).then_inc(g_ready, 1)

                def up_tile(i, q, first=False):
                    low(i, q + 2)
                    taps(i, q)
                    if not (first and q < 2):
                        hidden_low(i, q - 2)
                    if not (first and q < 1):
                        product(i, q - 1)

                for q in range(4):
                    up_tile(0, q, True)
                with dve.Fori(1, FT // 4) as i:
                    for q in range(4):
                        up_tile(i, q)
                hidden_low(0, FT - 2)
                product(0, FT - 1)
                hidden_low(0, FT - 1)
                for n in range(MLP - FT):
                    if FT + n + 2 < MLP:
                        low(0, FT + n + 2)
                    if l == 0:
                        if n == DN_SUM:
                            mod_vector(6)
                        mod_beside(DN_BLOCKS[n])
                u = 5 if l == 0 else 11
                dve.wait_ge(mod_ready, u + 1)
                g1 = PAIRS * l + PAIRS - 4
                for j in range(4):
                    residual(g1 + j, j, mod[:, u, :])
                if l == 0:
                    mod_vector(7)
            norm(4, col(0, "fg", 0, 8), None)

        @block.tensor
        def _(pe):
            MM = nc.tensor.matmul

            def mod_sum(u):
                pe.wait_ge(mod_used, 8 * (u + 1))
                if u:
                    pe.wait_ge(mod_ready, u)
                for j in range(KT):
                    i = MM(ps[:, 7, j:j + 1], macc[:, j * P:(j + 1) * P], sm[:, ONE1:ONE1 + 1], start=True, stop=True)
                i.then_inc(mod_mm, 1)

            def ones_sum(n):
                for m in range(KT):
                    pe.wait_ge(x_sq, 8 * n + m + 1)
                    i = MM(ps[:, 4, 0:S], ones[:, :], H[:, m, :], start=(m == 0), stop=(m == KT - 1))
                i.then_inc(x_ss, 1)

            def landed(g):
                pe.wait_ge(s_w[g % 4], 16 * (g // 4 + 1))

            def emptied(g, b):
                if EMPTIED[g][b]:
                    pe.wait_ge(bank_free[b], EMPTIED[g][b])

            def w_of(g, m, k, n=KT):
                return ring[:, g % 4, (m * n + k) * P:(m * n + k + 1) * P]

            def passes(out, w_high, w_low, n, high, low, start, stop):
                at = slice(n * P, (n + 1) * P)
                MM(out, w_high[:, at], high, start=start, stop=False, skip_group_check=True)
                MM(out, w_high[:, at], low, start=False, stop=False, skip_group_check=True)
                return MM(out, w_low[:, at], high, start=False, stop=stop, skip_group_check=True)

            def product(l, k, rhs, wait_h=None):
                g = PAIRS * l + k
                landed(g)
                emptied(g, g % 4)
                for m in range(2):
                    for i in range(KT):
                        if wait_h is not None and m == 0:
                            pe.wait_ge(h_ready, wait_h + i + 1)
                        last = MM(ps[:, g % 4, m * S:(m + 1) * S], w_of(g, m, i), rhs[:, i, :], start=(i == 0), stop=(i == KT - 1))
                last.then_inc(pair_done, 1)

            pe.wait_ge(bd_zero, 6)
            for l in range(L):
                ones_sum(2 * l)
                if l == 0:
                    mod_sum(0)
                    mod_sum(1)
                product(l, 0, H, wait_h=16 * l)
                for k in range(1, 4):
                    product(l, k, H)
                pe.wait_ge(s_par, 48)
                pe.wait_ge(s_sw, 80 * (l + 1))
                pe.wait_ge(lora_t, 3 * l + 3)
                pe.wait_ge(x_rt, 2 * l + 1)
                pe.wait_ge(mod_ready, 6 * l + 2)
                for i in range(2):
                    rows = slice(64 * i, 64 * i + 64)
                    for j in range(4):
                        last = MM(duo(4 + 2 * i + j // 2)[:, j % 2, :], SW[rows, WL + j * P:WL + (j + 1) * P], YA[rows, 0, :],
                                  start=True, stop=True)
                    last.then_inc(lora_mm, 1)
                product(l, 4, H)
                product(l, 5, H)
                pe.wait_ge(lora_act, 10 * l + 4)
                for j in range(4):
                    last = MM(duo(4 + j // 2)[:, j % 2, :], SW[:, WG + j * P:WG + (j + 1) * P], YA[:, 1, :], start=True, stop=True)
                last.then_inc(lora_mm, 1)
                product(l, 6, H)
                pe.wait_ge(lora_act, 10 * l + 8)
                mod_sum(6 * l + 2)
                if l:
                    pe.wait_ge(s_v12, 32)
                    pe.wait_ge(lora_act, 10 * l + 8)
                    for i in range(KT):
                        last = MM(ps[0:32, 6, 0:S], V1[:, i, :], H[:, i, :], start=(i == 0), stop=(i == KT - 1))
                    last.then_inc(zv_up, 1)
                    product(l, LR, H)
                    pe.wait_ge(zv_ready, 1)
                    pe.wait_ge(mod_ready, 9)
                    for j in range(4):
                        last = MM(duo(6 + j // 2)[:, j % 2, :], V2[0:32, j * P:(j + 1) * P], YB[0:32, 2, :], start=True, stop=True)
                    last.then_inc(zv_up, 1)
                    product(l, LR + 1, H)
                else:
                    product(l, LR, H)
                    product(l, LR + 1, H)
                pe.wait_ge(kk_sq, l + 1)
                pe.wait_ge(lora_act, 10 * l + 10)
                for b in range(2):
                    last = MM(ps[:, 4 + b, :], mat(BLOCKS), E[:, 2 * b:2 * b + 2, :], start=True, stop=True)
                last.then_inc(kk_mm, 1)
                product(l, LR + 2, H)
                product(l, LR + 3, H)
                pe.wait_ge(rk_ready, 4 * (l + 1))
                pe.wait_ge(lora_act, 10 * l + 8)
                if l:
                    pe.wait_ge(zv_up, 7)
                pe.wait_ge(mod_ready, 6 * l + 3)
                for b in range(2):
                    last = MM(ps[:, 6 + b, :], mat(BLOCKS), BON[:, 2 * b:2 * b + 2, :], start=True, stop=True)
                last.then_inc(bon_mm, 1)
                for k in range(AT, GA):
                    product(l, k, H)
                    b = k - AT - 1
                    if 0 <= b < 4:
                        g = PAIRS * l + AT + b
                        pe.wait_ge(bank_free[g % 4], EMPTIED[g][g % 4] + 1)
                        if b < 2:
                            pe.wait_ge(kk_rt, 2 * (l + 1))
                        else:
                            pe.wait_ge(bon_ready, 2 * (l + 1))
                        MM(ps[:, 4 + b, :], mat(ROT), QK[:, 2 * b:2 * b + 2, :], start=True, stop=True).then_inc(rot_mm, 1)
                for i in range(2):
                    for h in range(2):
                        pe.wait_ge(xc_ready, 4 * l + 2 * h + 2)
                        pe.wait_ge(rope_mul, 4 * l + 2 * i + h + 1)
                        for j in (2 * h, 2 * h + 1):
                            last = MM(duo((4 if i == 0 else 6) + h)[:, j % 2, :], SW[:, WA + W * i + j * P:WA + W * i + (j + 1) * P],
                                      XC[:, j, :], start=True, stop=True)
                        last.then_inc(lr_mm, 1)
                for t in range(2):
                    g = PAIRS * l + AT + 4 + t
                    pe.wait_ge(bank_free[g % 4], EMPTIED[g][g % 4] + 1)
                for t in range(2):
                    pe.wait_ge(lr_act, 8 * l + 2 * t + 2)
                    for j in range(4):
                        last = nc.tensor.transpose(ps[:, 4 + t, j * P:(j + 1) * P], VR[:, j, t * P:(t + 1) * P], mat(IDENT))
                    last.then_inc(avt_mm, 1)
                filled = [0]

                def fill(point):
                    fill_some(FILL[point])

                def fill_some(n):
                    for _ in range(min(n, 16 * GATES - filled[0])):
                        k, r = divmod(filled[0], 16)
                        m, i = divmod(r, 8)
                        g = PAIRS * l + GA + k
                        if r == 0:
                            landed(g)
                            emptied(g, g % 4)
                        last = MM(ps[:, g % 4, m * S:(m + 1) * S], w_of(g, m, i), H[:, i, :], start=(i == 0), stop=(i == KT - 1))
                        if r == 15:
                            last.then_inc(pair_done, 1)
                        filled[0] += 1

                def scores(n):
                    t, c, h0, nh = SCORES[n]
                    rows = slice(64 * c, 64 * c + 64)
                    nk = P * (t + 1)
                    for i in range(nh):
                        h = h0 + i
                        last = MM(ps[:, SCORE_BANK[n], i * nk:(i + 1) * nk], QK[rows, h, t * P:(t + 1) * P], QK[rows, 4 + h, 0:nk],
                                  start=True, stop=True)
                    last.then_inc(sc_mm, 1)

                fill(0)
                pe.wait_ge(qk_ready, 4 * (l + 1))
                pe.wait_ge(lr_act, 8 * (l + 1))
                scores(0)
                scores(1)
                fill(1)
                pe.wait_ge(avt_ev, 2 * (l + 1))
                scores(2)
                scores(3)
                pe.wait_ge(sc_read, 6 * l + 1)
                scores(4)
                pe.wait_ge(sc_read, 6 * l + 2)
                scores(5)
                fill(2)
                fill(3)
                fill(4)
                for n, (kt, qt) in enumerate(((0, 0), (0, 1), (1, 1))):
                    pe.wait_ge(sc_read, 6 * (l + 1))
                    for h in range(4):
                        pe.wait_ge(p_ready, 8 * l + 4 * qt + h + 1)
                        src = S0[:, 0, h, :] if qt == 0 else S1[:, 0, h, kt * P:(kt + 1) * P]
                        last = nc.tensor.transpose(ps[:, 4 + n, h * P:(h + 1) * P], src, mat(IDENT))
                    last.then_inc(pt_mm, 1)
                fill(5)
                for n, b in enumerate((7, 4)):
                    pe.wait_ge(pt_ev, 3 * (l + 1))
                    for h in (2 * n, 2 * n + 1):
                        MM(ps[:, b, (h % 2) * S:(h % 2 + 1) * S], AVT[:, 0, h * P:(h + 1) * P], PT[:, 0, h, :], start=True, stop=False)
                        last = MM(ps[:, b, (h % 2) * S + P:(h % 2 + 1) * S], AVT[:, 1, h * P:(h + 1) * P], PT[:, 1, h, P:S],
                                  start=False, stop=True)
                    last.then_inc(ao_mm, 1)
                for n in range(2):
                    pe.wait_ge(ao_sq, 2 * l + n + 1)
                    MM(ps[:, 5 + n, :], ones[:, :], E[:, 2 * n:2 * n + 2, :], start=True, stop=True).then_inc(as_mm, 1)
                fill(6)
                pe.wait_ge(feat, 4 * (l + 1))
                for n in range(8):
                    t = n % 2
                    src = (KK, AB, K_, V_)[n // 2]
                    pe.wait_ge(yb_ready, 2 * (l + 1))
                    if n == 0:
                        mod_sum(6 * l + 3)
                    if n == 3:
                        pe.wait_ge(mod_ready, 6 * l + 4)
                    if n >= 4:
                        pe.wait_ge(tk_ev, 8 * l + n - 3)
                    for j in range(4):
                        last = nc.tensor.transpose(ps[:, 4 + n % 4, j * P:(j + 1) * P], src[:, j, t * P:(t + 1) * P], mat(IDENT))
                    last.then_inc(tk_mm, 1)
                fill(7)
                for tt in range(2):
                    base = NSTEP * (2 * l + tt)
                    cols = slice(tt * P, (tt + 1) * P)
                    if tt:
                        pe.wait_ge(t_ev, base)
                        mod_sum(6 * l + 4)
                    for n, (kind, par, v, b) in enumerate(STEPS):
                        rows = slice(64 * par, 64 * par + 64)
                        t_ = 2 * tt + par
                        if kind in ("ak", "n", "nt"):
                            if kind != "nt":
                                if tt == 0:
                                    pe.wait_ge(tk_ev, 8 * l + 8)
                                else:
                                    pe.wait_ge(t_ev, base)
                            else:
                                pe.wait_ge(t_ev, base + par + 1)
                            if tt and (kind, par) == ("n", 1):
                                pe.wait_ge(mod_ready, 6 * l + 5)
                            a, bb = {"ak": (K_, KK), "n": (KK, AB), "nt": (AB, KK)}[kind]
                            for j in range(4):
                                last = MM(quad(b)[:, j, :], a[rows, j, cols], bb[rows, j, cols], start=True, stop=True)
                        elif kind == "m":
                            if v == 0:
                                pe.wait_ge(t_init, 4 * (2 * l + tt) + 2 * par + 2)
                                pe.wait_ge(w1_ev, 2 * l + tt + 1)
                            else:
                                pe.wait_ge(t_ev, base + step_no("x", par, v - 1) + 1)
                            for j in range(4):
                                last = MM(quad(b)[:, j, :], Nm[:, par, j, :], TTm[:, t_, j, :], start=True, stop=True)
                        elif kind == "x":
                            pe.wait_ge(t_ev, base + step_no("m", par, v) + 1)
                            if v:
                                pe.wait_ge(t_ev, base + step_no("xt", par, v - 1) + 1)
                            for j in range(4):
                                last = MM(quad(b)[:, j, :], Tm[:, par, j, :], Mm[:, par, j, :], start=True, stop=True)
                        else:
                            for j in range(4):
                                last = MM(quad(b)[:, j, :], Mm[:, par, j, :], Tm[:, par, j, :], start=True, stop=True)
                        last.then_inc(t_mm, 1)
                        if n == 5:
                            pe.wait_ge(t_ev, base + 4)
                            for j in range(4):
                                for p2 in range(2):
                                    h = 2 * j + p2
                                    last = MM(ps[:, 6, h * 64:(h + 1) * 64], Mm[:, p2, j, :], VT_[:, tt, h * 64:(h + 1) * 64],
                                              start=True, stop=True)
                            last.then_inc(w1_mm, 1)
                        if kind == "x" and par == 1:
                            fill(8 + 5 * tt + v)
                pe.wait_ge(t_ev, NSTEP * 2 * (l + 1))
                for tt in range(2):
                    for j in range(4):
                        for p2 in range(2):
                            h = 2 * j + p2
                            last = MM(quad(4 + tt)[64 * p2:64 * p2 + 64, j, :], AT_[:, tt, h * 64:(h + 1) * 64], TTm[:, 2 * tt + p2, j, :],
                                      start=True, stop=True)
                    last.then_inc(zy_mm, 1)
                for tt in range(2):
                    for j in range(4):
                        for p2 in range(2):
                            h = 2 * j + p2
                            last = MM(ps[:, 6 + tt, h * 64:(h + 1) * 64], TTm[:, 2 * tt + p2, j, :], WY[:, tt, h * 64:(h + 1) * 64],
                                      start=True, stop=True)
                    last.then_inc(zy_mm, 1)
                for n in range(8):
                    tt, par = n // 4, (n // 2) % 2
                    rows, cols = slice(64 * par, 64 * par + 64), slice(tt * P, (tt + 1) * P)
                    if n < 4:
                        pe.wait_ge(zy_ev, 4 * l + n + 1)
                    else:
                        pe.wait_ge(rb_ev, 8 * l + n - 3)
                    a = K_ if n % 2 == 0 else AB
                    for j in range(4):
                        last = MM(quad(4 + n % 4)[:, j, :], a[rows, j, cols], R_[rows, j, cols], start=True, stop=True)
                    last.then_inc(rb_mm, 1)

                def read_part(tt, m, tokm, first):
                    for j in range(4):
                        for p2 in range(2):
                            h = 2 * j + p2
                            last = MM(quad(6 + tt)[64 * p2:64 * p2 + 64, j, :], tokm[:, tt, h * 64:(h + 1) * 64], m[:, 2 * tt + p2, j, :],
                                      start=(first and j == 0), stop=False, skip_group_check=True)
                    return last

                pe.wait_ge(rb_ev, 8 * (l + 1))
                pe.wait_ge(zy_ev, 4 * (l + 1))
                read_part(0, RKm, VT_, True)
                read_part(1, RKm, VT_, True)
                for c in range(NCH):
                    tt, hf = c // 2, c % 2
                    rows = slice(64 * hf, 64 * hf + 64)
                    cols = slice(64 * c, 64 * c + 64)
                    if c < NCH - 1:
                        if c:
                            pe.wait_ge(st_ready, 3 * l + c)
                        for j in range(4):
                            MM(quad(5)[:, j, :], KT_[rows, tt, j * P:(j + 1) * P], VT_[rows, tt, j * P:(j + 1) * P],
                               start=(j == 0), stop=False, skip_group_check=True)
                    if c:
                        pe.wait_ge(st_ready, 3 * l + c)
                        for j in range(4):
                            last = MM(quad(4)[rows, j, :], KK[:, j, cols], ST[:, j, :], start=True, stop=True)
                        last.then_inc(u_mm, 1)
                        for j in range(4):
                            last = MM(quad(6 + tt)[:, j, rows], ST[:, j, :], R_[:, j, cols], start=False, stop=False, skip_group_check=True)
                        fill_some(FILL_CHAIN)
                        pe.wait_ge(u_ready, 3 * l + c)
                    if c < NCH - 1:
                        for j in range(4):
                            last = MM(quad(5)[:, j, :], BT_[rows, tt, j * P:(j + 1) * P], WY[rows, tt, j * P:(j + 1) * P],
                                      start=False, stop=(j == 3), skip_group_check=True)
                        last.then_inc(s_mm, 1)
                        fill_some(FILL_CHAIN)
                    if hf == 1:
                        read_part(tt, RBm, WY, False).then_inc(o_mm, 1)

                def merge(p, y):
                    g = PAIRS * l + MERGE + p
                    landed(g)
                    for i, b in enumerate(banks_of(g)):
                        emptied(g, b)
                        for m in (2 * i, 2 * i + 1):
                            for k in range(4):
                                last = MM(ps[:, b, (m % 2) * S:(m % 2 + 1) * S], w_of(g, m, k, 4), y[:, k, :], start=(k == 0), stop=(k == 3))
                    last.then_inc(pair_done, 1)

                fill_some(16 * GATES)
                for b in range(2):
                    pe.wait_ge(o_ev, 2 * (l + 1))
                    MM(ps[:, 4 + b, :], mat(BLOCKS), AB[:, 2 * b:2 * b + 2, :], start=True, stop=True).then_inc(gn_mm, 1)
                pe.wait_ge(ya_ready, 4 * (l + 1))
                merge(0, YA)
                pe.wait_ge(gn_sq, l + 1)
                for b in range(2):
                    MM(ps[:, 6 + b, :], mat(BLOCKS), E[:, 2 * b:2 * b + 2, :], start=True, stop=True).then_inc(gn_mm, 1)
                merge(1, YA)
                pe.wait_ge(gn_rt, 2 * (l + 1))
                mod_sum(6 * l + 5)
                pe.wait_ge(yb_ready, 2 * (l + 1))
                merge(2, YB)
                merge(3, YB)
                pe.wait_ge(yc_ready, l + 1)
                merge(4, AB)
                merge(5, AB)
                for j in range(4):
                    g = PAIRS * l + OU + j
                    emptied(g, g % 4)
                    pe.wait_ge(ol_ready, 4 * l + j + 1)
                    for m in range(2):
                        for k in range(KT):
                            pe.wait_ge(ml_ready, 4 * l + k // 2 + 1)
                            last = passes(ps[:, g % 4, m * S:(m + 1) * S], OWH[:, j % 2, :], OWL[:, j % 2, :], m * KT + k,
                                          MH[:, k, :], ML[:, k, :], k == 0, k == KT - 1)
                    last.then_inc(pair_done, 1)
                ones_sum(2 * l + 1)
                g0 = PAIRS * l + UP

                def up(i, q, first=False):
                    g = g0 + q
                    b = g % 4
                    pe.wait_ge(bank_free[b], i + EMPTIED[g][b])
                    for m in range(2):
                        pe.wait_ge(lo_ready, i * 8 + (2 * (MLP * l + q) + m + 1))
                        for k in range(KT):
                            if first and q == 0 and m == 0:
                                pe.wait_ge(hl_ready, KT * l + k + 1)
                            last = passes(ps[:, b, m * S:(m + 1) * S], WH[:, q % 2, :], WLO[:, q % 2, :], m * KT + k, HH[:, k, :], HL[:, k, :], k == 0, k == KT - 1)
                        last.then_inc((half_done, pair_done)[m], 1)

                for q in range(4):
                    up(0, q, True)
                with pe.Fori(1, FT // 4) as i:
                    for q in range(4):
                        up(i, q)

                def down(i, q, first=False):
                    g = PAIRS * l + DN + q
                    b = g % 4
                    if first:
                        emptied(g, b)
                    for m in range(2):
                        pe.wait_ge(lo_ready, i * 8 + (2 * (MLP * l + FT + q) + m + 1))
                        for k in range(KT):
                            if first and q == 0 and m == 0:
                                pe.wait_ge(g_ready, FT * l + k + 1)
                            at = k if first else bass.ds(i * 8 + k, 1)
                            last = passes(ps[:, b, m * S:(m + 1) * S], WH[:, q % 2, :], WLO[:, q % 2, :], m * KT + k, GH[:, at, :], GL[:, at, :],
                                          first and m == 0 and k == 0, False)
                        last.then_inc((half_done, pair_done)[m], 1)

                for q in range(4):
                    down(0, q, True)
                if l == 0:
                    for n in range(4, MLP - FT):
                        if n == 4:
                            pe.wait_ge(g_ready, FT)
                        down(n // 4, n % 4)
                        if n == DN_SUM:
                            mod_sum(6)
                    mod_sum(7)
                else:
                    pe.wait_ge(g_ready, FT * (l + 1))
                    with pe.Fori(1, 3) as i:
                        for q in range(4):
                            down(i, q)
            ones_sum(4)


def kernel(x, c, positions, w_mod, b_mod, norm1_g, norm2_g, final_g, w_in, w_merge_a, w_merge_b, w_merge_c, w_out,
           lru_conv_w, lru_conv_b, lru_wa, lru_ba, lru_wx, lru_bx, lru_lambda, diff_lq1, diff_lk1, diff_lq2, diff_lk2,
           diff_subln_g, rwkv_mu, rwkv_w0, rwkv_w2, rwkv_a0, rwkv_a2, rwkv_g2, rwkv_kk, rwkv_ka, rwkv_rk, rwkv_lnx_g,
           rwkv_lnx_b, rwkv_v0, rwkv_v1, rwkv_v2, rwkv_vmu, ffn_up, ffn_conv_w, ffn_conv_b, ffn_down):
    import concourse.bacc as bacc
    from concourse.bass_utils import run_bass_kernel_spmd

    f = np.ascontiguousarray

    def blocks(w):
        return w.reshape(w.shape[0] // P, P, w.shape[1] // P, P).transpose(2, 0, 1, 3)

    def pairs(b):
        return b.reshape(-1, 16, P, P).transpose(0, 2, 1, 3).reshape(-1, P, PAIR)

    def tiles(v):
        return v.reshape(-1, P).T

    wmain, wmod, small, prs = [], [], [], []
    zero = np.zeros
    for l in range(L):
        b = blocks(w_in[l])
        gate, lx, q, rw = b[0:24], b[24:32], b[32:44], b[44:58]
        rkv, lora = rw[0:12], rw[12:14]
        w_i = pairs(np.concatenate([lora, rkv[4:8], rkv[0:4], rkv[8:12], lx, q, gate]))
        w_m = pairs(np.concatenate([blocks(w[l]) for w in (w_merge_a, w_merge_b, w_merge_c)]))
        wmain += [w_i, w_m]
        wmain.append(pairs(blocks(w_out[l])))
        up = blocks(ffn_up[l])
        wmain.append(pairs(np.stack([up[0:FT], up[FT:]], axis=1)))
        dn = blocks(ffn_down[l])
        wmain.append(pairs(dn.reshape(KT, 3, KT, P, P).transpose(1, 0, 2, 3, 4)))
        vecs = w_mod[l].reshape(KT, P, 6, D)
        order = (1, 0, 2, 3, 4, 5)
        wmod.append(vecs[:, :, order].transpose(2, 0, 1, 3).reshape(6 * KT, P, D))
        bm = b_mod[l].reshape(6, D)[list(order)].reshape(-1)

        def bd(w):
            return w.reshape(4, 2, 64, 64).transpose(1, 2, 0, 3).reshape(P, 256)

        small.append(np.concatenate([np.concatenate([rwkv_w2[l], rwkv_a2[l]], axis=0), rwkv_g2[l], bd(lru_wa[l]), bd(lru_wx[l])], axis=1))
        mu = rwkv_mu[l]
        mu = np.concatenate([mu[3 * W:], mu[W:2 * W], mu[0:W], mu[2 * W:3 * W]])
        v0 = rwkv_v0[l - 1] if l else zero(W, np.float32)
        vmu = np.concatenate([rwkv_vmu[l - 1], zero(P - 32, np.float32)]) if l else zero(P, np.float32)
        parts = {"n1g": norm1_g[l], "n2g": norm2_g[l], "bmod": bm, "mu": mu, "w0": rwkv_w0[l], "a0": rwkv_a0[l], "v0": v0,
                 "ba": lru_ba[l].reshape(-1), "bx": lru_bx[l].reshape(-1), "kk": rwkv_kk[l], "ka": rwkv_ka[l],
                 "rk": rwkv_rk[l].reshape(-1), "lng": rwkv_lnx_g[l], "lnb": rwkv_lnx_b[l], "vmu": vmu, "sub": diff_subln_g[l],
                 "cw": lru_conv_w[l].reshape(-1), "cb": lru_conv_b[l], "lam": lru_lambda[l], "fw": ffn_conv_w[l].reshape(-1),
                 "fb": ffn_conv_b[l], "fg": final_g, "cc": c[0]}
        prs.append(np.concatenate([tiles(np.asarray(parts[n])) for n, _ in _NAMES], axis=1))
    v1v2 = np.concatenate([np.asarray(rwkv_v1[0]).reshape(KT, P, 32).transpose(1, 0, 2).reshape(P, 256),
                           np.concatenate([rwkv_v2[0], zero((P - 32, W), np.float32)])], axis=1)
    lqk = np.stack([diff_lq1, diff_lk1, diff_lq2, diff_lk2], axis=1).reshape(-1)

    i, j = np.arange(P)[:, None], np.arange(P)[None, :]
    same = i // CH == j // CH

    def level(s):
        return (i // (2 * s) == j // (2 * s)) & (i // s % 2 == 0) & (j // s % 2 == 1)

    rot = zero((P, P), np.float32)
    for p in range(P):
        if p % 64 < 8:
            rot[p + 8, p] = -1
        elif p % 64 < 16:
            rot[p - 8, p] = 1
    mats = [i == j, i // 64 == j // 64, same & (j < i), same & (j > i), same & (j >= i), level(1).T, level(1), level(2), level(4),
            level(8), level(16), level(32), rot]
    neg = np.where(np.arange(2 * P)[None, :] > P + i, np.float32(-1e30), np.float32(0))
    reset = np.broadcast_to((np.arange(S) % CH != 0)[None, :], (P, S))
    inv = (np.float32(500000.0) ** (-np.arange(0, 16, 2, dtype=np.float32) / np.float32(16))).astype(np.float32)
    freq = np.where(i % 64 < 16, inv[i % 8], np.float32(0))
    consts = np.concatenate([m.astype(np.float32) for m in mats] + [neg, reset.astype(np.float32), freq], axis=1).astype(np.float32)

    arrays = {
        "wmain": f(np.concatenate(wmain)), "wmod": f(np.concatenate(wmod)), "small": f(np.stack(small)), "v1v2": f(v1v2),
        "params": f(np.stack(prs, axis=1)), "consts": f(consts), "lqk": f(lqk),
        "x_t": f(np.asarray(x)[0].T.reshape(KT, P, S).transpose(1, 0, 2)), "positions": f(np.asarray(positions)[0]),
    }
    nc = bacc.Bacc("TRN2", target_bir_lowering=False, num_devices=1)
    args = [nc.dram_tensor(f"{n}_dram", a.shape, mybir.dt.from_np(a.dtype), kind="ExternalInput").ap() for n, a in arrays.items()]
    args.append(nc.dram_tensor("y_dram", (P, KT, S), F32, kind="ExternalOutput").ap())
    trunk_kernel(nc, *args)
    r = run_bass_kernel_spmd(nc, [{f"{n}_dram": a for n, a in arrays.items()}], core_ids=[0])
    y = r.results[0]["y_dram"]
    return y.transpose(1, 0, 2).reshape(D, S).T.reshape(1, S, D)
```
